# Optimizing a Trainium2 kernel written in Bass

```python
import jax, jax.numpy as jnp
from jax import lax
import numpy as np
import math

D_MODEL = 1024
BATCH = 1
SEQ = 512
DEPTH = 1

A_GROUPS = 4
A_GROUP_DIM = 128
A_WIDTH = A_GROUPS * A_GROUP_DIM
CHUNK = 128
N_HEADS = 4
HEAD_DIM = 128
B_WIDTH = N_HEADS * HEAD_DIM
KV_LATENT = 256
ROT_DIM = HEAD_DIM // 4
IDX_HEADS = 4
IDX_DIM = 64
IDX_ROT = IDX_DIM // 4
TOPK_MAX = 256
Q_BLOCK = 128
ROPE_THETA = 500000.0
N_BRANCHES = 2
PEER_HEADS = 8
PEER_KEY_DIM = 256
PEER_HALF = PEER_KEY_DIM // 2
N_KEYS = 128
N_EXPERTS = N_KEYS * N_KEYS
PEER_TOPK = 16
PEER_BLOCK = 128
EPS = 1e-6

SPLITS = (A_WIDTH, A_WIDTH, B_WIDTH, KV_LATENT, IDX_HEADS * IDX_DIM, IDX_DIM, IDX_HEADS, N_BRANCHES * D_MODEL)
IN_WIDTH = sum(SPLITS)
SPLIT_OFFSETS = tuple(int(o) for o in np.cumsum(SPLITS)[:-1])


def rms_norm(x, g):
    xf = x.astype(jnp.float32)
    y = xf * lax.rsqrt(jnp.mean(xf * xf, axis=-1, keepdims=True) + EPS)
    return (y * g.astype(jnp.float32)).astype(x.dtype)

def layer_norm(x, g, b):
    xf = x.astype(jnp.float32)
    mu = jnp.mean(xf, axis=-1, keepdims=True)
    xc = xf - mu
    y = xc * lax.rsqrt(jnp.mean(xc * xc, axis=-1, keepdims=True) + EPS)
    return (y * g.astype(jnp.float32) + b.astype(jnp.float32)).astype(x.dtype)

def partial_rope(x, pos, rot_dim):
    half = rot_dim // 2
    inv = jnp.power(jnp.float32(ROPE_THETA), -jnp.arange(half, dtype=jnp.float32) * 2.0 / rot_dim)
    ang = pos.astype(jnp.float32)[..., None] * inv
    cos = jnp.cos(ang)[:, :, None, :]
    sin = jnp.sin(ang)[:, :, None, :]
    xr = x[..., :rot_dim].astype(jnp.float32)
    x1, x2 = xr[..., :half], xr[..., half:]
    rot = jnp.concatenate([x1 * cos - x2 * sin, x2 * cos + x1 * sin], axis=-1)
    return jnp.concatenate([rot.astype(x.dtype), x[..., rot_dim:]], axis=-1)

def chunked_spatial_gating(u, v, v_g, v_b, w_s, b_s):
    bsz, s, _ = u.shape
    u = jax.nn.gelu(u)
    v = layer_norm(jax.nn.gelu(v), v_g, v_b)
    v = v.reshape(bsz, s // CHUNK, CHUNK, A_GROUPS, A_GROUP_DIM)
    causal = jnp.tril(jnp.ones((CHUNK, CHUNK), dtype=bool))
    w = jnp.where(causal[None], w_s, jnp.zeros_like(w_s))
    z = jnp.einsum('gts,bcsgd->bctgd', w, v) + b_s.T[None, None, :, :, None]
    return u * z.reshape(bsz, s, A_WIDTH)

def dsa_attention(q, k, v, q_idx, k_idx, w_idx):
    bsz, s = q.shape[:2]
    n_sel = min(TOPK_MAX, s // 4)
    nblk = s // Q_BLOCK
    key_pos = jnp.arange(s)

    def to_blocks(a):
        return a.reshape(bsz, nblk, Q_BLOCK, *a.shape[2:]).swapaxes(0, 1)

    def gather_rows(table, idx):
        return table[idx]

    def block_fn(args):
        blk, qb, qib, wib = args
        q_pos = blk * Q_BLOCK + jnp.arange(Q_BLOCK)
        causal = key_pos[None, :] <= q_pos[:, None]
        logits = jnp.einsum('bqhd,bsd->bqhs', qib, k_idx, preferred_element_type=jnp.float32) * (IDX_DIM ** -0.5)
        scores = jnp.einsum('bqh,bqhs->bqs', wib.astype(jnp.float32), jax.nn.relu(logits))
        scores = jnp.where(causal[None], scores, -jnp.inf)
        _, idx = lax.top_k(scores, n_sel)
        valid = idx <= q_pos[None, :, None]
        k_sel = jax.vmap(gather_rows)(k, idx)
        v_sel = jax.vmap(gather_rows)(v, idx)
        att = jnp.einsum('bqhd,bqnd->bqhn', qb, k_sel, preferred_element_type=jnp.float32) * (HEAD_DIM ** -0.5)
        att = jnp.where(valid[:, :, None, :], att, jnp.float32(-1e30))
        p = jax.nn.softmax(att, axis=-1).astype(v.dtype)
        return jnp.einsum('bqhn,bqnd->bqhd', p, v_sel)

    out = lax.map(block_fn, (jnp.arange(nblk), to_blocks(q), to_blocks(q_idx), to_blocks(w_idx)))
    return out.swapaxes(0, 1).reshape(bsz, s, B_WIDTH)

def peer(xn, wq, subkeys, u_tab, v_tab):
    bsz, s, d = xn.shape
    q = (xn @ wq).reshape(bsz, s, PEER_HEADS, 2, PEER_HALF)
    sub = jnp.einsum('bshpd,hpnd->bshpn', q, subkeys, preferred_element_type=jnp.float32)
    s_top, i_top = lax.top_k(sub, PEER_TOPK)
    cand = (s_top[..., 0, :, None] + s_top[..., 1, None, :]).reshape(bsz, s, PEER_HEADS, PEER_TOPK * PEER_TOPK)
    cand_idx = (i_top[..., 0, :, None] * N_KEYS + i_top[..., 1, None, :]).reshape(bsz, s, PEER_HEADS, PEER_TOPK * PEER_TOPK)
    best, pos = lax.top_k(cand, PEER_TOPK)
    expert = jnp.take_along_axis(cand_idx, pos, axis=-1)
    gate = jax.nn.softmax(best, axis=-1)
    nb = (bsz * s) // PEER_BLOCK
    hk = PEER_HEADS * PEER_TOPK
    xt = xn.reshape(nb, PEER_BLOCK, d)
    et = expert.reshape(nb, PEER_BLOCK, hk)
    gt = gate.reshape(nb, PEER_BLOCK, hk)

    def blk(args):
        xb, eb, gb = args
        ub = u_tab[eb]
        vb = v_tab[eb]
        a = jax.nn.gelu(jnp.einsum('td,ted->te', xb, ub, preferred_element_type=jnp.float32))
        return jnp.einsum('te,ted->td', (gb * a).astype(vb.dtype), vb)

    y = lax.map(blk, (xt, et, gt))
    return y.reshape(bsz, s, d)

def first_inputs(seed: int = 0) -> dict:
    key = jax.random.key(seed)
    ks = jax.random.split(key, 24)
    f32 = jnp.float32
    L = DEPTH
    nrm = lambda k, shape, scale: jax.random.normal(k, shape, f32) * scale
    x = jax.random.normal(ks[0], (BATCH, SEQ, D_MODEL), f32)
    positions = jnp.broadcast_to(jnp.arange(SEQ, dtype=jnp.int32)[None, :], (BATCH, SEQ))
    return {
        "x": x,
        "positions": positions,
        "norm1_g": 1.0 + nrm(ks[1], (L, D_MODEL), 0.02),
        "w_in": nrm(ks[2], (L, D_MODEL, IN_WIDTH), D_MODEL ** -0.5),
        "v_norm_g": 1.0 + nrm(ks[3], (L, A_WIDTH), 0.02),
        "v_norm_b": nrm(ks[4], (L, A_WIDTH), 0.02),
        "spatial_w": nrm(ks[5], (L, A_GROUPS, CHUNK, CHUNK), CHUNK ** -0.5),
        "spatial_b": 1.0 + nrm(ks[6], (L, A_GROUPS, CHUNK), 0.1),
        "kv_norm_g": 1.0 + nrm(ks[7], (L, KV_LATENT), 0.02),
        "w_uk": nrm(ks[8], (L, KV_LATENT, HEAD_DIM), KV_LATENT ** -0.5),
        "w_uv": nrm(ks[9], (L, KV_LATENT, HEAD_DIM), KV_LATENT ** -0.5),
        "q_norm_g": 1.0 + nrm(ks[10], (L, HEAD_DIM), 0.02),
        "k_norm_g": 1.0 + nrm(ks[11], (L, HEAD_DIM), 0.02),
        "w_a_out": nrm(ks[12], (L, A_WIDTH, D_MODEL), A_WIDTH ** -0.5),
        "w_b_out": nrm(ks[13], (L, B_WIDTH, D_MODEL), B_WIDTH ** -0.5),
        "w_o": nrm(ks[14], (L, D_MODEL, D_MODEL), D_MODEL ** -0.5),
        "norm2_g": 1.0 + nrm(ks[15], (L, D_MODEL), 0.02),
        "peer_wq": nrm(ks[16], (L, D_MODEL, PEER_HEADS * PEER_KEY_DIM), D_MODEL ** -0.5),
        "peer_subkeys": nrm(ks[17], (L, PEER_HEADS, 2, N_KEYS, PEER_HALF), PEER_HALF ** -0.5),
        "peer_u": nrm(ks[18], (L, N_EXPERTS, D_MODEL), D_MODEL ** -0.5),
        "peer_v": nrm(ks[19], (L, N_EXPERTS, D_MODEL), 0.5 * PEER_HEADS ** -0.5),
    }

def first_block(x, positions, norm1_g, w_in, v_norm_g, v_norm_b, spatial_w, spatial_b, kv_norm_g, w_uk, w_uv,
              q_norm_g, k_norm_g, w_a_out, w_b_out, w_o, norm2_g, peer_wq, peer_subkeys, peer_u, peer_v):
    bsz, s, d = x.shape
    h = x
    for l in range(DEPTH):
        xn = rms_norm(h, norm1_g[l])
        proj = xn @ w_in[l]
        u, v, q, c_kv, q_idx, k_idx, w_idx, gates = jnp.split(proj, SPLIT_OFFSETS, axis=-1)

        y_a = chunked_spatial_gating(u, v, v_norm_g[l], v_norm_b[l], spatial_w[l], spatial_b[l])

        c_n = rms_norm(c_kv, kv_norm_g[l])
        k = rms_norm(c_n @ w_uk[l], k_norm_g[l])
        vv = c_n @ w_uv[l]
        qh = rms_norm(q.reshape(bsz, s, N_HEADS, HEAD_DIM), q_norm_g[l])
        qh = partial_rope(qh, positions, ROT_DIM)
        k = partial_rope(k[:, :, None, :], positions, ROT_DIM)[:, :, 0, :]
        qi = partial_rope(q_idx.reshape(bsz, s, IDX_HEADS, IDX_DIM), positions, IDX_ROT)
        ki = partial_rope(k_idx[:, :, None, :], positions, IDX_ROT)[:, :, 0, :]
        wi = w_idx * (IDX_HEADS ** -0.5)
        y_b = dsa_attention(qh, k, vv, qi, ki, wi)

        g = jax.nn.sigmoid(gates.reshape(bsz, s, N_BRANCHES, d))
        merged = g[:, :, 0, :] * (y_a @ w_a_out[l]) + g[:, :, 1, :] * (y_b @ w_b_out[l])
        h = h + merged @ w_o[l]

        hn = rms_norm(h, norm2_g[l])
        h = h + peer(hn, peer_wq[l], peer_subkeys[l], peer_u[l], peer_v[l])
    return h


D_MIX = D_MODEL
NEG = -1e30
FORCE = 1e6
F_FLOOR = 1e-30
NSA_HEADS = 8
NSA_KV_GROUPS = 2
NSA_HD = 64
CMP_LEN = 32
CMP_STRIDE = 16
CMP_HID = 256
SEL_BLOCK = 64
SEL_TOPK = 16
SEL_QBLOCK = 32
WINDOW = 512
WIN_QBLOCK = 128
HG_HEADS = 4
HG_DK = 128
HG_DV = 128
HG_CHUNK = 64
D_FF = 2752

NSA_WIDTH = NSA_HEADS * NSA_HD
HG_WIDTH = HG_HEADS * HG_DV
KV_W = NSA_KV_GROUPS * NSA_HD
IN_SIZES = (NSA_WIDTH, KV_W, KV_W, KV_W, KV_W, KV_W, KV_W, NSA_HEADS * 3,
            HG_HEADS * HG_DK, HG_HEADS * HG_DK, HG_WIDTH, HG_WIDTH)
IN_COLS = sum(IN_SIZES)
IN_SPLITS = tuple(int(v) for v in np.cumsum(IN_SIZES)[:-1])


def rms_norm_2(x, g):
    xf = x.astype(jnp.float32)
    y = xf * lax.rsqrt(jnp.mean(xf * xf, axis=-1, keepdims=True) + EPS)
    return (y * g.astype(jnp.float32)).astype(x.dtype)

def swiglu(x, w_gu, w_down):
    gate, up = jnp.split(x @ w_gu, 2, axis=-1)
    return (jax.nn.silu(gate) * up) @ w_down

def alibi_slopes(n):
    return jnp.asarray([2.0 ** (-8.0 * (i + 1) / n) for i in range(n)], dtype=jnp.float32)

def compress(kv, pos_emb, w1, w2):
    B, S, G, dk = kv.shape
    chunks = kv.reshape(B, S // CMP_STRIDE, CMP_STRIDE, G, dk)
    blocks = jnp.concatenate([chunks[:, :-1], chunks[:, 1:]], axis=2) + pos_emb[:, None, :]
    nb = blocks.shape[1]
    flat = blocks.transpose(0, 1, 3, 2, 4).reshape(B, nb, G, CMP_LEN * dk)
    return jax.nn.gelu(flat @ w1) @ w2

def nsa_group(q, k_c, v_c, k_s, v_s, k_w, v_w, gate_logits,
              cmp_pos_k, cmp_pos_v, cmp_k_w1, cmp_k_w2, cmp_v_w1, cmp_v_w2):
    B, S = q.shape[:2]
    G, Hg, dk = NSA_KV_GROUPS, NSA_HEADS // NSA_KV_GROUPS, NSA_HD
    scale = dk ** -0.5
    slopes = alibi_slopes(NSA_HEADS).reshape(G, Hg)
    q5 = q.reshape(B, S, G, Hg, dk)
    kv4 = lambda t: t.reshape(B, S, G, dk)
    pos = jnp.arange(S, dtype=jnp.int32)

    kc = compress(kv4(k_c), cmp_pos_k, cmp_k_w1, cmp_k_w2)
    vc = compress(kv4(v_c), cmp_pos_v, cmp_v_w1, cmp_v_w2)
    nb = kc.shape[1]
    blk_end = jnp.arange(nb, dtype=jnp.int32) * CMP_STRIDE + (CMP_LEN - 1)
    dist_c = pos[:, None] - blk_end[None, :]
    s_c = jnp.einsum('bsgnd,bcgd->bsgnc', q5, kc).astype(jnp.float32) * scale
    s_c = s_c - slopes[:, :, None] * dist_c.astype(jnp.float32)[:, None, None, :]
    s_c = jnp.where((dist_c >= 0)[:, None, None, :], s_c, NEG)
    p_c = jax.nn.softmax(s_c, axis=-1)
    p_c = jnp.where((pos >= CMP_LEN - 1)[:, None, None, None], p_c, 0.0)
    o_cmp = jnp.einsum('bsgnc,bcgd->bsgnd', p_c.astype(vc.dtype), vc)

    imp = p_c.sum(axis=3)
    padded = jnp.pad(imp, ((0, 0), (0, 0), (0, 0), (1, 1)))
    chunk_imp = padded[..., :-1] + padded[..., 1:]
    ns = S // SEL_BLOCK
    p_slc = chunk_imp.reshape(B, S, G, ns, SEL_BLOCK // CMP_STRIDE).sum(-1)
    blk = jnp.arange(ns, dtype=jnp.int32)
    cur = pos // SEL_BLOCK
    forced = (blk[None] == 0) | (blk[None] == cur[:, None]) | (blk[None] == cur[:, None] - 1)
    causal = blk[None] * SEL_BLOCK <= pos[:, None]
    score = jnp.where(forced[:, None], FORCE, jnp.where(causal[:, None], p_slc, NEG))
    n_sel = min(SEL_TOPK, ns)
    _, sel_idx = lax.top_k(score, n_sel)

    k_blocks = kv4(k_s).reshape(B, ns, SEL_BLOCK, G, dk).transpose(0, 3, 1, 2, 4)
    v_blocks = kv4(v_s).reshape(B, ns, SEL_BLOCK, G, dk).transpose(0, 3, 1, 2, 4)
    nq = S // SEL_QBLOCK
    b_ix = jnp.arange(B)[:, None, None, None]
    g_ix = jnp.arange(G)[None, None, :, None]
    l_ar = jnp.arange(SEL_BLOCK, dtype=jnp.int32)

    def sel_step(args):
        qb, idx, qi = args
        kg = k_blocks[b_ix, g_ix, idx]
        vg = v_blocks[b_ix, g_ix, idx]
        s = jnp.einsum('btgnd,btgkld->btgnkl', qb, kg).astype(jnp.float32) * scale
        qpos = qi * SEL_QBLOCK + jnp.arange(SEL_QBLOCK, dtype=jnp.int32)
        kpos = idx[..., None] * SEL_BLOCK + l_ar
        dist = qpos[None, :, None, None, None] - kpos
        s = s - slopes[None, None, :, :, None, None] * dist.astype(jnp.float32)[:, :, :, None]
        s = jnp.where((dist >= 0)[:, :, :, None], s, NEG)
        p = jax.nn.softmax(s.reshape(s.shape[:4] + (-1,)), axis=-1).reshape(s.shape)
        return jnp.einsum('btgnkl,btgkld->btgnd', p.astype(vg.dtype), vg)

    o_sel = lax.map(sel_step, (q5.reshape(B, nq, SEL_QBLOCK, G, Hg, dk).swapaxes(0, 1),
                               sel_idx.reshape(B, nq, SEL_QBLOCK, G, n_sel).swapaxes(0, 1),
                               jnp.arange(nq, dtype=jnp.int32)))
    o_sel = o_sel.swapaxes(0, 1).reshape(B, S, G, Hg, dk)

    nwq = S // WIN_QBLOCK
    n_kb = WINDOW // WIN_QBLOCK + 1
    kw_len = n_kb * WIN_QBLOCK

    def band(t):
        tp = jnp.pad(kv4(t), ((0, 0), (WINDOW, 0), (0, 0), (0, 0)))
        tp = tp.reshape(B, nwq + WINDOW // WIN_QBLOCK, WIN_QBLOCK, G, dk)
        return jnp.concatenate([tp[:, j:j + nwq] for j in range(n_kb)], axis=2).swapaxes(0, 1)

    def win_step(args):
        qb, kb, vb, qi = args
        s = jnp.einsum('btgnd,bkgd->btgnk', qb, kb).astype(jnp.float32) * scale
        qpos = qi * WIN_QBLOCK + jnp.arange(WIN_QBLOCK, dtype=jnp.int32)
        kpos = qi * WIN_QBLOCK - WINDOW + jnp.arange(kw_len, dtype=jnp.int32)
        dist = qpos[:, None] - kpos[None, :]
        valid = (dist >= 0) & (dist < WINDOW) & (kpos >= 0)[None, :]
        s = s - slopes[None, None, :, :, None] * dist.astype(jnp.float32)[None, :, None, None, :]
        s = jnp.where(valid[None, :, None, None, :], s, NEG)
        p = jax.nn.softmax(s, axis=-1)
        return jnp.einsum('btgnk,bkgd->btgnd', p.astype(vb.dtype), vb)

    o_win = lax.map(win_step, (q5.reshape(B, nwq, WIN_QBLOCK, G, Hg, dk).swapaxes(0, 1),
                               band(k_w), band(v_w), jnp.arange(nwq, dtype=jnp.int32)))
    o_win = o_win.swapaxes(0, 1).reshape(B, S, G, Hg, dk)

    g = jax.nn.sigmoid(gate_logits.astype(jnp.float32)).reshape(B, S, G, Hg, 3)
    o = (g[..., 0:1] * o_cmp.astype(jnp.float32) + g[..., 1:2] * o_sel.astype(jnp.float32)
         + g[..., 2:3] * o_win.astype(jnp.float32))
    return o.reshape(B, S, NSA_WIDTH).astype(q.dtype)

def hgrn2_group(q, f_logit, i_in, g_in, lower_bound, out_norm):
    B, S = q.shape[:2]
    H, dk, dv, C = HG_HEADS, HG_DK, HG_DV, HG_CHUNK
    qf = jax.nn.silu(q.astype(jnp.float32)).reshape(B, S, H, dk)
    lb = lower_bound.astype(jnp.float32)
    z = f_logit.astype(jnp.float32)
    f = lb + (1.0 - lb) * jax.nn.sigmoid(z)
    logf = jnp.log(jnp.maximum(f, F_FLOOR)).reshape(B, S, H, dk)
    kf = ((1.0 - lb) * jax.nn.sigmoid(-z)).reshape(B, S, H, dk)
    vf = i_in.astype(jnp.float32).reshape(B, S, H, dv)
    nc = S // C
    to_chunks = lambda t: t.reshape(B, nc, C, H, t.shape[-1]).transpose(1, 0, 3, 2, 4)
    tril = jnp.tril(jnp.ones((C, C), dtype=bool))

    def step(state, inp):
        qc, kc, vc, lf = inp
        b = jnp.cumsum(lf, axis=2)
        decay = b[:, :, :, None, :] - b[:, :, None, :, :]
        decay = jnp.exp(jnp.where(tril[:, :, None], decay, NEG))
        a = jnp.einsum('bhtd,bhtsd,bhsd->bhts', qc, decay, kc)
        o_intra = jnp.einsum('bhts,bhsv->bhtv', a, vc)
        o_inter = jnp.einsum('bhtd,bhdv->bhtv', qc * jnp.exp(b), state)
        b_last = b[:, :, -1]
        new_state = (jnp.exp(b_last)[..., None] * state
                     + jnp.einsum('bhsd,bhsv->bhdv', kc * jnp.exp(b_last[:, :, None] - b), vc))
        return new_state, o_intra + o_inter

    state0 = jnp.zeros((B, H, dk, dv), jnp.float32)
    _, o = lax.scan(step, state0, (to_chunks(qf), to_chunks(kf), to_chunks(vf), to_chunks(logf)))
    o = o.transpose(1, 0, 3, 2, 4).reshape(B, S, H, dv)
    o = o * lax.rsqrt(jnp.mean(o * o, axis=-1, keepdims=True) + EPS) * out_norm.astype(jnp.float32)
    o = o.reshape(B, S, HG_WIDTH) * jax.nn.silu(g_in.astype(jnp.float32))
    return o.astype(q.dtype)

def hybrid_mixer(h, w_in, cmp_pos_k, cmp_pos_v, cmp_k_w1, cmp_k_w2, cmp_v_w1, cmp_v_w2,
                 lower_bound, hg_norm, w_out):
    parts = jnp.split(h @ w_in, IN_SPLITS, axis=-1)
    nq, k_c, v_c, k_s, v_s, k_w, v_w, gl, hq, hf, hi, hg = parts
    o_nsa = nsa_group(nq, k_c, v_c, k_s, v_s, k_w, v_w, gl,
                      cmp_pos_k, cmp_pos_v, cmp_k_w1, cmp_k_w2, cmp_v_w1, cmp_v_w2)
    o_hg = hgrn2_group(hq, hf, hi, hg, lower_bound, hg_norm)
    return jnp.concatenate([o_nsa, o_hg], axis=-1) @ w_out

def second_inputs(seed: int = 0) -> dict:
    key = jax.random.key(seed)
    ks = jax.random.split(key, 20)
    nrm = lambda k, shape, s: jax.random.normal(k, shape, jnp.float32) * s
    gain = lambda k, shape: 1.0 + 0.02 * jax.random.normal(k, shape, jnp.float32)
    L = DEPTH
    return {
        "x": jax.random.normal(ks[0], (BATCH, SEQ, D_MODEL), jnp.float32),
        "ffn1_norm": gain(ks[1], (L, D_MODEL)),
        "ffn1_w_gu": nrm(ks[2], (L, D_MODEL, 2 * D_FF), D_MODEL ** -0.5),
        "ffn1_w_down": nrm(ks[3], (L, D_FF, D_MODEL), D_FF ** -0.5),
        "mix_norm": gain(ks[4], (L, D_MODEL)),
        "w_in": nrm(ks[5], (L, D_MODEL, IN_COLS), D_MODEL ** -0.5),
        "cmp_pos_k": nrm(ks[6], (L, CMP_LEN, NSA_HD), 0.02),
        "cmp_pos_v": nrm(ks[7], (L, CMP_LEN, NSA_HD), 0.02),
        "cmp_k_w1": nrm(ks[8], (L, CMP_LEN * NSA_HD, CMP_HID), (CMP_LEN * NSA_HD) ** -0.5),
        "cmp_k_w2": nrm(ks[9], (L, CMP_HID, NSA_HD), CMP_HID ** -0.5),
        "cmp_v_w1": nrm(ks[10], (L, CMP_LEN * NSA_HD, CMP_HID), (CMP_LEN * NSA_HD) ** -0.5),
        "cmp_v_w2": nrm(ks[11], (L, CMP_HID, NSA_HD), CMP_HID ** -0.5),
        "hgrn_lower_bound": nrm(ks[12], (L, HG_HEADS * HG_DK), 0.1),
        "hgrn_out_norm": gain(ks[13], (L, HG_DV)),
        "w_out": nrm(ks[14], (L, D_MIX, D_MODEL), D_MIX ** -0.5),
        "ffn2_norm": gain(ks[15], (L, D_MODEL)),
        "ffn2_w_gu": nrm(ks[16], (L, D_MODEL, 2 * D_FF), D_MODEL ** -0.5),
        "ffn2_w_down": nrm(ks[17], (L, D_FF, D_MODEL), D_FF ** -0.5),
        "final_norm": gain(ks[18], (D_MODEL,)),
    }

def second_block(x, ffn1_norm, ffn1_w_gu, ffn1_w_down, mix_norm, w_in, cmp_pos_k, cmp_pos_v,
              cmp_k_w1, cmp_k_w2, cmp_v_w1, cmp_v_w2, hgrn_lower_bound, hgrn_out_norm, w_out,
              ffn2_norm, ffn2_w_gu, ffn2_w_down, final_norm):
    lb_sm = jax.nn.softmax(hgrn_lower_bound.astype(jnp.float32), axis=0)
    lower_bounds = jnp.cumsum(lb_sm, axis=0) - lb_sm[0]
    h = x
    for l in range(DEPTH):
        h = h + 0.5 * swiglu(rms_norm_2(h, ffn1_norm[l]), ffn1_w_gu[l], ffn1_w_down[l])
        h = h + hybrid_mixer(rms_norm_2(h, mix_norm[l]), w_in[l], cmp_pos_k[l], cmp_pos_v[l],
                             cmp_k_w1[l], cmp_k_w2[l], cmp_v_w1[l], cmp_v_w2[l],
                             lower_bounds[l], hgrn_out_norm[l], w_out[l])
        h = h + 0.5 * swiglu(rms_norm_2(h, ffn2_norm[l]), ffn2_w_gu[l], ffn2_w_down[l])
    return rms_norm_2(h, final_norm)


def setup_inputs(seed=0):
    out = dict(first_inputs(seed))
    for name, value in second_inputs(seed + 1).items():
        if name != "x":
            out[name + "_2"] = value
    return out


def reference(
    x, positions, norm1_g, w_in, v_norm_g, v_norm_b, spatial_w, spatial_b, kv_norm_g, w_uk,
    w_uv, q_norm_g, k_norm_g, w_a_out, w_b_out, w_o, norm2_g, peer_wq, peer_subkeys, peer_u,
    peer_v, ffn1_norm_2, ffn1_w_gu_2, ffn1_w_down_2, mix_norm_2, w_in_2, cmp_pos_k_2,
    cmp_pos_v_2, cmp_k_w1_2, cmp_k_w2_2, cmp_v_w1_2, cmp_v_w2_2, hgrn_lower_bound_2,
    hgrn_out_norm_2, w_out_2, ffn2_norm_2, ffn2_w_gu_2, ffn2_w_down_2, final_norm_2,
):
    x = first_block(
        x, positions, norm1_g, w_in, v_norm_g, v_norm_b, spatial_w, spatial_b, kv_norm_g, w_uk,
        w_uv, q_norm_g, k_norm_g, w_a_out, w_b_out, w_o, norm2_g, peer_wq, peer_subkeys, peer_u,
        peer_v,
    )
    return second_block(
        x, ffn1_norm_2, ffn1_w_gu_2, ffn1_w_down_2, mix_norm_2, w_in_2, cmp_pos_k_2,
        cmp_pos_v_2, cmp_k_w1_2, cmp_k_w2_2, cmp_v_w1_2, cmp_v_w2_2, hgrn_lower_bound_2,
        hgrn_out_norm_2, w_out_2, ffn2_norm_2, ffn2_w_gu_2, ffn2_w_down_2, final_norm_2,
    )


_drawn_inputs = setup_inputs


def setup_inputs(seed=0):
    import zlib

    import numpy as np

    out = dict(_drawn_inputs(seed))
    spreads = {}
    factors = {'norm1_g': 2.828,
     'v_norm_g': 7.087,
     'v_norm_b': 7.105,
     'kv_norm_g': 8.0,
     'q_norm_g': 8.0,
     'k_norm_g': 8.0,
     'norm2_g': 15.238,
     'ffn1_norm_2': 6.747,
     'mix_norm_2': 4.979,
     'cmp_pos_k_2': 200.0,
     'cmp_pos_v_2': 200.0,
     'hgrn_out_norm_2': 25.679,
     'ffn2_norm_2': 25.129,
     'final_norm_2': 21.615}
    for name, (base, spread) in spreads.items():
        noise = np.random.default_rng([zlib.crc32(name.encode()), seed]).standard_normal(out[name].shape)
        drawn = base * np.exp(spread * noise) if base else spread * noise
        out[name] = __import__('jax').numpy.asarray(drawn.astype(out[name].dtype))
    for name, factor in factors.items():
        out[name] = (out[name] * factor).astype(out[name].dtype)
    return out
```

```python
from contextlib import ExitStack

import concourse.bass as bass
from concourse import mybir
from concourse.alu_op_type import AluOpType as ALU

ACT = mybir.ActivationFunctionType
AX = mybir.AxisListType
F32 = mybir.dt.float32
F32R = mybir.dt.float32r
I32 = mybir.dt.int32
U32 = mybir.dt.uint32

P = 128
SEQ = 512
D = 1024
KC = D // P
EPS = 1e-6
PANEL = KC * P
RING = 4


class Chip:

    def __init__(self, nc, ctx):
        self.nc, self.ctx = nc, ctx

    def sb(self, name, shape, dt=F32):
        return self.ctx.enter_context(self.nc.sbuf_tensor(name, shape, dt))

    def ps(self, name, shape, dt=F32):
        return self.ctx.enter_context(self.nc.psum_tensor(name, shape, dt))

    def sem(self, name):
        return self.ctx.enter_context(self.nc.semaphore(name))


def clear_semaphores(nc, sems):
    with nc.Block() as block:
        @block.sync
        def _(sp):
            for s in sems:
                sp.sem_clear(s)


def three_products(pe, out, w_high, w_low, x_high, x_low, first, last):
    pe.matmul(out, w_high, x_high, start=first, stop=False)
    pe.matmul(out, w_high, x_low, start=False, stop=False)
    return pe.matmul(out, w_low, x_high, start=False, stop=last)


class NormStage:

    def __init__(self, c, name, hT, gain_dram, sum_ps, sq, xn, stat):
        self.hT, self.gain_dram, self.sum_ps, self.sq, self.xn = hT, gain_dram, sum_ps, sq, xn
        self.gain = c.sb(f"{name}_gain", [P, KC])
        self.ones = c.sb(f"{name}_ones", [P, P])
        self.stat = stat
        (self.gain_landed, self.ones_ready, self.sq_ready, self.sq_used, self.mean_ready,
         self.root_ready, self.rstd_ready, self.xn_ready, self.x_high, self.x_split) = self.sems = [
            c.sem(f"{name}_{x}") for x in ("gain_landed", "ones_ready", "sq_ready", "sq_used", "mean_ready",
                                           "root_ready", "rstd_ready", "xn_ready", "x_high", "x_split")]

    def sync(self, sp):
        sp.dma_start(self.gain[:], self.gain_dram).then_inc(self.gain_landed, 16)

    def gpsimd(self, pool):
        pool.memset(self.ones[:], 1.0).then_inc(self.ones_ready, 1)

    def scalar_root(self, act):
        for k in range(KC):
            if k >= 2:
                act.wait_ge(self.sq_used, k - 1)
            act.activation(self.sq[:, k % 2, :], self.hT[:, k, :], ACT.Square).then_inc(self.sq_ready, 1)
        act.wait_ge(self.mean_ready, 1)
        act.activation(self.stat[:, 1, :], self.stat[:, 0, :], ACT.Sqrt).then_inc(self.root_ready, 1)

    def scalar_high(self, act, x_hi):
        for k in range(KC):
            act.wait_ge(self.xn_ready, k + 1)
            act.copy(x_hi[:, k, :], self.xn[:, k % 2, :]).then_inc(self.x_high, 1)

    def vector_inverse(self, dve):
        dve.wait_ge(self.sq_used, KC)
        dve.tensor_scalar(self.stat[:, 0, :], self.sum_ps[:], 1.0 / D, EPS, ALU.mult, ALU.add
                          ).then_inc(self.mean_ready, 1)
        dve.wait_ge(self.root_ready, 1)
        dve.reciprocal(self.stat[:, 0, :], self.stat[:, 1, :]).then_inc(self.rstd_ready, 1)
        dve.wait_ge(self.rstd_ready, 1)
        dve.wait_ge(self.gain_landed, 16)

    def vector_split(self, dve, x_hi, x_lo):
        def low(k):
            dve.wait_ge(self.x_high, k + 1)
            dve.tensor_tensor(x_lo[:, k, :], self.xn[:, k % 2, :], x_hi[:, k, :].bitcast(F32), ALU.subtract
                              ).then_inc(self.x_split, 1)
        for k in range(KC):
            if k >= 2:
                dve.wait_ge(self.x_split, k - 1)
            dve.scalar_tensor_tensor(self.xn[:, k % 2, :], self.hT[:, k, :], self.gain[:, k:k + 1],
                                     self.stat[:, 0, :], ALU.mult, ALU.mult).then_inc(self.xn_ready, 1)
            if k >= 1:
                low(k - 1)
        low(KC - 1)

    def tensor(self, pe):
        pe.wait_ge(self.ones_ready, 1)
        for k in range(KC):
            pe.wait_ge(self.sq_ready, k + 1)
            last = pe.matmul(self.sum_ps[:], self.ones[:], self.sq[:, k % 2, :], start=k == 0, stop=k == KC - 1)
            last.then_inc(self.sq_used, 1)


def hidden_stage(nc, name, hT, x_hi, x_lo, up_w, down_w, norm_g=None, routing=None):
    swiglu = norm_g is not None
    PJ = 2 if swiglu else 1
    J = 4
    n_hid = up_w.shape[0] // PJ
    groups, rest = divmod(n_hid - 1, J)
    rest += 1
    assert groups and rest >= 2
    NP = PJ * J
    with ExitStack() as ctx:
        c = Chip(nc, ctx)
        a_raw = c.sb(f"{name}_a_raw", [P, RING, PANEL])
        a_hi = c.sb(f"{name}_a_hi", [P, RING, PANEL], F32R)
        a_lo = c.sb(f"{name}_a_lo", [P, RING, PANEL], F32R)
        b_raw = c.sb(f"{name}_b_raw", [P, J, D])
        b_hi = c.sb(f"{name}_b_hi", [P, J, D], F32R)
        b_lo = c.sb(f"{name}_b_lo", [P, J, D], F32R)
        g_hi = c.sb(f"{name}_g_hi", [P, J, SEQ], F32R)
        g_lo = c.sb(f"{name}_g_lo", [P, J, SEQ], F32R)
        act_out = c.sb(f"{name}_act", [P, 2, SEQ])
        prod = c.sb(f"{name}_prod", [P, 2, SEQ])
        route = None if swiglu else c.sb(f"{name}_route", [P, J, SEQ])
        u_ps = [[c.ps(f"{name}_u{a}{b}", [P, SEQ]) for b in range(PJ)] for a in range(2)]
        y_ps = [c.ps(f"{name}_y{a}", [P, SEQ]) for a in range(4)]
        norm = NormStage(c, name, hT, norm_g, y_ps[0], act_out, prod,
                         c.sb(f"{name}_stat", [P, 2, SEQ])) if swiglu else None

        a_landed = [c.sem(f"{name}_a_landed{s}") for s in range(RING)]
        b_landed = [c.sem(f"{name}_b_landed{s}") for s in range(J)]
        r_landed = [] if swiglu else [c.sem(f"{name}_r_landed{s}") for s in range(J)]
        (a_high, a_split, b_high, b_split, up_done, act_done, prod_done, hid_high, hid_split, y_done,
         y_added) = named = [c.sem(f"{name}_{x}") for x in (
             "a_high", "a_split", "b_high", "b_split", "up_done", "act_done", "prod_done", "hid_high",
             "hid_split", "y_done", "y_added")]
        sems = [*a_landed, *b_landed, *r_landed, *named, *(norm.sems if swiglu else [])]
        A_FREE, B_FREE, Y_USED, PAIRS, HID_FREE, Y_BANKS = RING, J, 1, 2, J, 4

        def group_loop(eng, body):
            with eng.Fori(0, groups) as g:
                body(g, J)
            body(groups, rest)

        def ahead(g, count, j):
            return [k for k in range(PJ * j + 2, PJ * j + 2 + PJ) if g is not groups or k < PJ * count]

        with nc.Block() as block:
            @block.sync
            def _(sp):
                if swiglu:
                    norm.sync(sp)

                def body(g, count):
                    for j in range(count):
                        for k in range(PJ * j, PJ * (j + 1)):
                            sp.wait_ge(a_split, g * NP + k + 1)
                            sp.dma_start(a_raw[:, k % RING, :],
                                         up_w[bass.ds(g * NP + k, 1)].rearrange("o p f -> p (o f)")
                                         ).then_inc(a_landed[k % RING], 16)
                        sp.wait_ge(b_split, g * J + j + 1)
                        sp.dma_start(b_raw[:, j, :], down_w(g * J + j)).then_inc(b_landed[j], 16)
                        if not swiglu:
                            sp.wait_ge(hid_split, g * J + j + 1)
                            sp.dma_start(route[:, j, :],
                                         routing[bass.ds(g * J + j, 1)].rearrange("o p f -> p (o f)")
                                         ).then_inc(r_landed[j], 16)
                group_loop(sp, body)

            def a_high_part(g, k):
                nc.scalar.wait_ge(a_landed[k % RING], g * (NP // RING * 16) + 16 * (k // RING + 1))
                nc.scalar.wait_ge(up_done, g * NP + k + 1)
                nc.scalar.copy(a_hi[:, k % RING, :], a_raw[:, k % RING, :]).then_inc(a_high, 1)

            def a_low_part(g, k):
                nc.vector.wait_ge(a_high, g * NP + k + 1)
                nc.vector.tensor_tensor(a_lo[:, k % RING, :], a_raw[:, k % RING, :],
                                        a_hi[:, k % RING, :].bitcast(F32), ALU.subtract).then_inc(a_split, 1)

            @block.scalar
            def _(act):
                if swiglu:
                    norm.scalar_root(act)
                a_high_part(0, 0)
                a_high_part(0, 1)
                if swiglu:
                    norm.scalar_high(act, x_hi)

                def body(g, count):
                    for j in range(count):
                        for k in ahead(g, count, j):
                            a_high_part(g, k)
                        act.wait_ge(up_done, g * NP + PJ * j + 1 + A_FREE)
                        act.wait_ge(prod_done, g * J + j + 1)
                        act.activation(act_out[:, j % 2, :], u_ps[j % 2][0][:],
                                       ACT.Silu if swiglu else ACT.Gelu_apprx_tanh).then_inc(act_done, 1)
                        act.wait_ge(b_landed[j], g * 16 + 16)
                        act.wait_ge(y_done, g * KC + Y_USED)
                        act.copy(b_hi[:, j, :], b_raw[:, j, :]).then_inc(b_high, 1)
                        act.wait_ge(prod_done, g * J + j + 1 + PAIRS)
                        act.copy(g_hi[:, j, :], prod[:, j % 2, :]).then_inc(hid_high, 1)
                group_loop(act, body)

            @block.vector
            def _(dve):
                dve.sem_inc(a_split, A_FREE)
                dve.sem_inc(prod_done, PAIRS)
                dve.sem_inc(hid_split, HID_FREE)
                dve.sem_inc(y_added, Y_BANKS)
                if swiglu:
                    norm.vector_inverse(dve)
                a_low_part(0, 0)
                a_low_part(0, 1)
                if swiglu:
                    norm.vector_split(dve, x_hi, x_lo)
                for k in ahead(0, J, 0):
                    a_low_part(0, k)

                def body(g, count):
                    for j in range(count):
                        for k in ahead(g, count, j) if j else []:
                            a_low_part(g, k)
                        dve.wait_ge(act_done, g * J + j + 1)
                        dve.wait_ge(hid_split, g * J + j - 1 + HID_FREE)
                        if swiglu:
                            dve.wait_ge(up_done, g * NP + PJ * j + 2 + A_FREE)
                            dve.scalar_tensor_tensor(prod[:, j % 2, :], act_out[:, j % 2, :], 0.5,
                                                     u_ps[j % 2][1][:], ALU.mult, ALU.mult
                                                     ).then_inc(prod_done, 1)
                        else:
                            dve.wait_ge(r_landed[j], g * 16 + 16)
                            dve.tensor_tensor(prod[:, j % 2, :], act_out[:, j % 2, :], route[:, j, :], ALU.mult
                                              ).then_inc(prod_done, 1)
                        dve.wait_ge(hid_high, g * J + j + 1)
                        dve.tensor_tensor(g_lo[:, j, :], prod[:, j % 2, :], g_hi[:, j, :].bitcast(F32),
                                          ALU.subtract).then_inc(hid_split, 1)
                    for k in ahead(g, count, J) if g is not groups else []:
                        a_low_part(g, k)
                    for f in range(KC):
                        dve.wait_ge(y_done, g * KC + f + 1 + Y_USED)
                        dve.tensor_tensor(hT[:, f, :], hT[:, f, :], y_ps[f % 4][:], ALU.add
                                          ).then_inc(y_added, 1)
                group_loop(dve, body)

            @block.gpsimd
            def _(pool):
                if swiglu:
                    norm.gpsimd(pool)
                pool.sem_inc(b_split, B_FREE)

                def body(g, count):
                    for j in range(count):
                        pool.wait_ge(b_high, g * J + j + 1)
                        pool.tensor_tensor(b_lo[:, j, :], b_raw[:, j, :], b_hi[:, j, :].bitcast(F32),
                                           ALU.subtract).then_inc(b_split, 1)
                group_loop(pool, body)

            @block.tensor
            def _(pe):
                pe.sem_inc(up_done, A_FREE)
                pe.sem_inc(y_done, Y_USED)
                if swiglu:
                    norm.tensor(pe)

                def up(g, j):
                    pe.wait_ge(prod_done, g * J + (j + 1))
                    for k in range(PJ * j, PJ * (j + 1)):
                        pe.wait_ge(a_split, g * NP + (k + 1 + A_FREE))
                        s = k % RING
                        for kc in range(KC):
                            if swiglu and k == 0:
                                pe.wait_ge(norm.x_split, kc + 1)
                            cols = slice(kc * P, (kc + 1) * P)
                            last = three_products(pe, u_ps[j % 2][k % PJ][:], a_hi[:, s, cols],
                                                  a_lo[:, s, cols], x_hi[:, kc, :], x_lo[:, kc, :], kc == 0,
                                                  kc == KC - 1)
                        last.then_inc(up_done, 1)

                up(0, 0)

                def body(g, count):
                    for j in range(1, count if g is groups else J + 1):
                        up(g, j)
                    for f in range(KC):
                        pe.wait_ge(y_added, g * KC + f + 1)
                        for j in range(count):
                            if f == 0:
                                pe.wait_ge(b_split, g * J + j + 1 + B_FREE)
                                pe.wait_ge(hid_split, g * J + j + 1 + HID_FREE)
                            cols = slice(f * P, (f + 1) * P)
                            last = three_products(pe, y_ps[f % 4][:], b_hi[:, j, cols], b_lo[:, j, cols],
                                                  g_hi[:, j, :], g_lo[:, j, :], j == 0, j == count - 1)
                        last.then_inc(y_done, 1)
                group_loop(pe, body)
    clear_semaphores(nc, sems)


class Projection:

    def __init__(self, c, name, w, x_hi, x_lo, dst, add=False):
        self.w, self.x_hi, self.x_lo, self.dst, self.add = w, x_hi, x_lo, dst, add
        self.n = w.shape[0]
        self.kc = w.shape[2] // P
        self.raw = c.sb(f"{name}_raw", [P, RING, self.kc * P])
        self.hi = c.sb(f"{name}_hi", [P, RING, self.kc * P], F32R)
        self.lo = c.sb(f"{name}_lo", [P, RING, self.kc * P], F32R)
        self.ps = [c.ps(f"{name}_ps{s}", [P, SEQ]) for s in range(RING)]
        self.landed = [c.sem(f"{name}_landed{s}") for s in range(RING)]
        self.high, self.split, self.product, self.taken = (
            c.sem(f"{name}_{x}") for x in ("high", "split", "product", "taken"))
        self.sems = [*self.landed, self.high, self.split, self.product, self.taken]
        self.groups, self.rest = divmod(self.n - 1, RING)
        self.rest += 1

    def loop(self, eng, body):
        if self.groups:
            with eng.Fori(0, self.groups) as g:
                body(g, RING)
        body(self.groups, self.rest)

    def sync(self, sp):
        def body(g, count):
            for k in range(count):
                sp.wait_ge(self.split, g * RING + k + 1)
                sp.dma_start(self.raw[:, k, :], self.w[bass.ds(g * RING + k, 1)].rearrange("o p f -> p (o f)")
                             ).then_inc(self.landed[k], 16)
        self.loop(sp, body)

    def scalar(self, act, then=None):
        def high(g, k):
            act.wait_ge(self.landed[k % RING], g * 16 + 16 * (k // RING + 1))
            act.wait_ge(self.product, g * RING + k + 1)
            act.copy(self.hi[:, k % RING, :], self.raw[:, k % RING, :]).then_inc(self.high, 1)

        for k in range(min(2, self.n)):
            high(0, k)
        if then is not None:
            then(act)

        def body(g, count):
            for k in range(count):
                if g is not self.groups or k + 2 < count:
                    high(g, k + 2)
                if not self.add:
                    act.wait_ge(self.product, g * RING + k + 1 + RING)
                    act.copy(self.dst[:, bass.ds(g * RING + k, 1), :].rearrange("p o s -> p (o s)"),
                             self.ps[k][:]).then_inc(self.taken, 1)
        self.loop(act, body)

    def vector(self, dve, then=None):
        dve.sem_inc(self.split, RING)

        def low(g, k):
            dve.wait_ge(self.high, g * RING + k + 1)
            dve.tensor_tensor(self.lo[:, k % RING, :], self.raw[:, k % RING, :],
                              self.hi[:, k % RING, :].bitcast(F32), ALU.subtract).then_inc(self.split, 1)

        for k in range(min(2, self.n)):
            low(0, k)
        if then is not None:
            then(dve)

        def body(g, count):
            for k in range(count):
                if g is not self.groups or k + 2 < count:
                    low(g, k + 2)
                if self.add:
                    dve.wait_ge(self.product, g * RING + k + 1 + RING)
                    old = self.dst[:, bass.ds(g * RING + k, 1), :].rearrange("p o s -> p (o s)")
                    dve.tensor_tensor(old, old, self.ps[k][:], ALU.add).then_inc(self.taken, 1)
        self.loop(dve, body)

    def tensor(self, pe, x_ready=None):
        pe.sem_inc(self.product, RING)
        pe.sem_inc(self.taken, RING)

        def body(g, count):
            for k in range(count):
                pe.wait_ge(self.split, g * RING + k + 1 + RING)
                pe.wait_ge(self.taken, g * RING + k + 1)
                for kc in range(self.kc):
                    if x_ready is not None and k == 0:
                        pe.wait_ge(x_ready, kc + 1)
                    cols = slice(kc * P, (kc + 1) * P)
                    last = three_products(pe, self.ps[k][:], self.hi[:, k, cols], self.lo[:, k, cols],
                                          self.x_hi[:, kc, :], self.x_lo[:, kc, :], kc == 0, kc == self.kc - 1)
                last.then_inc(self.product, 1)
        self.loop(pe, body)


class PanelStream:

    def __init__(self, c, name, w, x_hi, x_lo, result, function):
        self.w, self.x_hi, self.x_lo, self.result, self.n = w, x_hi, x_lo, result, w.shape[0]
        self.function = function
        self.raw = c.sb(f"{name}_raw", [P, RING, PANEL])
        self.hi = c.sb(f"{name}_hi", [P, RING, PANEL], F32R)
        self.lo = c.sb(f"{name}_lo", [P, RING, PANEL], F32R)
        self.out = c.sb(f"{name}_out", [P, 2, SEQ])
        self.ps = [c.ps(f"{name}_ps{s}", [P, SEQ]) for s in range(2)]
        self.landed = [c.sem(f"{name}_landed{s}") for s in range(RING)]
        self.stored = [c.sem(f"{name}_stored{s}") for s in range(2)]
        self.high, self.split, self.product, self.active = (
            c.sem(f"{name}_{x}") for x in ("high", "split", "product", "active"))
        self.sems = [*self.landed, *self.stored, self.high, self.split, self.product, self.active]

    def sync(self, sp):
        for s in self.stored:
            sp.sem_inc(s, 16)

        def load(g, k):
            sp.wait_ge(self.split, g * RING + k + 1)
            sp.dma_start(self.raw[:, k, :], self.w[bass.ds(g * RING + k, 1)].rearrange("o p f -> p (o f)")
                         ).then_inc(self.landed[k], 16)

        def store(g, k):
            sp.wait_ge(self.active, g * RING + k + 1 + 2)
            sp.dma_start(self.result[bass.ds(g * RING + k, 1)].rearrange("o p f -> p (o f)"),
                         self.out[:, k % 2, :]).then_inc(self.stored[k % 2], 16)

        groups = self.n // RING
        for k in range(RING):
            load(0, k)
        with sp.Fori(0, groups - 1) as g:
            for k in range(RING):
                load(g + 1, k)
                store(g, k)
        for k in range(RING):
            store(groups - 1, k)
        for s in self.stored:
            sp.wait_ge(s, 16 + 16 * (self.n // 2))

    def start_high(self, act):
        act.sem_inc(self.active, 2)
        self.high_part(act, 0, 0)
        self.high_part(act, 0, 1)

    def start_low(self, eng):
        eng.sem_inc(self.split, RING)

    def start_tensor(self, pe):
        pe.sem_inc(self.product, RING)

    def high_part(self, act, g, k):
        s = k % RING
        act.wait_ge(self.landed[s], g * 16 + 16 * (k // RING + 1))
        act.wait_ge(self.product, g * RING + (k + 1))
        act.copy(self.hi[:, s, :], self.raw[:, s, :]).then_inc(self.high, 1)

    def scalar(self, act, g, k, ends):
        if not ends or g * RING + k + 2 < self.n:
            self.high_part(act, g, k + 2)
        s = k % 2
        act.wait_ge(self.product, g * RING + (k + 1 + RING))
        act.wait_ge(self.stored[s], g * (RING // 2 * 16) + 16 * (k // 2 + 1))
        act.activation(self.out[:, s, :], self.ps[s][:], self.function).then_inc(self.active, 1)

    def low(self, eng, g, k):
        s = k % RING
        eng.wait_ge(self.high, g * RING + (k + 1))
        eng.tensor_tensor(self.lo[:, s, :], self.raw[:, s, :], self.hi[:, s, :].bitcast(F32), ALU.subtract
                          ).then_inc(self.split, 1)

    def tensor(self, pe, g, k, part=slice(0, KC)):
        s = k % RING
        if part.start == 0:
            pe.wait_ge(self.split, g * RING + (k + 1 + RING))
            pe.wait_ge(self.active, g * RING + (k + 1))
        for kc in range(part.start, part.stop):
            cols = slice(kc * P, (kc + 1) * P)
            last = three_products(pe, self.ps[k % 2][:], self.hi[:, s, cols], self.lo[:, s, cols],
                                  self.x_hi[:, kc, :], self.x_lo[:, kc, :], kc == 0, kc == KC - 1)
        if part.stop == KC:
            last.then_inc(self.product, 1)


class Attention:

    def __init__(self, c, name, units, scale, ident, stream=None):
        self.units, self.scale, self.ident, self.stream = units, scale, ident, stream
        if stream is not None:
            self.every = len(units) // stream.n
            self.share = KC // self.every
        n = len(units)
        self.biased = c.sb(f"{name}_biased", [P, 2, SEQ])
        self.probs = c.sb(f"{name}_probs", [P, 2, SEQ])
        self.probsT = c.sb(f"{name}_probsT", [P, 2, SEQ])
        self.top = c.sb(f"{name}_top", [P, n])
        self.shift = c.sb(f"{name}_shift", [P, n])
        self.total = c.sb(f"{name}_total", [P, n])
        self.inverse = c.sb(f"{name}_inverse", [P, n])
        self.s_ps = [c.ps(f"{name}_s{i}", [P, SEQ]) for i in range(2)]
        self.t_ps = [c.ps(f"{name}_t{i}", [P, SEQ]) for i in range(2)]
        self.o_ps = [c.ps(f"{name}_o{i}", [P, SEQ]) for i in range(2)]
        (self.scored, self.maxed, self.shifted, self.exped, self.turned, self.copied, self.weighted,
         self.inverted, self.gated, self.stored) = self.sems = [
            c.sem(f"{name}_{x}") for x in ("scored", "maxed", "shifted", "exped", "turned", "copied",
                                           "weighted", "inverted", "gated", "stored")]
        self.gated_units = 0

    def vector(self, dve):
        n = len(self.units)
        for i in range(n + 3):
            if i < n:
                u, w = self.units[i], self.units[i]["width"]
                dve.wait_ge(self.scored, i + 1)
                if i >= 2:
                    dve.wait_ge(self.exped, i - 1)
                dve.tensor_tensor_reduce(out=self.biased[:, i % 2, :w], in0=self.s_ps[i % 2][:, :w], in1=u["bias"],
                                         scale=1.0, scalar=-3.0e38, op0=ALU.add, op1=ALU.max,
                                         accum_out=self.top[:, i:i + 1]).then_inc(self.maxed, 1)
                dve.wait_ge(self.maxed, i + 1)
                dve.tensor_scalar(self.shift[:, i:i + 1], self.top[:, i:i + 1], -self.scale, None, ALU.mult
                                  ).then_inc(self.shifted, 1)
            if i >= 3:
                j = i - 3
                dve.wait_ge(self.exped, j + 1)
                u, inverse = self.units[j], self.inverse[:, j:j + 1]
                dve.reciprocal(inverse, self.total[:, j:j + 1]).then_inc(self.inverted, 1)
                dve.wait_ge(self.inverted, j + 1)
                if u["gate"] is not None:
                    self.gated_units += 1
                    dve.tensor_tensor(inverse, inverse, u["gate"], ALU.mult).then_inc(self.gated, 1)
                    dve.wait_ge(self.gated, self.gated_units)
                dve.wait_ge(self.weighted, j + 1)
                result = self.o_ps[j % 2][:, :u["dv"]]
                if u["add"]:
                    dve.wait_ge(self.stored, j)
                    done = dve.scalar_tensor_tensor(u["out"], result, inverse, u["out"], ALU.mult, ALU.add)
                else:
                    done = dve.tensor_scalar(u["out"], result, inverse, None, ALU.mult)
                done.then_inc(self.stored, 1)

    def scalar(self, act):
        n = len(self.units)
        if self.stream is not None:
            self.stream.start_high(act)
        for i in range(n + 1):
            if self.stream is not None and i >= self.every and i % self.every == 0:
                self.stream.scalar(act, 0, i // self.every - 1, ends=True)
            if i < n:
                w = self.units[i]["width"]
                act.wait_ge(self.shifted, i + 1)
                if i >= 2:
                    act.wait_ge(self.turned, i - 1)
                act.activation(self.probs[:, i % 2, :w], self.biased[:, i % 2, :w], ACT.Exp, scale=self.scale,
                               bias=self.shift[:, i:i + 1], accum_out=self.total[:, i:i + 1]
                               ).then_inc(self.exped, 1)
            if i >= 1:
                j, w = i - 1, self.units[i - 1]["width"]
                act.wait_ge(self.turned, j + 1)
                if j >= 2:
                    act.wait_ge(self.weighted, j - 1)
                act.copy(self.probsT[:, j % 2, :w], self.t_ps[j % 2][:, :w]).then_inc(self.copied, 1)

    def tensor(self, pe):
        n = len(self.units)
        if self.stream is not None:
            self.stream.start_tensor(pe)
        for i in range(n + 2):
            if i < n:
                u = self.units[i]
                if i >= 2:
                    pe.wait_ge(self.maxed, i - 1)
                pe.matmul(self.s_ps[i % 2][:, :u["width"]], u["q"], u["k"], start=True, stop=True
                          ).then_inc(self.scored, 1)
            if 1 <= i <= n:
                j = i - 1
                pe.wait_ge(self.exped, j + 1)
                if j >= 2:
                    pe.wait_ge(self.copied, j - 1)
                for b in range(self.units[j]["width"] // P):
                    cols = slice(b * P, (b + 1) * P)
                    last = pe.transpose(self.t_ps[j % 2][:, cols], self.probs[:, j % 2, cols], self.ident[:])
                last.then_inc(self.turned, 1)
            if self.stream is not None and i < n:
                at = i % self.every * self.share
                self.stream.tensor(pe, 0, i // self.every, slice(at, at + self.share))
            if i >= 2:
                j = i - 2
                u = self.units[j]
                pe.wait_ge(self.copied, j + 1)
                if j >= 2:
                    pe.wait_ge(self.stored, j - 1)
                blocks = u["width"] // P
                for b in range(blocks):
                    last = pe.matmul(self.o_ps[j % 2][:, :u["dv"]], self.probsT[:, j % 2, b * P:(b + 1) * P],
                                     u["v"](b), start=b == 0, stop=b == blocks - 1)
                last.then_inc(self.weighted, 1)


def stream_low(stream):
    def program(pool):
        stream.start_low(pool)
        for k in range(stream.n):
            stream.low(pool, 0, k)
    return program


def norm_and_project(nc, name, hT, x_hi, x_lo, gain, w, dst, load_more=None):
    with ExitStack() as ctx:
        c = Chip(nc, ctx)
        proj = Projection(c, name, w, x_hi, x_lo, dst)
        norm = NormStage(c, name, hT, gain, c.ps(f"{name}_sum", [P, SEQ]), c.sb(f"{name}_sq", [P, 2, SEQ]),
                         c.sb(f"{name}_xn", [P, 2, SEQ]), c.sb(f"{name}_stat", [P, 2, SEQ]))
        with nc.Block() as block:
            @block.sync
            def _(sp):
                norm.sync(sp)
                proj.sync(sp)
                if load_more is not None:
                    load_more(sp)

            @block.gpsimd
            def _(pool):
                norm.gpsimd(pool)

            @block.scalar
            def _(act):
                norm.scalar_root(act)
                proj.scalar(act, lambda a: norm.scalar_high(a, x_hi))

            @block.vector
            def _(dve):
                norm.vector_inverse(dve)
                proj.vector(dve, lambda v: norm.vector_split(v, x_hi, x_lo))

            @block.tensor
            def _(pe):
                norm.tensor(pe)
                proj.tensor(pe, norm.x_split)
    clear_semaphores(nc, [*norm.sems, *proj.sems])


def project_onto(nc, name, x_hi, x_lo, w, hT):
    with ExitStack() as ctx:
        proj = Projection(Chip(nc, ctx), name, w, x_hi, x_lo, hT, add=True)
        with nc.Block() as block:
            block.sync(proj.sync)
            block.scalar(proj.scalar)
            block.vector(proj.vector)
            block.tensor(proj.tensor)
    clear_semaphores(nc, proj.sems)



A_GROUPS = 4
N_HEADS = 4
KV_LATENT = 256
IDX_HEADS = 4
IDX_DIM = 64
TILES = SEQ // P
TOPK = SEQ // 4
TAKEN = -3.4e38
FUTURE = -3.0e38
MASKED = -1e30

U0, V0, Q0, C0, QI0, KI0, WI0 = 0, 4, 8, 12, 14, 16, 17
N_PROJ1 = 18


def gate_and_prepare(nc, proj, kT, vv, wi, ident, ya_hi, ya_lo, d):
    with ExitStack() as ctx:
        c = Chip(nc, ctx)
        ones = c.sb("m1_ones", [P, P])
        wsT = c.sb("m1_wsT", [P, A_GROUPS, P])
        bs = c.sb("m1_bs", [1, A_GROUPS, P])
        vg = c.sb("m1_vg", [P, SEQ])
        vb = c.sb("m1_vb", [P, SEQ])
        gains = c.sb("m1_gains", [P, 4])
        wuk = c.sb("m1_wuk", [P, 2, P])
        wuv = c.sb("m1_wuv", [P, 2, P])
        rot = c.sb("m1_rot", [P, 2, P])
        inv = c.sb("m1_inv", [P, 2])
        posi = c.sb("m1_posi", [P, SEQ], I32)
        pos = c.sb("m1_pos", [P, SEQ])
        ang = c.sb("m1_ang", [P, SEQ])
        turns = c.sb("m1_turns", [P, SEQ])
        sin = [c.sb(f"m1_sin{i}", [P, SEQ]) for i in range(2)]
        cos = [c.sb(f"m1_cos{i}", [P, SEQ]) for i in range(2)]
        sq = c.sb("m1_sq", [P, 3 + N_HEADS, SEQ])
        ms = c.sb("m1_ms", [P, 2, SEQ])
        rstd = c.sb("m1_rstd", [P, SEQ])
        vn = c.sb("m1_vn", [P, TILES, SEQ])
        stats = c.sb("m1_stats", [P, TILES, 6])
        mv = c.sb("m1_mv", [P, TILES, 2])
        sd = c.sb("m1_sd", [P, TILES])
        turned = c.sb("m1_turned", [P, SEQ])
        banks = [c.ps(f"m1_bank{i}", [P, SEQ]) for i in range(8)]

        S = {x: c.sem(f"m1_{x}") for x in (
            "small", "positions", "const", "masked", "gelu", "vt", "ln_var", "ln_sd", "vnorm", "seq",
            "sq", "job", "took", "ms", "root", "half", "angle", "sines", "normed", "roped", "gated")}
        small, job, took, seq = S["small"], S["job"], S["took"], S["seq"]
        SMALL = ["wsT", "bs", "vg", "vb", "gains", "wuk", "wuv", "rot", "inv"]
        R128, R64 = 0, 1
        JOBS = (["sum_c", "rot_qi0", "rot_qi1", "rot_ki"] + [f"sum_q{h}" for h in range(N_HEADS)]
                + ["k", "vv", "sum_k"] + [f"rot_q{h}" for h in range(N_HEADS)] + ["rot_k", "wi"]
                + [f"z{g}" for g in range(A_GROUPS)])
        NUM = {x: i for i, x in enumerate(JOBS)}
        SQS = ["c0", "c1"] + [f"q{h}" for h in range(N_HEADS)] + ["k"]
        QK = [f"q{h}" for h in range(N_HEADS)] + ["k"]

        def bank(x):
            return banks[4 + NUM[x] % 4]

        with nc.Block() as block:
            @block.sync
            def _(sp):
                sp.dma_start(posi[:], d["positions"].rearrange("a s -> (a s)").partition_broadcast(P)
                             ).then_inc(S["positions"], 16)
                sp.dma_start(inv[:], d["inv"]).then_inc(small, 16)
                sp.dma_start(rot[:], d["rot"]).then_inc(small, 16)
                sp.dma_start(gains[:], d["gains"]).then_inc(small, 16)
                sp.dma_start(wuk[:], d["wuk"]).then_inc(small, 16)
                sp.dma_start(wuv[:], d["wuv"]).then_inc(small, 16)
                sp.dma_start(wsT[:], d["wsT"]).then_inc(small, 16)
                sp.dma_start(bs[:], d["bs"]).then_inc(small, 16)
                sp.dma_start(vg[:], d["vg"].partition_broadcast(P)).then_inc(small, 16)
                sp.dma_start(vb[:], d["vb"].partition_broadcast(P)).then_inc(small, 16)

            @block.gpsimd
            def _(pool):
                pool.memset(ones[:], 1.0).then_inc(S["const"], 1)
                pool.memset(ident[:], 0.0).then_inc(S["const"], 1)
                pool.wait_ge(S["const"], 2)
                pool.affine_select(out=ident[:], in_=ident[:], compare_op=ALU.not_equal, fill=1.0, base=0,
                                   pattern=[[-1, P]], channel_multiplier=1).then_inc(S["const"], 1)
                pool.wait_ge(small, 16 * len(SMALL))
                pool.affine_select(out=wsT[:], in_=wsT[:], compare_op=ALU.is_ge, fill=0.0, base=0,
                                   pattern=[[0, A_GROUPS], [1, P]], channel_multiplier=-1
                                   ).then_inc(S["masked"], 1)

            @block.scalar
            def _(act):
                act.activation(proj[:, U0:U0 + 8, :], proj[:, U0:U0 + 8, :], ACT.Gelu_apprx_tanh
                               ).then_inc(S["gelu"], 1)
                for i, x in enumerate(SQS[:-1]):
                    src = proj[:, C0 + i, :] if i < 2 else proj[:, Q0 + i - 2, :]
                    act.activation(sq[:, i, :], src, ACT.Square).then_inc(S["sq"], 1)
                def root(n):
                    act.wait_ge(S["ms"], n + 1)
                    act.activation(ms[:, n % 2, :], ms[:, n % 2, :], ACT.Sqrt).then_inc(S["root"], 1)
                for kind in (R128, R64):
                    act.wait_ge(S["angle"], kind + 1)
                    act.activation(sin[kind][:], ang[:], ACT.Sin).then_inc(S["sines"], 1)
                    act.activation(cos[kind][:], ang[:], ACT.Sin, scale=0.5).then_inc(S["sines"], 1)
                act.wait_ge(S["ln_var"], 1)
                act.activation(sd[:], sd[:], ACT.Sqrt).then_inc(S["ln_sd"], 1)
                for n in range(1 + N_HEADS):
                    root(n)
                act.wait_ge(took, NUM["k"] + 1)
                act.activation(sq[:, 2 + N_HEADS, :], kT[:], ACT.Square).then_inc(S["sq"], 1)
                root(1 + N_HEADS)
                for g in range(A_GROUPS):
                    act.wait_ge(S["gated"], g + 1)
                    act.copy(ya_hi[:, g, :], proj[:, U0 + g, :]).then_inc(S["half"], 1)

            @block.vector
            def _(dve):
                done = [0]

                def then(instruction):
                    done[0] += 1
                    instruction.then_inc(seq, 1)
                    dve.wait_ge(seq, done[0])

                def take(x):
                    dve.wait_ge(job, NUM[x] + 1)

                TWO_PI_1, TWO_PI_2 = 6.28125, 1.9353071795e-3
                ROUND = 12582912.0
                dve.wait_ge(S["positions"], 16)
                then(dve.tensor_copy(pos[:], posi[:]))
                dve.wait_ge(small, 16 * len(SMALL))
                for kind in (R128, R64):
                    if kind:
                        dve.wait_ge(S["sines"], 2)
                    then(dve.tensor_scalar(ang[:], pos[:], inv[:, kind:kind + 1], None, ALU.mult))
                    then(dve.tensor_scalar(turns[:], ang[:], 1.0 / (2 * 3.141592653589793), ROUND, ALU.mult,
                                           ALU.add))
                    then(dve.tensor_scalar(turns[:], turns[:], -ROUND, None, ALU.add))
                    then(dve.scalar_tensor_tensor(ang[:], turns[:], -TWO_PI_1, ang[:], ALU.mult, ALU.add))
                    then(dve.scalar_tensor_tensor(ang[:], turns[:], -TWO_PI_2, ang[:], ALU.mult, ALU.add))
                    dve.tensor_scalar(ang[:], ang[:], 3.1415925, -3.1415925, ALU.min, ALU.max
                                      ).then_inc(S["angle"], 1)
                    if kind == R64:
                        break
                    for t in range(TILES):
                        dve.wait_ge(S["vt"], t + 1)
                        then(dve.bn_stats(stats[:, t, :], banks[t][:]))
                        then(dve.bn_aggr(mv[:, t, :], stats[:, t, :]))
                    dve.tensor_scalar(sd[:], mv[:, :, 1], EPS, None, ALU.add).then_inc(S["ln_var"], 1)

                def mean_square(x, features, n):
                    take(x)
                    dve.tensor_scalar(ms[:, n % 2, :], bank(x)[:], 1.0 / features, EPS, ALU.mult, ALU.add
                                      ).then_inc(S["ms"], 1)
                    dve.wait_ge(S["ms"], n + 1)
                    dve.sem_inc(took, 1)

                def reciprocal_root(n):
                    dve.wait_ge(S["root"], n + 1)
                    then(dve.reciprocal(rstd[:], ms[:, n % 2, :]))

                def rope(x, tile, kind):
                    take(x)
                    then(dve.tensor_tensor(tile, tile, cos[kind][:], ALU.mult))
                    dve.tensor_tensor(turned[:], bank(x)[:], sin[kind][:], ALU.mult).then_inc(took, 1)
                    dve.wait_ge(took, NUM[x] + 1)
                    then(dve.tensor_tensor(tile, tile, turned[:], ALU.add))

                mean_square("sum_c", KV_LATENT, 0)
                reciprocal_root(0)
                for k in range(2):
                    dve.scalar_tensor_tensor(proj[:, C0 + k, :], proj[:, C0 + k, :], gains[:, k:k + 1], rstd[:],
                                             ALU.mult, ALU.mult).then_inc(S["normed"] if k else seq, 1)
                    if not k:
                        done[0] += 1
                for kind in (R128, R64):
                    dve.wait_ge(S["sines"], 2 * kind + 2)
                    then(dve.tensor_tensor(cos[kind][:], cos[kind][:], cos[kind][:], ALU.mult))
                    then(dve.tensor_scalar(cos[kind][:], cos[kind][:], -2.0, 1.0, ALU.mult, ALU.add))
                rope("rot_qi0", proj[:, QI0, :], R64)
                rope("rot_qi1", proj[:, QI0 + 1, :], R64)
                rope("rot_ki", proj[:, KI0, :], R64)
                for h in range(N_HEADS):
                    mean_square(f"sum_q{h}", P, 1 + h)
                    reciprocal_root(1 + h)
                    dve.scalar_tensor_tensor(proj[:, Q0 + h, :], proj[:, Q0 + h, :], gains[:, 2:3], rstd[:],
                                             ALU.mult, ALU.mult).then_inc(S["normed"], 1)
                    dve.wait_ge(S["normed"], h + 2)
                take("k")
                dve.tensor_copy(kT[:], bank("k")[:]).then_inc(took, 1)
                take("vv")
                dve.tensor_copy(vv[:].rearrange("p t n -> p (t n)"), bank("vv")[:]).then_inc(took, 1)
                mean_square("sum_k", P, 1 + N_HEADS)
                reciprocal_root(1 + N_HEADS)
                dve.scalar_tensor_tensor(kT[:], kT[:], gains[:, 3:4], rstd[:], ALU.mult, ALU.mult
                                         ).then_inc(S["normed"], 1)
                dve.wait_ge(S["normed"], N_HEADS + 2)
                for i, x in enumerate(QK):
                    rope(f"rot_{x}", kT[:] if x == "k" else proj[:, Q0 + i, :], R128)
                take("wi")
                dve.tensor_scalar(wi[:], bank("wi")[:].rearrange("p (t n) -> p t n", t=TILES)[:, :, 0:IDX_HEADS],
                                  float(IDX_HEADS) ** -0.5, None, ALU.mult).then_inc(took, 1)
                dve.wait_ge(S["ln_sd"], 1)
                then(dve.reciprocal(sd[:], sd[:]))
                for t in range(TILES):
                    then(dve.tensor_scalar(vn[:, t, :], banks[t][:], mv[:, t, 0:1], sd[:, t:t + 1], ALU.subtract,
                                           ALU.mult))
                    then(dve.tensor_tensor(vn[:, t, :], vn[:, t, :], vg[:], ALU.mult))
                    dve.tensor_tensor(vn[:, t, :], vn[:, t, :], vb[:], ALU.add).then_inc(S["vnorm"], 1)
                for g in range(A_GROUPS):
                    take(f"z{g}")
                    dve.tensor_tensor(proj[:, U0 + g, :], proj[:, U0 + g, :], bank(f"z{g}")[:], ALU.mult
                                      ).then_inc(S["gated"], 1)
                    dve.wait_ge(S["half"], g + 1)
                    then(dve.tensor_tensor(ya_lo[:, g, :], proj[:, U0 + g, :], ya_hi[:, g, :].bitcast(F32),
                                           ALU.subtract))

            @block.tensor
            def _(pe):
                def start(x):
                    if NUM[x] >= 4:
                        pe.wait_ge(took, NUM[x] - 3)

                def finish(instruction):
                    instruction.then_inc(job, 1)

                pe.wait_ge(S["const"], 3)
                pe.wait_ge(small, 16 * len(SMALL))
                pe.wait_ge(S["gelu"], 1)
                for t in range(TILES):
                    for f in range(4):
                        last = pe.transpose(banks[t][:, f * P:(f + 1) * P], proj[:, V0 + f, t * P:(t + 1) * P],
                                            ident[:])
                    last.then_inc(S["vt"], 1)
                start("sum_c")
                pe.wait_ge(S["sq"], 2)
                for k in range(2):
                    last = pe.matmul(bank("sum_c")[:], ones[:], sq[:, k, :], start=k == 0, stop=k == 1)
                finish(last)
                for x, tile in (("rot_qi0", QI0), ("rot_qi1", QI0 + 1), ("rot_ki", KI0)):
                    start(x)
                    finish(pe.matmul(bank(x)[:], rot[:, R64, :], proj[:, tile, :], start=True, stop=True))
                for h in range(N_HEADS):
                    x = f"sum_q{h}"
                    start(x)
                    pe.wait_ge(S["sq"], 3 + h)
                    finish(pe.matmul(bank(x)[:], ones[:], sq[:, 2 + h, :], start=True, stop=True))
                pe.wait_ge(S["normed"], 1)
                start("k")
                for k in range(2):
                    last = pe.matmul(bank("k")[:], wuk[:, k, :], proj[:, C0 + k, :], start=k == 0, stop=k == 1)
                finish(last)
                start("vv")
                for t in range(TILES):
                    for k in range(2):
                        last = pe.matmul(bank("vv")[:, t * P:(t + 1) * P], proj[:, C0 + k, t * P:(t + 1) * P],
                                         wuv[:, k, :], start=k == 0, stop=k == 1)
                finish(last)
                start("sum_k")
                pe.wait_ge(S["sq"], 3 + N_HEADS)
                finish(pe.matmul(bank("sum_k")[:], ones[:], sq[:, 2 + N_HEADS, :], start=True, stop=True))
                pe.wait_ge(S["normed"], 1 + N_HEADS)
                for h in range(N_HEADS):
                    start(f"rot_q{h}")
                    finish(pe.matmul(bank(f"rot_q{h}")[:], rot[:, R128, :], proj[:, Q0 + h, :], start=True,
                                     stop=True))
                start("rot_k")
                pe.wait_ge(S["normed"], N_HEADS + 2)
                finish(pe.matmul(bank("rot_k")[:], rot[:, R128, :], kT[:], start=True, stop=True))
                start("wi")
                for t in range(TILES):
                    last = pe.transpose(bank("wi")[:, t * P:(t + 1) * P], proj[:, WI0, t * P:(t + 1) * P], ident[:])
                finish(last)
                pe.wait_ge(S["masked"], 1)
                pe.wait_ge(S["vnorm"], TILES)
                for g in range(A_GROUPS):
                    start(f"z{g}")
                    for t in range(TILES):
                        out = bank(f"z{g}")[:, t * P:(t + 1) * P]
                        pe.matmul(out, vn[:, t, g * P:(g + 1) * P], wsT[:, g, :], start=True, stop=False)
                        last = pe.matmul(out, ones[0:1, :], bs[:, g, :], start=False, stop=True)
                    finish(last)
    clear_semaphores(nc, S.values())


def select_keys(nc, proj, wi, select, w_gates, x_hi, x_lo, gates):
    with ExitStack() as ctx:
        c = Chip(nc, ctx)
        relu = c.sb("sel_relu", [P, 4, SEQ])
        score = c.sb("sel_score", [P, TILES, SEQ])
        best = c.sb("sel_best", [P, 8])
        banks = [c.ps(f"sel_bank{i}", [P, SEQ]) for i in range(4)]
        S = {x: c.sem(f"sel_{x}") for x in ("logits", "relu", "added", "scored", "causal", "seq")}
        units = [(t, h) for t in range(1, TILES) for h in range(IDX_HEADS)]
        stream = PanelStream(c, "gs", w_gates, x_hi, x_lo, gates, ACT.Sigmoid)
        with nc.Block() as block:
            block.sync(stream.sync)

            @block.tensor
            def _(pe):
                stream.start_tensor(pe)
                for n, (t, h) in enumerate(units):
                    if n >= 4:
                        pe.wait_ge(S["relu"], n - 3)
                    half = slice(IDX_DIM * (h % 2), IDX_DIM * (h % 2 + 1))
                    pe.matmul(banks[n % 4][:, :(t + 1) * P], proj[half, QI0 + h // 2, t * P:(t + 1) * P],
                              proj[half, KI0, :(t + 1) * P], start=True, stop=True).then_inc(S["logits"], 1)
                for k in range(stream.n):
                    stream.tensor(pe, 0, k)

            @block.scalar
            def _(act):
                for n, (t, h) in enumerate(units):
                    act.wait_ge(S["logits"], n + 1)
                    if n >= 4:
                        act.wait_ge(S["added"], n - 3)
                    act.activation(relu[:, n % 4, :(t + 1) * P], banks[n % 4][:, :(t + 1) * P], ACT.Relu,
                                   scale=float(IDX_DIM) ** -0.5).then_inc(S["relu"], 1)
                    if n == 5:
                        stream.start_high(act)
                for k in range(stream.n):
                    stream.scalar(act, 0, k, ends=True)

            @block.gpsimd
            def _(pool):
                stream.start_low(pool)
                pool.memset(select[:, 0, :P], 0.0).then_inc(S["causal"], 1)
                pool.wait_ge(S["causal"], 1)
                pool.affine_select(out=select[:, 0, :P], in_=select[:, 0, :P], compare_op=ALU.is_ge, fill=MASKED,
                                   base=0, pattern=[[-1, P]], channel_multiplier=1).then_inc(S["causal"], 1)
                for t in range(1, TILES):
                    pool.wait_ge(S["added"], IDX_HEADS * t)
                    diagonal = score[:, t, t * P:(t + 1) * P]
                    pool.affine_select(out=diagonal, in_=diagonal, compare_op=ALU.is_ge, fill=FUTURE, base=0,
                                       pattern=[[-1, P]], channel_multiplier=1).then_inc(S["causal"], 1)
                for k in range(stream.n):
                    stream.low(pool, 0, k)

            @block.vector
            def _(dve):
                done = [0]

                def then(instruction):
                    done[0] += 1
                    instruction.then_inc(S["seq"], 1)
                    dve.wait_ge(S["seq"], done[0])

                for n, (t, h) in enumerate(units):
                    w = (t + 1) * P
                    dve.wait_ge(S["relu"], n + 1)
                    if h == 0:
                        dve.tensor_scalar(score[:, t, :w], relu[:, n % 4, :w], wi[:, t, h:h + 1], None, ALU.mult
                                          ).then_inc(S["added"], 1)
                    else:
                        dve.wait_ge(S["added"], n)
                        dve.scalar_tensor_tensor(score[:, t, :w], relu[:, n % 4, :w], wi[:, t, h:h + 1],
                                                 score[:, t, :w], ALU.mult, ALU.add).then_inc(S["added"], 1)
                for t in range(1, TILES):
                    w = (t + 1) * P
                    dve.wait_ge(S["causal"], 2 + t)
                    for _ in range(TOPK // 8):
                        then(dve.max(best[:], score[:, t, :w]))
                        then(dve.match_replace(score[:, t, :w], best[:], score[:, t, :w], TAKEN))
                    dve.tensor_scalar(select[:, t, :w], score[:, t, :w], (TAKEN + FUTURE) / 2, MASKED, ALU.is_gt,
                                      ALU.mult).then_inc(S["scored"], 1)
    clear_semaphores(nc, [*S.values(), *stream.sems])


def turn_to_features(nc, name, tok, n, hi, lo, ident):
    with ExitStack() as ctx:
        c = Chip(nc, ctx)
        banks = [c.ps(f"{name}_bank{i}", [P, SEQ]) for i in range(4)]
        turned, high, low = (c.sem(f"{name}_{x}") for x in ("turned", "high", "low"))
        with nc.Block() as block:
            @block.tensor
            def _(pe):
                for f in range(n):
                    if f >= 4:
                        pe.wait_ge(low, f - 3)
                    for t in range(TILES):
                        last = pe.transpose(banks[f % 4][:, t * P:(t + 1) * P], tok[:, t, f * P:(f + 1) * P],
                                            ident[:])
                    last.then_inc(turned, 1)

            @block.scalar
            def _(act):
                for f in range(n):
                    act.wait_ge(turned, f + 1)
                    act.copy(hi[:, f, :], banks[f % 4][:]).then_inc(high, 1)

            @block.vector
            def _(dve):
                for f in range(n):
                    dve.wait_ge(high, f + 1)
                    dve.tensor_tensor(lo[:, f, :], banks[f % 4][:], hi[:, f, :].bitcast(F32), ALU.subtract
                                      ).then_inc(low, 1)
    clear_semaphores(nc, [turned, high, low])


def attend_selected(nc, proj, kT, vv, select, ident, yb_hi, yb_lo):
    with ExitStack() as outer:
        yb = Chip(nc, outer).sb("yb", [P, TILES, N_HEADS * P])
        with ExitStack() as ctx:
            c = Chip(nc, ctx)

            def unit(t, h):
                w = (t + 1) * P
                return dict(q=proj[:, Q0 + h, t * P:(t + 1) * P], k=kT[:, :w], width=w, bias=select[:, t, :w],
                            v=lambda b: vv[:, b, :], dv=P, gate=None, add=False,
                            out=yb[:, t, h * P:(h + 1) * P])
            att = Attention(c, "att1", [unit(t, h) for t in range(TILES) for h in range(N_HEADS)],
                            float(P) ** -0.5, ident)
            with nc.Block() as block:
                block.scalar(att.scalar)
                block.vector(att.vector)
                block.tensor(att.tensor)
            clear_semaphores(nc, att.sems)
        turn_to_features(nc, "yb_turn", yb, N_HEADS, yb_hi, yb_lo, ident)


def merge_branches(nc, w, gates, ya_hi, ya_lo, yb_hi, yb_lo, m_hi, m_lo):
    with ExitStack() as ctx:
        c = Chip(nc, ctx)
        R = 3
        raw = c.sb("mg_raw", [P, R, PANEL])
        hi = c.sb("mg_hi", [P, R, PANEL], F32R)
        lo = c.sb("mg_lo", [P, R, PANEL], F32R)
        gate = c.sb("mg_gate", [P, R, 2, SEQ])
        m = c.sb("mg_m", [P, 2, SEQ])
        pa, pb = ([c.ps(f"mg_{x}{i}", [P, SEQ]) for i in range(2)] for x in ("pa", "pb"))
        landed = [c.sem(f"mg_landed{i}") for i in range(R)]
        gate_landed = [c.sem(f"mg_gate_landed{i}") for i in range(R)]
        S = {x: c.sem(f"mg_{x}") for x in ("high", "split", "product", "a", "b", "merged", "m_high", "m_split")}
        with nc.Block() as block:
            @block.sync
            def _(sp):
                for n in range(KC):
                    if n >= R:
                        sp.wait_ge(S["split"], n - R + 1)
                    sp.dma_start(raw[:, n % R, :], w[n]).then_inc(landed[n % R], 16)
                    if n >= R:
                        sp.wait_ge(S["merged"], n - R + 1)
                    sp.dma_start(gate[:, n % R], gates[2 * n:2 * n + 2].rearrange("n p s -> p n s")
                                 ).then_inc(gate_landed[n % R], 16)

            @block.scalar
            def _(act):
                def high(n):
                    act.wait_ge(landed[n % R], 16 * (n // R + 1))
                    if n >= R:
                        act.wait_ge(S["product"], n - R + 1)
                    act.copy(hi[:, n % R, :], raw[:, n % R, :]).then_inc(S["high"], 1)

                high(0)
                high(1)
                for n in range(KC):
                    if n + 2 < KC:
                        high(n + 2)
                    act.wait_ge(S["merged"], n + 1)
                    act.copy(m_hi[:, n, :], m[:, n % 2, :]).then_inc(S["m_high"], 1)

            @block.gpsimd
            def _(pool):
                for n in range(KC):
                    pool.wait_ge(S["high"], n + 1)
                    pool.tensor_tensor(lo[:, n % R, :], raw[:, n % R, :], hi[:, n % R, :].bitcast(F32),
                                       ALU.subtract).then_inc(S["split"], 1)

            @block.vector
            def _(dve):
                for n in range(KC):
                    now = gate[:, n % R]
                    dve.wait_ge(S["product"], n + 1)
                    dve.wait_ge(gate_landed[n % R], 16 * (n // R + 1))
                    dve.tensor_tensor(now[:, 0, :], now[:, 0, :], pa[n % 2][:], ALU.mult).then_inc(S["a"], 1)
                    dve.tensor_tensor(now[:, 1, :], now[:, 1, :], pb[n % 2][:], ALU.mult).then_inc(S["b"], 1)
                    dve.wait_ge(S["a"], n + 1)
                    dve.wait_ge(S["b"], n + 1)
                    if n >= 2:
                        dve.wait_ge(S["m_split"], n - 1)
                    dve.tensor_tensor(m[:, n % 2, :], now[:, 0, :], now[:, 1, :], ALU.add
                                      ).then_inc(S["merged"], 1)
                    dve.wait_ge(S["m_high"], n + 1)
                    dve.tensor_tensor(m_lo[:, n, :], m[:, n % 2, :], m_hi[:, n, :].bitcast(F32), ALU.subtract
                                      ).then_inc(S["m_split"], 1)

            @block.tensor
            def _(pe):
                for n in range(KC):
                    if n >= 2:
                        pe.wait_ge(S["merged"], n - 1)
                    pe.wait_ge(S["split"], n + 1)
                    for out, y_hi, y_lo, at in ((pa[n % 2], ya_hi, ya_lo, 0), (pb[n % 2], yb_hi, yb_lo, 4)):
                        for i in range(4):
                            cols = slice((at + i) * P, (at + i + 1) * P)
                            last = three_products(pe, out[:], hi[:, n % R, cols], lo[:, n % R, cols],
                                                  y_hi[:, i, :], y_lo[:, i, :], i == 0, i == 3)
                    last.then_inc(S["product"], 1)
    clear_semaphores(nc, [*landed, *gate_landed, *S.values()])


def first_mixer(nc, hT, x_hi, x_lo, d):
    with ExitStack() as ctx:
        c = Chip(nc, ctx)
        ya_hi, ya_lo, yb_hi, yb_lo = (c.sb(x, [P, 4, SEQ], F32R) for x in ("ya_hi", "ya_lo", "yb_hi", "yb_lo"))
        with ExitStack() as inner:
            c = Chip(nc, inner)
            proj = c.sb("m1_proj", [P, N_PROJ1, SEQ])
            norm_and_project(nc, "p1", hT, x_hi, x_lo, d["norm1_g"], d["w_in1"], proj)
            kT = c.sb("m1_kT", [P, SEQ])
            vv = c.sb("m1_vv", [P, TILES, P])
            wi = c.sb("m1_wi", [P, TILES, IDX_HEADS])
            ident = c.sb("m1_ident", [P, P])
            gate_and_prepare(nc, proj, kT, vv, wi, ident, ya_hi, ya_lo, d)
            select = c.sb("m1_select", [P, TILES, SEQ])
            select_keys(nc, proj, wi, select, d["w_gates"], x_hi, x_lo, d["gates"])
            attend_selected(nc, proj, kT, vv, select, ident, yb_hi, yb_lo)
        m_hi, m_lo = (Chip(nc, ctx).sb(x, [P, KC, SEQ], F32R) for x in ("m_hi", "m_lo"))
        merge_branches(nc, d["w_merge"], d["gates"], ya_hi, ya_lo, yb_hi, yb_lo, m_hi, m_lo)
        project_onto(nc, "wo", m_hi, m_lo, d["w_o"], hT)



PEER_HEADS = 8
N_KEYS = 128
PEER_TOPK = 16
HALVES = 2 * PEER_HEADS
SLOTS = PEER_HEADS * PEER_TOPK


EARLY_CHUNKS = (44, 36)


def route_tokens(nc, qT, subkeys, iota, rowT, colT, gateT, up_w, x_hi, x_lo, hidden):
    units = hidden.shape[0]
    with ExitStack() as ctx:
        c = Chip(nc, ctx)
        keys = c.sb("rt_keys", [P, HALVES, N_KEYS])
        ident = c.sb("rt_ident", [P, P])
        sub = c.sb("rt_sub", [P, 2, HALVES, N_KEYS])
        rest = c.sb("rt_rest", [P, HALVES, N_KEYS])
        top = c.sb("rt_top", [P, HALVES, PEER_TOPK])
        index = c.sb("rt_index", [P, HALVES, PEER_TOPK], U32)
        indexf = c.sb("rt_indexf", [P, HALVES, PEER_TOPK])
        cand = c.sb("rt_cand", [P, PEER_HEADS, PEER_TOPK, PEER_TOPK])
        cand_rest = c.sb("rt_cand_rest", [P, PEER_HEADS, PEER_TOPK * PEER_TOPK])
        best = c.sb("rt_best", [P, PEER_HEADS, PEER_TOPK])
        place = c.sb("rt_place", [P, PEER_HEADS, PEER_TOPK], U32)
        half = c.sb("rt_half", [P, 2, PEER_HEADS, PEER_TOPK], U32)
        halff = c.sb("rt_halff", [P, 2, PEER_HEADS, PEER_TOPK])
        found = c.sb("rt_found", [P, PEER_HEADS, PEER_TOPK, PEER_TOPK])
        result = c.sb("rt_result", [P, 3, PEER_HEADS, PEER_TOPK])
        total = c.sb("rt_total", [P, PEER_HEADS])
        banks = [c.ps(f"rt_bank{i}", [P, SEQ]) for i in range(4)]
        out_ps = c.ps("rt_out", [P, SEQ])
        stream = PanelStream(c, "rs", up_w, x_hi, x_lo, hidden, ACT.Gelu_apprx_tanh)
        share = units // TILES
        S = {x: c.sem(f"rt_{x}") for x in ("keys", "const", "scored", "copied", "searched", "seq", "shifted",
                                           "exped", "resulted", "turned", "stored")}
        with nc.Block() as block:
            @block.sync
            def _(sp):
                sp.dma_start(keys[:], subkeys).then_inc(S["keys"], 16)
                stream.sync(sp)

            @block.gpsimd
            def _(pool):
                stream.start_low(pool)
                pool.memset(ident[:], 0.0).then_inc(S["const"], 1)
                pool.wait_ge(S["const"], 1)
                pool.affine_select(out=ident[:], in_=ident[:], compare_op=ALU.not_equal, fill=1.0, base=0,
                                   pattern=[[-1, P]], channel_multiplier=1).then_inc(S["const"], 1)
                pool.iota(iota[:], pattern=[[1, N_KEYS]], base=0, channel_multiplier=0,
                          allow_small_or_imprecise_dtypes=True).then_inc(S["const"], 1)
                for n in range(units):
                    stream.low(pool, 0, n)

            @block.tensor
            def _(pe):
                pe.wait_ge(S["keys"], 16)
                pe.wait_ge(S["const"], 2)

                def turn(t):
                    pe.wait_ge(S["resulted"], t + 1)
                    if t >= 1:
                        pe.wait_ge(S["stored"], t)
                    for i in range(3):
                        last = pe.transpose(out_ps[:, i * P:(i + 1) * P],
                                            result[:, i].rearrange("p h k -> p (h k)"), ident[:])
                    last.then_inc(S["turned"], 1)

                def score(t):
                    for i in range(HALVES):
                        if i % 4 == 0 and t >= 1:
                            pe.wait_ge(S["copied"], 4 * (t - 1) + i // 4 + 1)
                        last = pe.matmul(banks[i // 4][:, (i % 4) * P:(i % 4 + 1) * P],
                                         qT[:, i, t * P:(t + 1) * P], keys[:, i, :], start=True, stop=True)
                        if i % 4 == 3:
                            last.then_inc(S["scored"], 1)

                stream.start_tensor(pe)
                score(0)
                for t in range(TILES):
                    if t + 1 < TILES:
                        score(t + 1)
                    for n in range(share):
                        if t >= 1 and n == share - 1:
                            turn(t - 1)
                        stream.tensor(pe, 0, t * share + n)
                turn(TILES - 1)

            @block.scalar
            def _(act):
                def copy_scores(t):
                    for b in range(4):
                        act.wait_ge(S["scored"], 4 * t + b + 1)
                        if t >= 2:
                            act.wait_ge(S["searched"], t - 1)
                        act.copy(sub[:, t % 2, 4 * b:4 * b + 4, :].rearrange("p i n -> p (i n)"), banks[b][:]
                                 ).then_inc(S["copied"], 1)

                def exps(t):
                    act.wait_ge(S["shifted"], t + 1)
                    act.activation(result[:, 2], result[:, 2], ACT.Exp).then_inc(S["exped"], 1)

                copy_scores(0)
                stream.start_high(act)
                for t in range(TILES):
                    if t + 1 < TILES:
                        copy_scores(t + 1)
                    for n in range(share):
                        if t >= 1 and n == share // 3:
                            exps(t - 1)
                        stream.scalar(act, 0, t * share + n, ends=t == TILES - 1)
                exps(TILES - 1)

            @block.vector
            def _(dve):
                done = [0]

                def all_of(instructions):
                    for instruction in instructions:
                        done[0] += 1
                        instruction.then_inc(S["seq"], 1)
                    dve.wait_ge(S["seq"], done[0])

                def top16(n, scores, left, values, places):
                    all_of(dve.max(values(i)[:, 0:8], scores(i)) for i in range(n))
                    all_of(dve.match_replace(left(i), values(i)[:, 0:8], scores(i), TAKEN) for i in range(n))
                    all_of(dve.max(values(i)[:, 8:16], left(i)) for i in range(n))
                    all_of(dve.max_index(places(i)[:, 0:8], values(i)[:, 0:8], scores(i)) for i in range(n))
                    all_of(dve.max_index(places(i)[:, 8:16], values(i)[:, 8:16], left(i)) for i in range(n))

                def finish(t):
                    dve.wait_ge(S["exped"], t + 1)
                    all_of([dve.tensor_reduce(total[:], result[:, 2], AX.X, ALU.add)])
                    all_of([dve.reciprocal(total[:], total[:])])
                    dve.tensor_tensor(result[:, 2], result[:, 2], total[:].unsqueeze(2).broadcast_to(small),
                                      ALU.mult).then_inc(S["resulted"], 1)

                def keep(t):
                    dve.wait_ge(S["turned"], t + 1)
                    cols = slice(t * P, (t + 1) * P)
                    for i, to in enumerate((rowT, colT, gateT)):
                        last = dve.tensor_copy(to[:, cols], out_ps[:, i * P:(i + 1) * P])
                        if i < 2:
                            all_of([last])
                    last.then_inc(S["stored"], 1)

                small = [P, PEER_HEADS, PEER_TOPK]
                dve.wait_ge(S["const"], 3)
                for t in range(TILES):
                    dve.wait_ge(S["copied"], 4 * t + 4)
                    top16(HALVES, lambda i: sub[:, t % 2, i, :], lambda i: rest[:, i, :], lambda i: top[:, i, :],
                          lambda i: index[:, i, :])
                    all_of([dve.tensor_copy(indexf[:], index[:])])
                    by_half = top[:].rearrange("p (h two) k -> p h two k", two=2)
                    dve.sem_inc(S["searched"], 1)
                    if t >= 1:
                        finish(t - 1)
                    shape = [P, PEER_HEADS, PEER_TOPK, PEER_TOPK]
                    all_of([dve.tensor_tensor(cand[:], by_half[:, :, 0, :].unsqueeze(3).broadcast_to(shape),
                                              by_half[:, :, 1, :].unsqueeze(2).broadcast_to(shape), ALU.add)])
                    flat = cand[:].rearrange("p h a b -> p h (a b)")
                    top16(PEER_HEADS, lambda i: flat[:, i, :], lambda i: cand_rest[:, i, :],
                          lambda i: best[:, i, :], lambda i: place[:, i, :])
                    all_of([dve.tensor_scalar(half[:, 0], place[:], 4, None, ALU.logical_shift_right),
                            dve.tensor_scalar(half[:, 1], place[:], 15, None, ALU.bitwise_and)])
                    all_of([dve.tensor_copy(halff[:], half[:])])
                    ranks = iota[:, 0:PEER_TOPK].unsqueeze(1).unsqueeze(1).broadcast_to(shape)
                    keys_of = indexf[:].rearrange("p (h two) k -> p h two k", two=2)
                    if t >= 1:
                        keep(t - 1)
                    for side in range(2):
                        all_of([dve.tensor_tensor(found[:], halff[:, side].unsqueeze(3).broadcast_to(shape),
                                                  ranks, ALU.is_equal)])
                        all_of([dve.tensor_tensor(found[:], found[:],
                                                  keys_of[:, :, side, :].unsqueeze(2).broadcast_to(shape),
                                                  ALU.mult)])
                        all_of([dve.tensor_reduce(result[:, side], found[:], AX.X, ALU.add)])
                    dve.tensor_tensor(result[:, 2], best[:], best[:, :, 0:1].broadcast_to(small), ALU.subtract
                                      ).then_inc(S["shifted"], 1)
                finish(TILES - 1)
                keep(TILES - 1)
                dve.wait_ge(S["stored"], TILES)
    clear_semaphores(nc, [*S.values(), *stream.sems])


def build_routing(nc, iota, rowT, colT, gateT, routing, up_w, x_hi, x_lo, hidden):
    B = 8
    BLOCK = 64
    steps = BLOCK // B
    n_blocks = SEQ // BLOCK
    units = (hidden.shape[0] - RING) // n_blocks
    every = steps // units
    with ExitStack() as ctx:
        c = Chip(nc, ctx)
        hot = c.sb("br_hot", [P, 2, B, N_KEYS])
        row_hot = c.sb("br_row", [P, 2, B, N_KEYS])
        col_hot = c.sb("br_col", [P, 2, B, N_KEYS])
        block_out = c.sb("br_out", [P, 2, N_KEYS, BLOCK])
        banks = [c.ps(f"br_bank{i}", [P, 4, N_KEYS]) for i in range(4)]
        stream = PanelStream(c, "bs", up_w, x_hi, x_lo, hidden, ACT.Gelu_apprx_tanh)
        S = {x: c.sem(f"br_{x}") for x in ("hot", "rows", "cols", "product", "taken", "stored0", "stored1")}
        stored = [S["stored0"], S["stored1"]]
        to = routing.rearrange("j i s -> i j s")
        shape = [P, B, N_KEYS]
        keys = iota[:].unsqueeze(1).broadcast_to(shape)
        with nc.Block() as block:
            def both(eng, body, unit=None):
                with eng.Fori(0, n_blocks // 2) as b2:
                    for o in range(2):
                        for step in range(steps):
                            if unit is not None and step % every == 0:
                                unit(b2 * (2 * units // RING), o * units + step // every, False)
                            body(b2, o, step, b2 * (2 * steps) + (o * steps + step), step % 2)
                if unit is not None:
                    for k in range(RING):
                        unit(n_blocks * units // RING, k, True)

            @block.vector
            def _(dve):
                def body(b2, o, step, n, k):
                    at = bass.ds(n * B, B)
                    dve.wait_ge(S["rows"], n + 1)
                    dve.tensor_tensor(hot[:, k], keys, rowT[:, at].unsqueeze(2).broadcast_to(shape),
                                      ALU.is_equal).then_inc(S["hot"], 1)
                    dve.wait_ge(S["product"], n + 1)
                    dve.tensor_tensor(col_hot[:, k], keys, colT[:, at].unsqueeze(2).broadcast_to(shape),
                                      ALU.is_equal).then_inc(S["cols"], 1)
                both(dve, body)

            @block.gpsimd
            def _(pool):
                pool.sem_inc(S["rows"], 2)
                stream.start_low(pool)

                def body(b2, o, step, n, k):
                    pool.wait_ge(S["hot"], n + 1)
                    pool.wait_ge(S["product"], n + 1)
                    pool.tensor_tensor(row_hot[:, k], hot[:, k],
                                       gateT[:, bass.ds(n * B, B)].unsqueeze(2).broadcast_to(shape), ALU.mult
                                       ).then_inc(S["rows"], 1)
                both(pool, body, lambda g, k, ends: stream.low(pool, g, k))

            @block.tensor
            def _(pe):
                pe.sem_inc(S["product"], 2)
                stream.start_tensor(pe)

                def body(b2, o, step, n, k):
                    pe.wait_ge(S["rows"], n + 1 + 2)
                    pe.wait_ge(S["cols"], n + 1)
                    pe.wait_ge(S["taken"], n + 1)
                    for b in range(B):
                        last = pe.matmul(banks[2 * k + b // 4][:, b % 4, :], row_hot[:, k, b, :],
                                         col_hot[:, k, b, :], start=True, stop=True)
                    last.then_inc(S["product"], 1)
                both(pe, body, lambda g, k, ends: stream.tensor(pe, g, k))

            @block.scalar
            def _(act):
                act.sem_inc(S["taken"], 2)
                for o in range(2):
                    act.sem_inc(stored[o], 16)
                stream.start_high(act)

                def body(b2, o, step, n, k):
                    act.wait_ge(S["product"], n + 1 + 2)
                    act.wait_ge(stored[o], b2 * 16 + 16)
                    for i in range(2):
                        at = step * B + 4 * i
                        last = act.copy(block_out[:, o, :, at:at + 4].rearrange("p n b -> p b n"),
                                        banks[2 * k + i][:])
                    last.then_inc(S["taken"], 1)
                    if step == steps - 1:
                        act.wait_ge(S["taken"], n + 1 + 2)
                        act.dma_start(to[:, :, bass.ds(b2 * (2 * BLOCK) + o * BLOCK, BLOCK)], block_out[:, o]
                                      ).then_inc(stored[o], 16)
                both(act, body, lambda g, k, ends: stream.scalar(act, g, k, ends))
                for o in range(2):
                    act.wait_ge(stored[o], 16 + 16 * (n_blocks // 2))

            @block.sync
            def _(sp):
                stream.sync(sp)
    clear_semaphores(nc, [*S.values(), *stream.sems])


def add_chunks(nc, name, hT, hidden, routing, down_w):
    J = 4
    n_groups = hidden.shape[0] // J
    with ExitStack() as ctx:
        c = Chip(nc, ctx)
        b_raw = c.sb(f"{name}_b_raw", [P, J, D])
        b_hi = c.sb(f"{name}_b_hi", [P, 2 * J, D], F32R)
        b_lo = c.sb(f"{name}_b_lo", [P, 2 * J, D], F32R)
        g_hi = c.sb(f"{name}_g_hi", [P, 2 * J, SEQ], F32R)
        g_lo = c.sb(f"{name}_g_lo", [P, 2 * J, SEQ], F32R)
        unit = c.sb(f"{name}_unit", [P, J, SEQ])
        route = c.sb(f"{name}_route", [P, J, SEQ])
        prod = c.sb(f"{name}_prod", [P, 2, SEQ])
        y_ps = [c.ps(f"{name}_y{f}", [P, SEQ]) for f in range(KC)]
        b_landed = [c.sem(f"{name}_b_landed{s}") for s in range(J)]
        h_landed = [c.sem(f"{name}_h_landed{s}") for s in range(J)]
        b_high, b_split, prod_done, hid_high, hid_split, y_done, y_added = named = [
            c.sem(f"{name}_{x}") for x in ("b_high", "b_split", "prod_done", "hid_high", "hid_split", "y_done",
                                           "y_added")]

        def pairs(eng, body):
            with eng.Fori(0, n_groups // 2 - 1) as p:
                for half in range(2):
                    body(p, half, False)
            for half in range(2):
                body(n_groups // 2 - 1, half, half == 1)

        with nc.Block() as block:
            @block.sync
            def _(sp):
                def body(p, half, ends):
                    for j in range(J):
                        n = p * (2 * J) + (half * J + j)
                        sp.wait_ge(prod_done, n + 1)
                        sp.dma_start(unit[:, j, :], hidden[bass.ds(n, 1)].rearrange("o p f -> p (o f)")
                                     ).then_inc(h_landed[j], 16)
                        sp.dma_start(route[:, j, :], routing[bass.ds(n, 1)].rearrange("o p f -> p (o f)")
                                     ).then_inc(h_landed[j], 16)
                        sp.wait_ge(b_split, n + 1)
                        sp.dma_start(b_raw[:, j, :], down_w(n)).then_inc(b_landed[j], 16)
                pairs(sp, body)

            @block.scalar
            def _(act):
                def body(p, half, ends):
                    for j in range(J):
                        i = half * J + j
                        act.wait_ge(y_done, p * (2 * KC) + (half + 1) * KC)
                        act.wait_ge(prod_done, p * (2 * J) + (i + 1 + J))
                        act.copy(g_hi[:, i, :], prod[:, j % 2, :]).then_inc(hid_high, 1)
                        act.wait_ge(b_landed[j], p * 32 + (16 * half + 16))
                        act.copy(b_hi[:, i, :], b_raw[:, j, :]).then_inc(b_high, 1)
                pairs(act, body)

            @block.gpsimd
            def _(pool):
                pool.sem_inc(b_split, J)

                def body(p, half, ends):
                    for j in range(J):
                        i = half * J + j
                        pool.wait_ge(b_high, p * (2 * J) + (i + 1))
                        pool.tensor_tensor(b_lo[:, i, :], b_raw[:, j, :], b_hi[:, i, :].bitcast(F32),
                                           ALU.subtract).then_inc(b_split, 1)
                pairs(pool, body)

            @block.vector
            def _(dve):
                dve.sem_inc(prod_done, J)
                dve.sem_inc(hid_split, 2)
                dve.sem_inc(y_added, KC)

                def one_unit(p, i):
                    n, s, j = p * (2 * J) + i, i % (2 * J), i % J
                    dve.wait_ge(h_landed[j], p * 64 + 32 * (i // J + 1))
                    dve.wait_ge(hid_split, n + 1)
                    dve.tensor_tensor(prod[:, j % 2, :], unit[:, j, :], route[:, j, :], ALU.mult
                                      ).then_inc(prod_done, 1)
                    dve.wait_ge(hid_high, n + 1)
                    dve.tensor_tensor(g_lo[:, s, :], prod[:, j % 2, :], g_hi[:, s, :].bitcast(F32),
                                      ALU.subtract).then_inc(hid_split, 1)

                for j in range(J):
                    one_unit(0, j)

                def body(p, half, ends):
                    for f in range(KC):
                        dve.wait_ge(y_done, p * (2 * KC) + (half * KC + f + 1 + 2 * KC))
                        dve.tensor_tensor(hT[:, f, :], hT[:, f, :], y_ps[f][:], ALU.add).then_inc(y_added, 1)
                        if f < J and not ends:
                            one_unit(p, (half + 1) * J + f)
                pairs(dve, body)

            @block.tensor
            def _(pe):
                pe.sem_inc(y_done, 2 * KC)

                def body(p, half, ends):
                    for f in range(KC):
                        pe.wait_ge(y_added, p * (2 * KC) + (half * KC + f + 1))
                        for j in range(J):
                            i = half * J + j
                            if f == 0:
                                pe.wait_ge(b_split, p * (2 * J) + (i + 1 + J))
                                pe.wait_ge(hid_split, p * (2 * J) + (i + 1 + 2))
                            cols = slice(f * P, (f + 1) * P)
                            last = three_products(pe, y_ps[f][:], b_hi[:, i, cols], b_lo[:, i, cols],
                                                  g_hi[:, i, :], g_lo[:, i, :], j == 0, j == J - 1)
                        last.then_inc(y_done, 1)
                pairs(pe, body)
    clear_semaphores(nc, [*b_landed, *h_landed, *named])


def experts(nc, hT, x_hi, x_lo, d, routing, hidden):
    searching, building = EARLY_CHUNKS
    early = searching + building
    up_w = d["peer_u"]
    with ExitStack() as ctx:
        c = Chip(nc, ctx)
        iota = c.sb("ex_iota", [P, N_KEYS])
        rowT, colT, gateT = (c.sb(f"ex_{x}", [P, SEQ]) for x in ("rowT", "colT", "gateT"))
        with ExitStack() as inner:
            qT = Chip(nc, inner).sb("ex_qT", [P, HALVES, SEQ])
            norm_and_project(nc, "pq", hT, x_hi, x_lo, d["norm2_g"], d["peer_wq"], qT)
            route_tokens(nc, qT, d["subkeys"], iota, rowT, colT, gateT, up_w[0:searching], x_hi, x_lo,
                         hidden[0:searching])
        build_routing(nc, iota, rowT, colT, gateT, routing, up_w[searching:early], x_hi, x_lo,
                      hidden[searching:early])
    rows = d["peer_v"].rearrange("(i j) f -> i j f", j=N_KEYS)

    def down(start):
        return lambda n: rows[:, bass.ds(start + n, 1), :].rearrange("i o f -> i (o f)")
    add_chunks(nc, "early", hT, hidden, routing[0:early], down(0))
    hidden_stage(nc, "peer", hT, x_hi, x_lo, up_w[early:], down(early), routing=routing[early:])



NSA_HEADS = 8
NSA_GROUPS = 2
NSA_HD = 64
CMP_LEN = 32
CMP_STRIDE = 16
CMP_HID = 256
CMP_BLOCKS = (SEQ - CMP_LEN) // CMP_STRIDE + 1
HG_HEADS = 4
CHUNK = 16
N_CHUNKS = SEQ // CHUNK
F_FLOOR = 1e-30
PITCH = P + CHUNK

NQ0, KCMP, VCMP, KSEL, VSEL, KWIN, VWIN, GL = 0, 4, 5, 6, 7, 8, 9, 10
N_PROJ2 = 11


def compress_and_attend(nc, proj, ident, w1k, w1_landed, vsel, vwin, gates, bias, o_tok, d):
    scale = float(NSA_HD) ** -0.5
    slopes = [2.0 ** (-8.0 * (h + 1) / NSA_HEADS) / scale for h in range(NSA_HEADS)]
    NB = CMP_BLOCKS
    with ExitStack() as ctx:
        c = Chip(nc, ctx)
        w1v = c.sb("cp_w1v", [P, CMP_LEN, CMP_HID])
        w2k = c.sb("cp_w2k", [P, 2, 3 * NSA_HD])
        w2v = c.sb("cp_w2v", [P, 2, NSA_HD])
        pos = c.sb("cp_pos", [P, 2, CMP_LEN])
        blocks = c.sb("cp_blocks", [P, 2, CMP_LEN, NSA_GROUPS, NB])
        hidden = c.sb("cp_hidden", [P, 2, 2, NSA_GROUPS, NB])
        kcT = c.sb("cp_kcT", [P, NB])
        vc = c.sb("cp_vc", [NB, NSA_GROUPS * NSA_HD])
        cbias = c.sb("cp_cbias", [P, NSA_HEADS, TILES, NB])
        away = c.sb("cp_away", [P, TILES, NB])
        far = bias[:, NSA_HEADS - 1]
        s = c.sb("cp_s", [P, 2, NSA_HEADS, NB])
        top = c.sb("cp_top", [P, NSA_HEADS])
        total = c.sb("cp_total", [P, NSA_HEADS])
        pT = c.sb("cp_pT", [NB, NSA_HEADS, P])
        small_ps = c.ps("cp_small", [P, SEQ])
        turn_ps = [c.ps(f"cp_turn{i}", [P, SEQ]) for i in range(2)]
        o_ps = c.ps("cp_ops", [P, SEQ])
        pT_ps = [c.ps(f"cp_pTps{i}", [P, SEQ]) for i in range(2)]
        s_ps = turn_ps
        S = {x: c.sem(f"cp_{x}") for x in (
            "w", "w1v", "cleared", "const", "biases", "turned", "copied", "gates", "gated", "blocks", "hid", "gelu", "kc", "kcopied",
            "scored", "seq", "shifted", "exped", "weights", "pturned", "pcopied", "out", "stored")}
        n_small = 3
        with nc.Block() as block:
            @block.sync
            def _(sp):
                sp.dma_start(pos[:], d["cmp_pos"]).then_inc(S["w"], 16)
                sp.dma_start(w2k[:, :, NSA_HD:2 * NSA_HD], d["cmp_w2"][:, 0]).then_inc(S["w"], 16)
                sp.dma_start(w2v[:], d["cmp_w2"][:, 1]).then_inc(S["w"], 16)
                sp.dma_start(w1v[:], d["cmp_w1"][1]).then_inc(S["w1v"], 16)
                sp.wait_ge(S["w1v"], 16)

            @block.gpsimd
            def _(pool):
                pool.memset(blocks[:], 0.0).then_inc(S["cleared"], 1)
                pool.memset(ident[:], 0.0).then_inc(S["const"], 1)
                pool.memset(w2k[:, :, 0:NSA_HD], 0.0).then_inc(S["const"], 1)
                pool.memset(w2k[:, :, 2 * NSA_HD:], 0.0).then_inc(S["const"], 1)
                pool.wait_ge(S["const"], 3)
                pool.affine_select(out=ident[:], in_=ident[:], compare_op=ALU.not_equal, fill=1.0, base=0,
                                   pattern=[[-1, P]], channel_multiplier=1).then_inc(S["const"], 1)
                pool.iota(away[:], pattern=[[-P, TILES], [CMP_STRIDE, NB]], base=CMP_LEN - 1,
                          channel_multiplier=-1, allow_small_or_imprecise_dtypes=True).then_inc(S["const"], 1)
                pool.iota(far, pattern=[[1, 7 * P]], base=-3 * P, channel_multiplier=-1,
                          allow_small_or_imprecise_dtypes=True).then_inc(S["const"], 1)
                pool.wait_ge(S["const"], 6)
                for h in range(NSA_HEADS):
                    pool.tensor_scalar(cbias[:, h], away[:], slopes[h], None, ALU.mult).then_inc(S["const"], 1)
                pool.wait_ge(S["const"], 6 + NSA_HEADS)
                pool.affine_select(out=cbias[:], in_=cbias[:], compare_op=ALU.is_ge, fill=MASKED,
                                   base=1 - CMP_LEN, pattern=[[0, NSA_HEADS], [P, TILES], [-CMP_STRIDE, NB]],
                                   channel_multiplier=1).then_inc(S["biases"], 1)
                pool.wait_ge(S["gates"], TILES)
                first = gates[:, 0, 0:3 * NSA_HEADS:3]
                pool.affine_select(out=first, in_=first, compare_op=ALU.is_ge, fill=0.0, base=1 - CMP_LEN,
                                   pattern=[[0, NSA_HEADS]], channel_multiplier=1).then_inc(S["gated"], 1)
                for h in range(NSA_HEADS):
                    if h == NSA_HEADS - 1:
                        pool.wait_ge(S["const"], 6 + 2 * NSA_HEADS - 1)
                    pool.tensor_scalar(bias[:, h], far, slopes[h], None, ALU.mult).then_inc(S["const"], 1)
                pool.wait_ge(S["const"], 6 + 2 * NSA_HEADS)
                pool.affine_select(out=bias[:], in_=bias[:], compare_op=ALU.is_ge, fill=MASKED, base=3 * P,
                                   pattern=[[0, NSA_HEADS], [-1, 7 * P]], channel_multiplier=1
                                   ).then_inc(S["biases"], 1)

            @block.tensor
            def _(pe):
                pe.wait_ge(S["const"], 4)
                n = 0
                for t in range(TILES):
                    if n >= 2:
                        pe.wait_ge(S["copied"], n - 1)
                    for i, tile in enumerate((VSEL, VWIN, GL)):
                        last = pe.transpose(turn_ps[n % 2][:, i * P:(i + 1) * P], proj[:, tile, t * P:(t + 1) * P],
                                            ident[:])
                    last.then_inc(S["turned"], 1)
                    n += 1
                pe.wait_ge(S["w"], 16 * n_small)
                pe.wait_ge(w1_landed, 16)
                pe.wait_ge(S["blocks"], 8)
                for kv, w1 in enumerate((w1k, w1v)):
                    if kv:
                        pe.wait_ge(S["w1v"], 16)
                    for i in range(2):
                        at, width = (kv * 2 + i) * NSA_GROUPS * NB, NSA_GROUPS * NB
                        for l in range(CMP_LEN):
                            last = pe.matmul(pT_ps[0][:, at:at + width], w1[:, l, i * P:(i + 1) * P],
                                             blocks[:, kv, l].rearrange("p g n -> p (g n)"), start=l == 0,
                                             stop=l == CMP_LEN - 1)
                last.then_inc(S["hid"], 1)
                pe.wait_ge(S["gelu"], 1)
                for g in range(NSA_GROUPS):
                    for i in range(2):
                        at = NSA_HD * (1 - g)
                        last = pe.matmul(small_ps[:, 0:NB], w2k[:, i, at:at + P], hidden[:, 0, i, g, :],
                                         start=g == 0 and i == 0, stop=g == 1 and i == 1)
                for g in range(NSA_GROUPS):
                    for i in range(2):
                        last = pe.matmul(small_ps[0:NB, P + g * NSA_HD:P + (g + 1) * NSA_HD], hidden[:, 1, i, g, :],
                                         w2v[:, i, :], start=i == 0, stop=i == 1)
                last.then_inc(S["kc"], 1)
                pe.wait_ge(S["kcopied"], 2)
                pe.wait_ge(S["copied"], TILES)
                for t in range(TILES):
                    if t >= 1:
                        pe.wait_ge(S["shifted"], t)
                    for h in range(NSA_HEADS):
                        part = slice(h // 4 * NSA_HD, (h // 4 + 1) * NSA_HD)
                        last = pe.matmul(s_ps[h // 4][:, h % 4 * NB:(h % 4 + 1) * NB], proj[part, NQ0 + h % 4, t * P:(t + 1) * P],
                                         kcT[part, :], start=True, stop=True)
                    last.then_inc(S["scored"], 1)
                    pe.wait_ge(S["weights"], t + 1)
                    if t >= 1:
                        pe.wait_ge(S["pcopied"], 2 * t)
                    for h in range(NSA_HEADS):
                        last = pe.transpose(pT_ps[h // 4][0:NB, (h % 4) * P:(h % 4 + 1) * P], s[:, t % 2, h, :],
                                            ident[:])
                    last.then_inc(S["pturned"], 1)
                    pe.wait_ge(S["pcopied"], 2 * t + 2)
                    if t >= 1:
                        pe.wait_ge(S["stored"], t)
                    for h in range(NSA_HEADS):
                        g = h // 4
                        last = pe.matmul(o_ps[:, h * NSA_HD:(h + 1) * NSA_HD], pT[:, h, :],
                                         vc[:, g * NSA_HD:(g + 1) * NSA_HD], start=True, stop=True)
                    last.then_inc(S["out"], 1)

            @block.scalar
            def _(act):
                for t in range(TILES):
                    act.wait_ge(S["turned"], t + 1)
                    act.activation(gates[:, t, :], turn_ps[t % 2][:, 2 * P:2 * P + 3 * NSA_HEADS], ACT.Sigmoid
                                   ).then_inc(S["gates"], 1)
                act.wait_ge(S["hid"], 1)
                act.activation(hidden[:].rearrange("p a b g n -> p (a b g n)"), pT_ps[0][:, :4 * NSA_GROUPS * NB],
                               ACT.Gelu_apprx_tanh).then_inc(S["gelu"], 1)
                for t in range(TILES):
                    act.wait_ge(S["shifted"], t + 1)
                    act.activation(s[:, t % 2], s[:, t % 2], ACT.Exp, scale=scale).then_inc(S["exped"], 1)
                    act.wait_ge(S["pturned"], t + 1)
                    for i in range(2):
                        act.copy(pT[:, 4 * i:4 * i + 4, :].rearrange("p h q -> p (h q)"), pT_ps[i][0:NB, :]
                                 ).then_inc(S["pcopied"], 1)

            @block.vector
            def _(dve):
                done = [0]

                def then(instruction):
                    done[0] += 1
                    instruction.then_inc(S["seq"], 1)
                    dve.wait_ge(S["seq"], done[0])

                dve.wait_ge(S["w"], 16 * n_small)
                dve.wait_ge(S["cleared"], 1)
                for kv, tile in enumerate((KCMP, VCMP)):
                    for a in range(2):
                        tokens = proj[:, tile, CMP_STRIDE * a:CMP_STRIDE * (a + NB)]
                        place = pos[:, kv, CMP_STRIDE * a:CMP_STRIDE * (a + 1)]
                        for g in range(NSA_GROUPS):
                            part = slice(g * NSA_HD, (g + 1) * NSA_HD)
                            dve.tensor_tensor(blocks[part, kv, CMP_STRIDE * a:CMP_STRIDE * (a + 1), g, :],
                                              tokens[part].rearrange("p (c r) -> p r c", r=CMP_STRIDE),
                                              place[part].unsqueeze(2).broadcast_to([NSA_HD, CMP_STRIDE, NB]),
                                              ALU.add).then_inc(S["blocks"], 1)
                for t in range(TILES):
                    dve.wait_ge(S["gates"], t + 1)
                    then(dve.tensor_copy(vsel[:, t, :], turn_ps[t % 2][:, 0:P]))
                    dve.tensor_copy(vwin[:, t, :], turn_ps[t % 2][:, P:2 * P]).then_inc(S["copied"], 1)
                dve.wait_ge(S["kc"], 1)
                dve.tensor_copy(kcT[:], small_ps[:, 0:NB]).then_inc(S["kcopied"], 1)
                dve.tensor_copy(vc[:], small_ps[0:NB, P:2 * P]).then_inc(S["kcopied"], 1)
                dve.wait_ge(S["biases"], 1)
                dve.wait_ge(S["gated"], 1)
                wide = [P, NSA_HEADS, NB]
                for t in range(TILES):
                    now = s[:, t % 2]
                    dve.wait_ge(S["scored"], t + 1)
                    for g in range(NSA_GROUPS):
                        heads = slice(4 * g, 4 * g + 4)
                        then(dve.tensor_tensor(now[:, heads], s_ps[g][:, :4 * NB].rearrange("p (h n) -> p h n", n=NB),
                                               cbias[:, heads, t, :], ALU.add))
                    then(dve.tensor_reduce(top[:], now, AX.X, ALU.max))
                    dve.tensor_tensor(now, now, top[:].unsqueeze(2).broadcast_to(wide), ALU.subtract
                                      ).then_inc(S["shifted"], 1)
                    dve.wait_ge(S["exped"], t + 1)
                    then(dve.tensor_reduce(total[:], now, AX.X, ALU.add))
                    then(dve.reciprocal(total[:], total[:]))
                    then(dve.tensor_tensor(total[:], gates[:, t, 0:3 * NSA_HEADS:3], total[:], ALU.mult))
                    dve.tensor_tensor(now, now, total[:].unsqueeze(2).broadcast_to(wide), ALU.mult
                                      ).then_inc(S["weights"], 1)
                    dve.wait_ge(S["out"], t + 1)
                    dve.tensor_copy(o_tok[:, t, :], o_ps[:]).then_inc(S["stored"], 1)
    clear_semaphores(nc, S.values())


def second_mixer(nc, hT, x_hi, x_lo, d):
    with ExitStack() as ctx:
        c = Chip(nc, ctx)
        o_tok = c.sb("n_otok", [P, TILES, NSA_HEADS * NSA_HD])
        ident = c.sb("n_ident", [P, P])
        with ExitStack() as inner:
            c = Chip(nc, inner)
            proj = c.sb("n_proj", [P, N_PROJ2, SEQ])
            vsel, vwin = (c.sb(x, [P, TILES, P]) for x in ("n_vsel", "n_vwin"))
            gates = c.sb("n_gates", [P, TILES, 3 * NSA_HEADS])
            bias = c.sb("n_bias", [P, NSA_HEADS, 7 * P])
            w1_landed = c.sem("n_w1_landed")
            with ExitStack() as compressing:
                w1k = Chip(nc, compressing).sb("n_w1k", [P, CMP_LEN, CMP_HID])

                def load_w1k(sp):
                    sp.dma_start(w1k[:], d["cmp_w1"][0]).then_inc(w1_landed, 16)
                norm_and_project(nc, "p2", hT, x_hi, x_lo, d["mix_norm"], d["w_nsa"], proj, load_w1k)
                compress_and_attend(nc, proj, ident, w1k, w1_landed, vsel, vwin, gates, bias, o_tok, d)

            def unit(t, h, branch):
                part = slice(h // 4 * NSA_HD, (h // 4 + 1) * NSA_HD)
                w, at = (t + 1) * P, (TILES - 1 - t) * P
                keys, values = ((KSEL, vsel), (KWIN, vwin))[branch - 1]
                return dict(q=proj[part, NQ0 + h % 4, t * P:(t + 1) * P], k=proj[part, keys, :w], width=w,
                            bias=bias[:, h, at:at + w], v=lambda b: values[:, b, part], dv=NSA_HD, add=True,
                            gate=gates[:, t, 3 * h + branch:3 * h + branch + 1],
                            out=o_tok[:, t, h * NSA_HD:(h + 1) * NSA_HD])
            with ExitStack() as attending:
                c = Chip(nc, attending)
                stream = PanelStream(c, "p3", d["w_hg"], x_hi, x_lo, d["hg_proj"], ACT.Copy)
                att = Attention(c, "att2", [unit(t, h, branch) for t in range(TILES) for branch in (1, 2)
                                            for h in range(NSA_HEADS)], float(NSA_HD) ** -0.5, ident, stream)
                with nc.Block() as block:
                    block.sync(stream.sync)
                    block.gpsimd(stream_low(stream))
                    block.scalar(att.scalar)
                    block.vector(att.vector)
                    block.tensor(att.tensor)
                clear_semaphores(nc, [*att.sems, *stream.sems, w1_landed])
        hgrn(nc, x_hi, x_lo, o_tok, ident, d)
    project_onto(nc, "wo2", x_hi, x_lo, d["w_out"], hT)


HQ, HF, HI, HG = 0, 4, 8, 12
N_PROJ3 = 16


def hgrn_operands(nc, projections, proj, ident, write, fold, ends, v_tok, w_tok, lower_bound):
    with ExitStack() as ctx:
        c = Chip(nc, ctx)
        lb = c.sb("hf_lb", [P, HG_HEADS])
        lb_e = c.sb("hf_lbe", [P, HG_HEADS])
        free = c.sb("hf_free", [P, HG_HEADS])
        sig = c.sb("hf_sig", [P, HG_HEADS, SEQ])
        tiny = c.sb("hf_tiny", [P, HG_HEADS, SEQ])
        inside = c.sb("hf_inside", [P, HG_HEADS * SEQ])
        part = c.sb("hf_part", [P, 1], I32)
        odd = c.sb("hf_odd", [P, 1], I32)
        parity = c.sb("hf_parity", [P, 2])
        banks = [c.ps(f"hf_bank{i}", [P, SEQ]) for i in range(4)]
        S = {x: c.sem(f"hf_{x}") for x in ("lb", "lb_shift", "lb_exp", "const", "sigmoids", "f", "seq", "logs",
                                           "b", "eb", "rest", "erest", "w", "turned", "taken")}
        landed = {x: c.sem(f"hf_landed{x}") for x in (HQ, HF, HI, HG)}
        q, z, inp, gate = (proj[:, x:x + 4, :] for x in (HQ, HF, HI, HG))

        def flat(x):
            return x.rearrange("p h s -> p (h s)")

        def chunked(x):
            return flat(x).rearrange("p (c i) -> p c i", i=CHUNK)
        PART = 2.0 ** -50
        with nc.Block() as block:
            @block.sync
            def _(sp):
                for x in (HF, HI, HQ, HG):
                    sp.dma_start(proj[:, x:x + 4, :], projections[x:x + 4].rearrange("n p s -> p n s")
                                 ).then_inc(landed[x], 16)
                sp.dma_start(lb[:], lower_bound).then_inc(S["lb"], 16)

            @block.gpsimd
            def _(pool):
                pool.memset(inside[:], 1.0).then_inc(S["const"], 1)
                pool.iota(part[:], pattern=[[0, 1]], base=0, channel_multiplier=1).then_inc(S["const"], 1)
                pool.wait_ge(S["const"], 2)
                pool.memset(inside[:].rearrange("p (c i) -> p c i", i=CHUNK)[:, :, 0:1], 0.0
                            ).then_inc(S["const"], 1)

            @block.scalar
            def _(act):
                act.wait_ge(landed[HF], 16)
                act.activation(flat(sig[:]), flat(z), ACT.Sigmoid).then_inc(S["sigmoids"], 1)
                act.activation(flat(write[:]), flat(z), ACT.Sigmoid, scale=-1.0).then_inc(S["sigmoids"], 1)
                act.wait_ge(landed[HQ], 16)
                act.activation(flat(q), flat(q), ACT.Silu).then_inc(S["sigmoids"], 1)
                act.wait_ge(landed[HG], 16)
                act.activation(flat(gate), flat(gate), ACT.Silu).then_inc(S["sigmoids"], 1)
                act.wait_ge(S["lb_shift"], 1)
                act.activation(lb_e[:], lb_e[:], ACT.Exp).then_inc(S["lb_exp"], 1)
                act.wait_ge(S["f"], 2)
                act.activation(flat(z), flat(z), ACT.Ln).then_inc(S["logs"], 1)
                act.activation(flat(tiny[:]), flat(tiny[:]), ACT.Ln, scale=1.0 / PART).then_inc(S["logs"], 1)
                act.wait_ge(S["b"], 1)
                act.activation(flat(tiny[:]), flat(z), ACT.Exp).then_inc(S["eb"], 1)
                act.wait_ge(S["rest"], 1)
                act.activation(flat(sig[:]), flat(sig[:]), ACT.Exp).then_inc(S["erest"], 1)

            @block.vector
            def _(dve):
                done = [0]

                def then(instruction):
                    done[0] += 1
                    instruction.then_inc(S["seq"], 1)
                    dve.wait_ge(S["seq"], done[0])

                dve.wait_ge(S["const"], 3)
                then(dve.tensor_scalar(odd[:], part[:], CHUNK.bit_length() - 1, 1, ALU.logical_shift_right,
                                       ALU.bitwise_and))
                then(dve.tensor_copy(parity[:, 1:2], odd[:]))
                then(dve.tensor_scalar(parity[:, 0:1], parity[:, 1:2], -1.0, 1.0, ALU.mult, ALU.add))
                dve.wait_ge(S["lb"], 16)
                dve.tensor_tensor(lb_e[:], lb[:], lb[:], ALU.subtract).then_inc(S["lb_shift"], 1)
                dve.wait_ge(S["lb_exp"], 1)
                then(dve.reciprocal(lb[:], lb_e[:]))
                then(dve.tensor_tensor(lb_e[:], lb_e[:], lb[:], ALU.mult))
                then(dve.tensor_tensor(lb[:], lb_e[:], lb_e[:], ALU.subtract))
                then(dve.tensor_scalar(free[:], lb[:], -1.0, 1.0, ALU.mult, ALU.add))
                dve.wait_ge(S["sigmoids"], 2)
                for h in range(HG_HEADS):
                    then(dve.tensor_scalar(sig[:, h, :], sig[:, h, :], free[:, h:h + 1], lb[:, h:h + 1], ALU.mult,
                                           ALU.add))
                    then(dve.tensor_scalar(write[:, h, :], write[:, h, :], free[:, h:h + 1], None, ALU.mult))
                dve.tensor_scalar(flat(tiny[:]), flat(sig[:]), F_FLOOR, PART, ALU.max, ALU.min
                                  ).then_inc(S["f"], 1)
                dve.tensor_scalar(flat(z), flat(sig[:]), PART, None, ALU.max).then_inc(S["f"], 1)
                for t in range(TILES):
                    dve.wait_ge(S["turned"], t + 1)
                    dve.tensor_copy(v_tok[:, t, :], banks[t][:]).then_inc(S["taken"], 1)
                dve.wait_ge(S["logs"], 2)
                then(dve.tensor_tensor(flat(sig[:]), flat(z), flat(tiny[:]), ALU.add))
                dve.tensor_tensor_scan(flat(z), inside[:], flat(sig[:]), 0.0, ALU.mult, ALU.add
                                       ).then_inc(S["b"], 1)
                dve.wait_ge(S["b"], 1)
                last = chunked(z)[:, :, CHUNK - 1:CHUNK].broadcast_to([P, HG_HEADS * N_CHUNKS, CHUNK])
                dve.tensor_tensor(chunked(sig[:]), last, chunked(z), ALU.subtract).then_inc(S["rest"], 1)
                dve.wait_ge(S["eb"], 1)
                dve.wait_ge(S["sigmoids"], 4)
                then(dve.tensor_tensor(flat(fold[:]), flat(q), flat(tiny[:]), ALU.mult))
                then(dve.tensor_copy(ends[:], chunked(tiny[:])[:, :, CHUNK - 1]))
                dve.wait_ge(S["erest"], 1)
                dve.tensor_tensor(flat(sig[:]), flat(sig[:]), flat(write[:]), ALU.mult).then_inc(S["w"], 1)
                for t in range(TILES):
                    dve.wait_ge(S["turned"], TILES + t + 1)
                    for i in range(2):
                        last = dve.tensor_scalar(w_tok[:, i, t, :], banks[t][:], parity[:, i:i + 1], None, ALU.mult)
                        last.then_inc(S["taken"], 1)

            @block.tensor
            def _(pe):
                def turn(x):
                    for t in range(TILES):
                        for h in range(HG_HEADS):
                            last = pe.transpose(banks[t][:, h * P:(h + 1) * P], x[:, h, t * P:(t + 1) * P],
                                                ident[:])
                        last.then_inc(S["turned"], 1)
                pe.wait_ge(landed[HI], 16)
                turn(inp)
                pe.wait_ge(S["w"], 1)
                pe.wait_ge(S["taken"], TILES)
                turn(sig)
    clear_semaphores(nc, [*S.values(), *landed.values()])


def hgrn_within_chunks(nc, proj, write, ident, inner, scratch):
    with ExitStack() as ctx:
        c = Chip(nc, ctx)
        bc, qc, kc = (c.sb(f"hw_{x}", [P, CHUNK, P]) for x in ("b", "q", "k"))
        pair = c.sb("hw_pair", [P, 3, CHUNK, P])
        weights = c.sb("hw_weights", [P, CHUNK * CHUNK])
        zeros = c.sb("hw_zeros", [P, scratch.shape[0] * scratch.shape[1] // P])
        banks = [c.ps(f"hw_bank{i}", [P, SEQ]) for i in range(4)]
        S = {x: c.sem(f"hw_{x}") for x in ("turned", "chunked", "zeros", "cleared", "diff", "exp", "keyed",
                                           "product", "summed", "placed", "loaded")}
        sources = [proj[:, HF:HF + 4, :], write[:], proj[:, HQ:HQ + 4, :]]
        n_banks = CHUNK * P // SEQ
        with nc.Block() as block:
            @block.sync
            def _(sp):
                sp.wait_ge(S["zeros"], 2)
                sp.dma_start(scratch.rearrange("a x -> (a x)").rearrange("(p x) -> p x", p=P), zeros[:]
                             ).then_inc(S["cleared"], 16)
                sp.wait_ge(S["cleared"], 16)
                sp.wait_ge(S["summed"], CHUNK)
                for a in range(HG_HEADS * TILES):
                    to = scratch[a].rearrange("(c x) -> c x", c=P // CHUNK)[:, :CHUNK * PITCH]
                    sp.dma_start(to.rearrange("c (s y) -> c s y", y=PITCH)[:, :, :CHUNK],
                                 weights[a * (P // CHUNK):(a + 1) * (P // CHUNK), :].rearrange(
                                     "c (s t) -> c s t", t=CHUNK)).then_inc(S["placed"], 16)
                sp.wait_ge(S["placed"], 16 * HG_HEADS * TILES)
                sp.dma_start(inner[:], scratch[:, :P * PITCH].rearrange("a (s y) -> s a y", y=PITCH)[:, :, :P]
                             ).then_inc(S["loaded"], 16)
                sp.wait_ge(S["loaded"], 16)

            @block.tensor
            def _(pe):
                for n in range(3 * n_banks):
                    x = sources[n // n_banks].rearrange("p h s -> p (h s)").rearrange("p (c i) -> p c i", i=CHUNK)
                    if n >= 4:
                        pe.wait_ge(S["chunked"], n - 3)
                    for k in range(SEQ // P):
                        last = pe.transpose(banks[n % 4][:, k * P:(k + 1) * P], x[:, :, n % n_banks * 4 + k],
                                            ident[:])
                    last.then_inc(S["turned"], 1)

            @block.scalar
            def _(act):
                for n in range(3 * n_banks):
                    act.wait_ge(S["turned"], n + 1)
                    to = (bc, kc, qc)[n // n_banks][:, n % n_banks * 4:n % n_banks * 4 + 4, :]
                    act.copy(to.rearrange("p i d -> p (i d)"), banks[n % 4][:]).then_inc(S["chunked"], 1)
                for j in range(CHUNK):
                    act.wait_ge(S["diff"], j + 1)
                    x = pair[:, j % 3, :CHUNK - j, :]
                    act.activation(x, x, ACT.Exp).then_inc(S["exp"], 1)

            @block.gpsimd
            def _(pool):
                pool.memset(zeros[:], 0.0).then_inc(S["zeros"], 1)
                pool.memset(weights[:], 0.0).then_inc(S["zeros"], 1)
                pool.wait_ge(S["chunked"], 2 * n_banks)
                for j in range(CHUNK):
                    pool.wait_ge(S["exp"], j + 1)
                    x = pair[:, j % 3, :CHUNK - j, :]
                    pool.tensor_tensor(x, x, kc[:, :CHUNK - j, :], ALU.mult).then_inc(S["keyed"], 1)

            @block.vector
            def _(dve):
                dve.wait_ge(S["chunked"], n_banks)

                def diff(j):
                    if j >= 3:
                        dve.wait_ge(S["summed"], j - 2)
                    dve.tensor_tensor(pair[:, j % 3, :CHUNK - j, :], bc[:, j:, :], bc[:, :CHUNK - j, :],
                                      ALU.subtract).then_inc(S["diff"], 1)

                diff(0)
                diff(1)
                dve.wait_ge(S["chunked"], 3 * n_banks)
                dve.wait_ge(S["zeros"], 2)
                for j in range(CHUNK):
                    if j + 2 < CHUNK:
                        diff(j + 2)
                    x = pair[:, j % 3, :CHUNK - j, :]
                    dve.wait_ge(S["keyed"], j + 1)
                    dve.tensor_tensor(x, x, qc[:, j:, :], ALU.mult).then_inc(S["product"], 1)
                    dve.wait_ge(S["product"], j + 1)
                    dve.tensor_reduce(weights[:, j:j + (CHUNK + 1) * (CHUNK - j - 1) + 1:CHUNK + 1], x, AX.X,
                                      ALU.add).then_inc(S["summed"], 1)
    clear_semaphores(nc, S.values())


def hgrn_recurrence(nc, proj, fold, ends, v_tok, w_tok, inner, out_norm, y_hi, y_lo):
    with ExitStack() as ctx:
        c = Chip(nc, ctx)
        state = c.sb("hr_state", [P, 2, HG_HEADS, P])
        ones = c.sb("hr_ones", [P, P])
        gain = c.sb("hr_gain", [P, 1])
        sq = c.sb("hr_sq", [P, HG_HEADS, SEQ])
        ms = c.sb("hr_ms", [P, HG_HEADS, SEQ])
        o_ps = [c.ps(f"hr_o{h}", [P, SEQ]) for h in range(HG_HEADS)]
        kv_ps = [c.ps(f"hr_kv{i}", [P, HG_HEADS, P]) for i in range(2)]
        sum_ps = [c.ps(f"hr_sum{i}", [P, SEQ]) for i in range(2)]
        S = {x: c.sem(f"hr_{x}") for x in ("gain", "const", "written", "state", "read", "sq", "sum", "mean",
                                           "root", "rstd", "normed", "out", "high", "low")}
        with nc.Block() as block:
            @block.sync
            def _(sp):
                sp.dma_start(gain[:], out_norm).then_inc(S["gain"], 16)

            @block.gpsimd
            def _(pool):
                pool.memset(ones[:], 1.0).then_inc(S["const"], 1)

            @block.tensor
            def _(pe):
                for h in range(HG_HEADS):
                    for t in range(TILES):
                        pe.matmul(o_ps[h][:, t * P:(t + 1) * P], v_tok[:, t, h * P:(h + 1) * P],
                                  inner[:, h * TILES + t, :], start=t == 0, stop=False, skip_group_check=True)
                for n in range(N_CHUNKS):
                    if n < N_CHUNKS - 1:
                        tile, rows = n * CHUNK // P, slice(n // 2 % 4 * 32, n // 2 % 4 * 32 + 32)
                        if n >= 2:
                            pe.wait_ge(S["state"], n - 1)
                        for h in range(HG_HEADS):
                            cols = slice(h * P, (h + 1) * P)
                            last = pe.matmul(kv_ps[n % 2][:, h, :], w_tok[rows, n % 2, tile, cols],
                                             v_tok[rows, tile, cols], start=True, stop=True)
                        last.then_inc(S["written"], 1)
                    if n >= 1:
                        pe.wait_ge(S["state"], n)
                        at = slice(n * CHUNK, (n + 1) * CHUNK)
                        for h in range(HG_HEADS):
                            last = pe.matmul(o_ps[h][:, at], state[:, n % 2, h, :], fold[:, h, at], start=False,
                                             stop=n == N_CHUNKS - 1, skip_group_check=True)
                        last.then_inc(S["read"], 1)
                pe.wait_ge(S["const"], 1)
                for h in range(HG_HEADS):
                    pe.wait_ge(S["sq"], h + 1)
                    if h >= 2:
                        pe.wait_ge(S["mean"], h - 1)
                    pe.matmul(sum_ps[h % 2][:], ones[:], sq[:, h, :], start=True, stop=True).then_inc(S["sum"], 1)

            @block.scalar
            def _(act):
                act.wait_ge(S["read"], N_CHUNKS - 1)
                for h in range(HG_HEADS):
                    act.activation(sq[:, h, :], o_ps[h][:], ACT.Square).then_inc(S["sq"], 1)
                for h in range(HG_HEADS):
                    act.wait_ge(S["mean"], h + 1)
                    act.activation(ms[:, h, :], ms[:, h, :], ACT.Sqrt).then_inc(S["root"], 1)
                for h in range(HG_HEADS):
                    act.wait_ge(S["out"], h + 1)
                    act.copy(y_hi[:, h, :], ms[:, h, :]).then_inc(S["high"], 1)

            @block.vector
            def _(dve):
                for n in range(N_CHUNKS - 1):
                    dve.wait_ge(S["written"], n + 1)
                    if n == 0:
                        dve.tensor_copy(state[:, 1], kv_ps[0][:]).then_inc(S["state"], 1)
                        continue
                    dve.wait_ge(S["state"], n)
                    if n >= 2:
                        dve.wait_ge(S["read"], n - 1)
                    for h in range(HG_HEADS):
                        end = ends[:, h * N_CHUNKS + n:h * N_CHUNKS + n + 1]
                        last = dve.scalar_tensor_tensor(state[:, (n + 1) % 2, h, :], state[:, n % 2, h, :], end,
                                                        kv_ps[n % 2][:, h, :], ALU.mult, ALU.add)
                    last.then_inc(S["state"], 1)
                for h in range(HG_HEADS):
                    dve.wait_ge(S["sum"], h + 1)
                    dve.tensor_scalar(ms[:, h, :], sum_ps[h % 2][:], 1.0 / P, EPS, ALU.mult, ALU.add
                                      ).then_inc(S["mean"], 1)
                dve.wait_ge(S["gain"], 16)
                for h in range(HG_HEADS):
                    dve.wait_ge(S["root"], h + 1)
                    dve.reciprocal(sq[:, h, :], ms[:, h, :]).then_inc(S["rstd"], 1)
                    dve.wait_ge(S["rstd"], h + 1)
                    dve.scalar_tensor_tensor(sq[:, h, :], o_ps[h][:], gain[:, 0:1], sq[:, h, :], ALU.mult,
                                             ALU.mult).then_inc(S["normed"], 1)
                    dve.wait_ge(S["normed"], h + 1)
                    dve.tensor_tensor(ms[:, h, :], sq[:, h, :], proj[:, HG + h, :], ALU.mult
                                      ).then_inc(S["out"], 1)
                    dve.wait_ge(S["high"], h + 1)
                    dve.tensor_tensor(y_lo[:, h, :], ms[:, h, :], y_hi[:, h, :].bitcast(F32), ALU.subtract
                                      ).then_inc(S["low"], 1)
    clear_semaphores(nc, S.values())


def hgrn(nc, x_hi, x_lo, o_tok, ident, d):
    with ExitStack() as ctx:
        c = Chip(nc, ctx)
        proj = c.sb("h_proj", [P, N_PROJ3, SEQ])
        turn_to_features(nc, "on_turn", o_tok, 4, x_hi, x_lo, ident)
        fold = c.sb("h_fold", [P, HG_HEADS, SEQ])
        ends = c.sb("h_ends", [P, HG_HEADS * N_CHUNKS])
        v_tok = c.sb("h_vtok", [P, TILES, HG_HEADS * P])
        w_tok = c.sb("h_wtok", [P, 2, TILES, HG_HEADS * P])
        inner = c.sb("h_inner", [P, HG_HEADS * TILES, P])
        with ExitStack() as within:
            write = Chip(nc, within).sb("h_write", [P, HG_HEADS, SEQ])
            hgrn_operands(nc, d["hg_proj"], proj, ident, write, fold, ends, v_tok, w_tok, d["lower_bound"])
            hgrn_within_chunks(nc, proj, write, ident, inner, d["hg_scratch"])
        hgrn_recurrence(nc, proj, fold, ends, v_tok, w_tok, inner, d["out_norm"], x_hi[:, 4:8, :], x_lo[:, 4:8, :])


def final_norm(nc, hT, gain, out):
    with ExitStack() as ctx:
        c = Chip(nc, ctx)
        result = c.sb("fn_result", [P, KC, SEQ])
        norm = NormStage(c, "fn", hT, gain, c.ps("fn_sum", [P, SEQ]), c.sb("fn_sq", [P, 2, SEQ]), None,
                         c.sb("fn_stat", [P, 2, SEQ]))
        scaled, stored = c.sem("fn_scaled"), c.sem("fn_stored")
        with nc.Block() as block:
            @block.sync
            def _(sp):
                norm.sync(sp)
                for k in range(KC):
                    sp.wait_ge(scaled, k + 1)
                    sp.dma_start(out[:, k, :], result[:, k, :]).then_inc(stored, 16)
                sp.wait_ge(stored, 16 * KC)

            @block.gpsimd
            def _(pool):
                norm.gpsimd(pool)

            @block.scalar
            def _(act):
                norm.scalar_root(act)

            @block.vector
            def _(dve):
                norm.vector_inverse(dve)
                for k in range(KC):
                    dve.scalar_tensor_tensor(result[:, k, :], hT[:, k, :], norm.gain[:, k:k + 1],
                                             norm.stat[:, 0, :], ALU.mult, ALU.mult).then_inc(scaled, 1)

            @block.tensor
            def _(pe):
                norm.tensor(pe)
    clear_semaphores(nc, [*norm.sems, scaled, stored])


def build_program(nc, a, out):
    with ExitStack() as ctx:
        c = Chip(nc, ctx)
        hT = c.sb("hT", [P, KC, SEQ])
        x_hi, x_lo = (c.sb(x, [P, KC, SEQ], F32R) for x in ("x_hi", "x_lo"))
        routing = nc.dram_tensor("routing", [N_KEYS, N_KEYS, SEQ], F32).ap()
        a["hg_scratch"] = nc.dram_tensor("hg_scratch", [HG_HEADS * TILES, P // CHUNK * (CHUNK * PITCH + CHUNK)],
                                         F32).ap()
        hidden = nc.dram_tensor("hidden", [sum(EARLY_CHUNKS), P, SEQ], F32).ap()
        a["hg_proj"] = nc.dram_tensor("hg_proj", [N_PROJ3, P, SEQ], F32).ap()
        a["gates"] = nc.dram_tensor("gates", [2 * KC, P, SEQ], F32).ap()
        loaded = c.sem("h_loaded")
        with nc.Block() as block:
            @block.sync
            def _(sp):
                sp.dma_start(hT[:], a["x"]).then_inc(loaded, 16)
                sp.wait_ge(loaded, 16)
        first_mixer(nc, hT, x_hi, x_lo, a)
        experts(nc, hT, x_hi, x_lo, a, routing, hidden)

        def down(w):
            return lambda n: w[bass.ds(n, 1)].rearrange("o p f -> p (o f)")
        hidden_stage(nc, "ffn1", hT, x_hi, x_lo, a["gu1"], down(a["down1"]), norm_g=a["ffn1_norm"])
        second_mixer(nc, hT, x_hi, x_lo, a)
        hidden_stage(nc, "ffn2", hT, x_hi, x_lo, a["gu2"], down(a["down2"]), norm_g=a["ffn2_norm"])
        final_norm(nc, hT, a["final_norm"], out)



def panels(w):
    import numpy as np
    k, n = w.shape
    return np.ascontiguousarray(w.reshape(k // P, P, n // P, P).transpose(2, 1, 0, 3)).reshape(n // P, P, k)


def columns(g):
    import numpy as np
    return np.ascontiguousarray(g.reshape(-1, P).T)


def rotary_constants():
    import numpy as np
    inv, rot = np.zeros((P, 2), np.float32), np.zeros((P, 2, P), np.float32)
    for kind, half, heads in ((0, 16, (0,)), (1, 8, (0, 64))):
        freq = np.power(np.float32(500000.0), -np.arange(half, dtype=np.float32) * np.float32(2.0 / (2 * half)))
        for at in heads:
            for i in range(half):
                inv[at + i, kind] = inv[at + half + i, kind] = freq[i]
                rot[at + half + i, kind, at + i] = -1.0
                rot[at + i, kind, at + half + i] = 1.0
    return inv, rot


def laid_out(inputs):
    import numpy as np
    I = {k: np.asarray(v) for k, v in inputs.items()}
    cat, stack, whole = np.concatenate, np.stack, np.ascontiguousarray
    w_in = I["w_in"][0]
    at = [512, 1024, 1536, 1792, 2048, 2112, 2116]
    k_idx = w_in[:, at[4]:at[5]]
    w_in1 = cat([w_in[:, :at[4]], k_idx, k_idx, w_in[:, at[5]:at[5] + P]], 1)
    gates = w_in[:, at[6]:]
    w_gates = stack([panels(gates[:, :D]), panels(gates[:, D:])], 1).reshape(2 * KC, P, PANEL)
    w_merge = cat([panels(I["w_a_out"][0]), panels(I["w_b_out"][0])], 2)
    inv, rot = rotary_constants()
    w2 = I["w_in_2"][0]
    q_end, gl = NSA_HEADS * NSA_HD, NSA_HEADS * NSA_HD + 6 * P
    q2 = w2[:, :q_end].reshape(D, 2, 4, NSA_HD).transpose(0, 2, 1, 3).reshape(D, q_end)
    w_nsa = cat([q2, w2[:, q_end:gl], w2[:, gl:gl + P]], 1)

    def twice(x):
        return cat([x, x], 0)

    def gate_up(w):
        w = np.pad(w.reshape(KC, P, 2, -1), ((0, 0), (0, 0), (0, 0), (0, -w.shape[1] // 2 % P)))
        w = w.reshape(KC, P, 2, -1, P)
        return whole(w.transpose(3, 2, 1, 0, 4)).reshape(-1, P, PANEL)

    def down(w):
        return np.pad(w, ((0, -w.shape[0] % P), (0, 0))).reshape(-1, P, D)

    return dict(
        x=whole(I["x"][0].reshape(SEQ, KC, P).transpose(2, 1, 0)), positions=I["positions"],
        norm1_g=columns(I["norm1_g"][0]), w_in1=panels(w_in1), w_gates=w_gates, w_merge=w_merge, w_o=panels(I["w_o"][0]),
        inv=inv, rot=rot,
        gains=columns(cat([I["kv_norm_g"][0], I["q_norm_g"][0], I["k_norm_g"][0]])),
        wuk=whole(I["w_uk"][0].reshape(2, P, P).transpose(1, 0, 2)),
        wuv=whole(I["w_uv"][0].reshape(2, P, P).transpose(1, 0, 2)),
        wsT=whole(I["spatial_w"][0].transpose(2, 0, 1)), bs=I["spatial_b"].reshape(1, A_GROUPS, P),
        vg=I["v_norm_g"][0], vb=I["v_norm_b"][0],
        norm2_g=columns(I["norm2_g"][0]), peer_wq=panels(I["peer_wq"][0]),
        subkeys=whole(I["peer_subkeys"][0].reshape(HALVES, N_KEYS, P).transpose(2, 0, 1)),
        peer_u=whole(I["peer_u"][0].reshape(N_KEYS, N_KEYS, KC, P).transpose(1, 3, 2, 0)).reshape(N_KEYS, P, PANEL),
        peer_v=I["peer_v"][0],
        ffn1_norm=columns(I["ffn1_norm_2"][0]), gu1=gate_up(I["ffn1_w_gu_2"][0]), down1=down(I["ffn1_w_down_2"][0]),
        mix_norm=columns(I["mix_norm_2"][0]), w_nsa=panels(w_nsa), w_hg=panels(w2[:, gl + 3 * NSA_HEADS:]),
        w_out=panels(I["w_out_2"][0]),
        cmp_pos=stack([twice(I["cmp_pos_k_2"][0].T), twice(I["cmp_pos_v_2"][0].T)], 1),
        cmp_w1=stack([twice(I[x][0].reshape(CMP_LEN, NSA_HD, CMP_HID).transpose(1, 0, 2))
                      for x in ("cmp_k_w1_2", "cmp_v_w1_2")]),
        cmp_w2=stack([I[x][0].reshape(2, P, NSA_HD).transpose(1, 0, 2) for x in ("cmp_k_w2_2", "cmp_v_w2_2")], 1),
        lower_bound=columns(I["hgrn_lower_bound_2"][0]), out_norm=columns(I["hgrn_out_norm_2"][0]),
        ffn2_norm=columns(I["ffn2_norm_2"][0]), gu2=gate_up(I["ffn2_w_gu_2"][0]), down2=down(I["ffn2_w_down_2"][0]),
        final_norm=columns(I["final_norm_2"]))


def kernel(**inputs):
    import numpy as np
    import concourse.bacc as bacc
    from concourse.bass_utils import run_bass_kernel_spmd

    nc = bacc.Bacc("TRN2", target_bir_lowering=False, num_devices=1)
    arrays, args = {}, {}
    for name, value in laid_out(inputs).items():
        value = np.ascontiguousarray(value)
        arrays[f"in_{name}"] = value
        args[name] = nc.dram_tensor(f"in_{name}", value.shape, mybir.dt.from_np(value.dtype),
                                    kind="ExternalInput").ap()
    out = nc.dram_tensor("out", (P, KC, SEQ), F32, kind="ExternalOutput").ap()
    build_program(nc, args, out)
    result = run_bass_kernel_spmd(nc, [arrays], core_ids=[0]).results[0]["out"]
    return np.ascontiguousarray(result.transpose(2, 1, 0)).reshape(1, SEQ, D)
```

```python
from contextlib import ExitStack

import concourse.bass as bass
from concourse import mybir
from concourse.alu_op_type import AluOpType as ALU

ACT = mybir.ActivationFunctionType
AX = mybir.AxisListType
F32 = mybir.dt.float32
F32R = mybir.dt.float32r
I32 = mybir.dt.int32
U32 = mybir.dt.uint32

P = 128
SEQ = 512
D = 1024
KC = D // P
EPS = 1e-6
PANEL = KC * P
RING = 4
TOKENS = 64


class Chip:

    def __init__(self, nc, ctx):
        self.nc, self.ctx = nc, ctx

    def sb(self, name, shape, dt=F32):
        return self.ctx.enter_context(self.nc.sbuf_tensor(name, shape, dt))

    def ps(self, name, shape, dt=F32):
        return self.ctx.enter_context(self.nc.psum_tensor(name, shape, dt))

    def sem(self, name):
        return self.ctx.enter_context(self.nc.semaphore(name))


def clear_semaphores(nc, sems):
    with nc.Block() as block:
        @block.sync
        def _(sp):
            for s in sems:
                sp.sem_clear(s)


def three_products(pe, out, w_high, w_low, x_high, x_low, first, last):
    pe.matmul(out, w_high, x_high, start=first, stop=False)
    pe.matmul(out, w_high, x_low, start=False, stop=False)
    return pe.matmul(out, w_low, x_high, start=False, stop=last)


class NormStage:

    def __init__(self, c, name, hT, gain_dram, sum_ps, sq, xn, stat):
        self.hT, self.gain_dram, self.sum_ps, self.sq, self.xn = hT, gain_dram, sum_ps, sq, xn
        self.gain = c.sb(f"{name}_gain", [P, KC])
        self.ones = c.sb(f"{name}_ones", [P, P])
        self.stat = stat
        (self.gain_landed, self.ones_ready, self.sq_ready, self.sq_added, self.sum_ready, self.mean_ready,
         self.root_ready, self.rstd_ready, self.xn_ready, self.x_high, self.x_split) = self.sems = [
            c.sem(f"{name}_{x}") for x in ("gain_landed", "ones_ready", "sq_ready", "sq_added", "sum_ready",
                                           "mean_ready", "root_ready", "rstd_ready", "xn_ready", "x_high", "x_split")]

    def sync(self, sp):
        sp.dma_start(self.gain[:], self.gain_dram).then_inc(self.gain_landed, 16)

    def vector_scale(self, dve, x_hi, x_lo):
        dve.wait_ge(self.gain_landed, 16)
        self.vector_split(dve, x_hi, x_lo, scaled=False)

    def gpsimd(self, pool):
        pool.memset(self.ones[:], 1.0).then_inc(self.ones_ready, 1)

    def scalar_squares(self, act):
        for k in range(KC):
            if k >= 2:
                act.wait_ge(self.sq_added, max(1, k - 2))
            act.activation(self.sq[:, k % 2, :], self.hT[:, k, :], ACT.Square).then_inc(self.sq_ready, 1)

    def scalar_root(self, act):
        act.wait_ge(self.mean_ready, 1)
        act.activation(self.stat[:, 1, :], self.stat[:, 0, :], ACT.Sqrt).then_inc(self.root_ready, 1)

    def scalar_high(self, act, x_hi):
        for k in range(KC):
            act.wait_ge(self.xn_ready, k + 1)
            act.copy(x_hi[:, k, :], self.xn[:, k % 2, :]).then_inc(self.x_high, 1)

    def vector_add(self, dve):
        for k in range(1, KC):
            dve.wait_ge(self.sq_ready, k + 1)
            if k >= 2:
                dve.wait_ge(self.sq_added, k - 1)
            dve.tensor_tensor(self.stat[:, 1, :], self.sq[:, 0, :] if k == 1 else self.stat[:, 1, :],
                              self.sq[:, k % 2, :], ALU.add).then_inc(self.sq_added, 1)

    def vector_inverse(self, dve):
        dve.wait_ge(self.sum_ready, 1)
        dve.tensor_scalar(self.stat[:, 0, :], self.sum_ps[:], 1.0 / D, EPS, ALU.mult, ALU.add
                          ).then_inc(self.mean_ready, 1)
        dve.wait_ge(self.root_ready, 1)
        dve.reciprocal(self.stat[:, 0, :], self.stat[:, 1, :]).then_inc(self.rstd_ready, 1)
        dve.wait_ge(self.rstd_ready, 1)
        dve.wait_ge(self.gain_landed, 16)

    def vector_split(self, dve, x_hi, x_lo, scaled=True):
        def low(k):
            dve.wait_ge(self.x_high, k + 1)
            dve.tensor_tensor(x_lo[:, k, :], self.xn[:, k % 2, :], x_hi[:, k, :].bitcast(F32), ALU.subtract
                              ).then_inc(self.x_split, 1)
        for k in range(KC):
            if k >= 2:
                dve.wait_ge(self.x_split, k - 1)
            if scaled:
                dve.scalar_tensor_tensor(self.xn[:, k % 2, :], self.hT[:, k, :], self.gain[:, k:k + 1],
                                         self.stat[:, 0, :], ALU.mult, ALU.mult).then_inc(self.xn_ready, 1)
            else:
                dve.tensor_scalar(self.xn[:, k % 2, :], self.hT[:, k, :], self.gain[:, k:k + 1], None, ALU.mult
                                  ).then_inc(self.xn_ready, 1)
            if k >= 1:
                low(k - 1)
        low(KC - 1)

    def tensor(self, pe):
        pe.wait_ge(self.ones_ready, 1)
        pe.wait_ge(self.sq_added, KC - 1)
        pe.matmul(self.sum_ps[:], self.ones[:], self.stat[:, 1, :], start=True, stop=True
                  ).then_inc(self.sum_ready, 1)


def in_blocks(x):
    return x.rearrange("p (b t) -> p b t", t=TOKENS)


def routing_of(routing, column, count):
    return routing[:, :, bass.ds(column, count), :].rearrange("b r c t -> r b (c t)")


def hidden_stage(nc, name, hT, x_hi, x_lo, up_w, down_w, norm_g=None, routing=None, column=0):
    swiglu = norm_g is not None
    PJ = 2 if swiglu else 1
    J = 4
    n_hid = up_w.shape[0] // PJ
    groups, rest = divmod(n_hid - 1, J)
    rest += 1
    assert groups and rest >= 2
    assert swiglu or rest == J
    NP = PJ * J
    with ExitStack() as ctx:
        c = Chip(nc, ctx)
        a_raw = c.sb(f"{name}_a_raw", [P, RING, PANEL])
        a_hi = c.sb(f"{name}_a_hi", [P, RING, PANEL], F32R)
        a_lo = c.sb(f"{name}_a_lo", [P, RING, PANEL], F32R)
        b_raw = c.sb(f"{name}_b_raw", [P, J, D])
        b_hi = c.sb(f"{name}_b_hi", [P, J, D], F32R)
        b_lo = c.sb(f"{name}_b_lo", [P, J, D], F32R)
        g_hi = c.sb(f"{name}_g_hi", [P, J, SEQ], F32R)
        g_lo = c.sb(f"{name}_g_lo", [P, J, SEQ], F32R)
        act_out = c.sb(f"{name}_act", [P, 2, SEQ])
        prod = c.sb(f"{name}_prod", [P, 2, SEQ])
        route = None if swiglu else c.sb(f"{name}_route", [P, SEQ // TOKENS, J * TOKENS])
        scaled = c.sb(f"{name}_scaled", [P, 2, 2, SEQ]) if swiglu else None
        u_ps = [[c.ps(f"{name}_u{a}{b}", [P, SEQ]) for b in range(PJ)] for a in range(2)]
        y_ps = [c.ps(f"{name}_y{a}", [P, SEQ]) for a in range(4)]
        norm = NormStage(c, name, hT, norm_g, y_ps[0], act_out, prod,
                         c.sb(f"{name}_stat", [P, 2, SEQ])) if swiglu else None

        a_landed = [c.sem(f"{name}_a_landed{s}") for s in range(RING)]
        b_landed = [c.sem(f"{name}_b_landed{s}") for s in range(J)]
        r_landed = None if swiglu else c.sem(f"{name}_r_landed")
        (a_high, a_split, b_high, b_split, up_done, gate_scaled, up_scaled, act_done, prod_done, hid_high, hid_split, y_done,
         y_added) = named = [c.sem(f"{name}_{x}") for x in (
             "a_high", "a_split", "b_high", "b_split", "up_done", "gate_scaled", "up_scaled", "act_done", "prod_done", "hid_high",
             "hid_split", "y_done", "y_added")]
        sems = [*a_landed, *b_landed, *named, *(norm.sems if swiglu else [r_landed])]
        A_FREE, B_FREE, Y_USED, PAIRS, HID_FREE, Y_BANKS = RING, J, 1, 2, J, 4

        def group_loop(eng, body):
            with eng.Fori(0, groups) as g:
                body(g, J)
            body(groups, rest)

        def ahead(g, count, j):
            return [k for k in range(PJ * j + 2, PJ * j + 2 + PJ) if g is not groups or k < PJ * count]

        with nc.Block() as block:
            @block.sync
            def _(sp):
                if swiglu:
                    norm.sync(sp)

                def body(g, count):
                    for j in range(count):
                        for k in range(PJ * j, PJ * (j + 1)):
                            sp.wait_ge(a_split, g * NP + k + 1)
                            sp.dma_start(a_raw[:, k % RING, :],
                                         up_w[bass.ds(g * NP + k, 1)].rearrange("o p f -> p (o f)")
                                         ).then_inc(a_landed[k % RING], 16)
                        if not swiglu and j == 1:
                            sp.wait_ge(hid_split, g * J + HID_FREE)
                            sp.dma_start(route[:], routing_of(routing, g * J + column, J)).then_inc(r_landed, 16)
                        sp.wait_ge(b_split, g * J + j + 1)
                        sp.dma_start(b_raw[:, j, :], down_w(g * J + j)).then_inc(b_landed[j], 16)
                group_loop(sp, body)

            def a_high_part(g, k):
                nc.scalar.wait_ge(a_landed[k % RING], g * (NP // RING * 16) + 16 * (k // RING + 1))
                nc.scalar.wait_ge(up_done, g * NP + k + 1)
                nc.scalar.copy(a_hi[:, k % RING, :], a_raw[:, k % RING, :]).then_inc(a_high, 1)

            def a_low_part(g, k):
                nc.vector.wait_ge(a_high, g * NP + k + 1)
                nc.vector.tensor_tensor(a_lo[:, k % RING, :], a_raw[:, k % RING, :],
                                        a_hi[:, k % RING, :].bitcast(F32), ALU.subtract).then_inc(a_split, 1)

            @block.scalar
            def _(act):
                a_high_part(0, 0)
                if swiglu:
                    norm.scalar_high(act, x_hi)
                a_high_part(0, 1)
                for k in ahead(0, J, 0):
                    a_high_part(0, k)
                if swiglu:
                    norm.scalar_squares(act)
                    norm.scalar_root(act)

                def body(g, count):
                    for j in range(count):
                        for k in ahead(g, count, j) if j else []:
                            a_high_part(g, k)
                        act.wait_ge(prod_done, g * J + j + 1)
                        if swiglu:
                            act.wait_ge(gate_scaled, g * J + j + 1)
                            act.activation(act_out[:, j % 2, :], scaled[:, j % 2, 0, :], ACT.Silu
                                           ).then_inc(act_done, 1)
                        else:
                            act.wait_ge(up_done, g * NP + PJ * j + 1 + A_FREE)
                            act.activation(act_out[:, j % 2, :], u_ps[j % 2][0][:], ACT.Gelu_apprx_tanh
                                           ).then_inc(act_done, 1)
                        act.wait_ge(b_landed[j], g * 16 + 16)
                        act.wait_ge(y_done, g * KC + Y_USED)
                        act.copy(b_hi[:, j, :], b_raw[:, j, :]).then_inc(b_high, 1)
                        act.wait_ge(prod_done, g * J + j + 1 + PAIRS)
                        act.copy(g_hi[:, j, :], prod[:, j % 2, :]).then_inc(hid_high, 1)
                    for k in ahead(g, count, J) if g is not groups else []:
                        a_high_part(g, k)
                group_loop(act, body)

            @block.vector
            def _(dve):
                dve.sem_inc(a_split, A_FREE)
                dve.sem_inc(prod_done, PAIRS)
                dve.sem_inc(hid_split, HID_FREE)
                dve.sem_inc(y_added, Y_BANKS)
                a_low_part(0, 0)
                if swiglu:
                    norm.vector_scale(dve, x_hi, x_lo)
                a_low_part(0, 1)
                for k in ahead(0, J, 0):
                    a_low_part(0, k)
                if swiglu:
                    norm.vector_add(dve)
                    norm.vector_inverse(dve)

                def body(g, count):
                    for j in range(count):
                        for k in ahead(g, count, j) if j else []:
                            a_low_part(g, k)
                        if swiglu:
                            dve.wait_ge(prod_done, g * J + j + 1)
                            dve.wait_ge(up_done, g * NP + PJ * j + 1 + A_FREE)
                            dve.tensor_tensor(scaled[:, j % 2, 0, :], u_ps[j % 2][0][:], norm.stat[:, 0, :],
                                              ALU.mult).then_inc(gate_scaled, 1)
                            dve.wait_ge(up_done, g * NP + PJ * j + 2 + A_FREE)
                            dve.scalar_tensor_tensor(scaled[:, j % 2, 1, :], u_ps[j % 2][1][:], 0.5,
                                                     norm.stat[:, 0, :], ALU.mult, ALU.mult
                                                     ).then_inc(up_scaled, 1)
                            dve.wait_ge(up_scaled, g * J + j + 1)
                        dve.wait_ge(act_done, g * J + j + 1)
                        dve.wait_ge(hid_split, g * J + j - 1 + HID_FREE)
                        if swiglu:
                            dve.tensor_tensor(prod[:, j % 2, :], act_out[:, j % 2, :], scaled[:, j % 2, 1, :],
                                              ALU.mult).then_inc(prod_done, 1)
                        else:
                            dve.wait_ge(r_landed, g * 16 + 16)
                            dve.tensor_tensor(in_blocks(prod[:, j % 2, :]), in_blocks(act_out[:, j % 2, :]),
                                              route[:, :, j * TOKENS:(j + 1) * TOKENS], ALU.mult
                                              ).then_inc(prod_done, 1)
                        dve.wait_ge(hid_high, g * J + j + 1)
                        dve.tensor_tensor(g_lo[:, j, :], prod[:, j % 2, :], g_hi[:, j, :].bitcast(F32),
                                          ALU.subtract).then_inc(hid_split, 1)
                    for k in ahead(g, count, J) if g is not groups else []:
                        a_low_part(g, k)
                    for f in range(KC):
                        dve.wait_ge(y_done, g * KC + f + 1 + Y_USED)
                        dve.tensor_tensor(hT[:, f, :], hT[:, f, :], y_ps[f % 4][:], ALU.add
                                          ).then_inc(y_added, 1)
                group_loop(dve, body)

            @block.gpsimd
            def _(pool):
                if swiglu:
                    norm.gpsimd(pool)
                pool.sem_inc(b_split, B_FREE)

                def body(g, count):
                    for j in range(count):
                        pool.wait_ge(b_high, g * J + j + 1)
                        pool.tensor_tensor(b_lo[:, j, :], b_raw[:, j, :], b_hi[:, j, :].bitcast(F32),
                                           ALU.subtract).then_inc(b_split, 1)
                group_loop(pool, body)

            @block.tensor
            def _(pe):
                pe.sem_inc(up_done, A_FREE)
                pe.sem_inc(y_done, Y_USED)

                def up(g, j):
                    pe.wait_ge(prod_done, g * J + (j + 1))
                    for k in range(PJ * j, PJ * (j + 1)):
                        pe.wait_ge(a_split, g * NP + (k + 1 + A_FREE))
                        s = k % RING
                        for kc in range(KC):
                            if swiglu and k == 0:
                                pe.wait_ge(norm.x_split, kc + 1)
                            cols = slice(kc * P, (kc + 1) * P)
                            last = three_products(pe, u_ps[j % 2][k % PJ][:], a_hi[:, s, cols],
                                                  a_lo[:, s, cols], x_hi[:, kc, :], x_lo[:, kc, :], kc == 0,
                                                  kc == KC - 1)
                        last.then_inc(up_done, 1)

                up(0, 0)
                if swiglu:
                    norm.tensor(pe)

                def body(g, count):
                    for j in range(1, count if g is groups else J + 1):
                        up(g, j)
                    for f in range(KC):
                        pe.wait_ge(y_added, g * KC + f + 1)
                        for j in range(count):
                            if f == 0:
                                pe.wait_ge(b_split, g * J + j + 1 + B_FREE)
                                pe.wait_ge(hid_split, g * J + j + 1 + HID_FREE)
                            cols = slice(f * P, (f + 1) * P)
                            last = three_products(pe, y_ps[f % 4][:], b_hi[:, j, cols], b_lo[:, j, cols],
                                                  g_hi[:, j, :], g_lo[:, j, :], j == 0, j == count - 1)
                        last.then_inc(y_done, 1)
                group_loop(pe, body)
    clear_semaphores(nc, sems)


class Projection:

    def __init__(self, c, name, w, x_hi, x_lo, dst, add=False):
        self.w, self.x_hi, self.x_lo, self.dst, self.add = w, x_hi, x_lo, dst, add
        self.n = w.shape[0]
        self.kc = w.shape[2] // P
        self.raw = c.sb(f"{name}_raw", [P, RING, self.kc * P])
        self.hi = c.sb(f"{name}_hi", [P, RING, self.kc * P], F32R)
        self.lo = c.sb(f"{name}_lo", [P, RING, self.kc * P], F32R)
        self.ps = [c.ps(f"{name}_ps{s}", [P, SEQ]) for s in range(RING)]
        self.landed = [c.sem(f"{name}_landed{s}") for s in range(RING)]
        self.high, self.split, self.product, self.taken = (
            c.sem(f"{name}_{x}") for x in ("high", "split", "product", "taken"))
        self.sems = [*self.landed, self.high, self.split, self.product, self.taken]
        self.groups, self.rest = divmod(self.n - 1, RING)
        self.rest += 1

    def loop(self, eng, body):
        if self.groups:
            with eng.Fori(0, self.groups) as g:
                body(g, RING)
        body(self.groups, self.rest)

    def sync(self, sp):
        def body(g, count):
            for k in range(count):
                sp.wait_ge(self.split, g * RING + k + 1)
                sp.dma_start(self.raw[:, k, :], self.w[bass.ds(g * RING + k, 1)].rearrange("o p f -> p (o f)")
                             ).then_inc(self.landed[k], 16)
        self.loop(sp, body)

    def scalar(self, act, then=None):
        def high(g, k):
            act.wait_ge(self.landed[k % RING], g * 16 + 16 * (k // RING + 1))
            act.wait_ge(self.product, g * RING + k + 1)
            act.copy(self.hi[:, k % RING, :], self.raw[:, k % RING, :]).then_inc(self.high, 1)

        for k in range(min(2, self.n)):
            high(0, k)
        if then is not None:
            then(act)

        def body(g, count):
            for k in range(count):
                if g is not self.groups or k + 2 < count:
                    high(g, k + 2)
                if not self.add:
                    act.wait_ge(self.product, g * RING + k + 1 + RING)
                    act.copy(self.dst[:, bass.ds(g * RING + k, 1), :].rearrange("p o s -> p (o s)"),
                             self.ps[k][:]).then_inc(self.taken, 1)
        self.loop(act, body)

    def vector(self, dve, first=None, then=None):
        dve.sem_inc(self.split, RING)
        if first is not None:
            first(dve)

        def low(g, k):
            dve.wait_ge(self.high, g * RING + k + 1)
            dve.tensor_tensor(self.lo[:, k % RING, :], self.raw[:, k % RING, :],
                              self.hi[:, k % RING, :].bitcast(F32), ALU.subtract).then_inc(self.split, 1)

        for k in range(min(2, self.n)):
            low(0, k)
        if then is not None:
            then(dve)

        def body(g, count):
            for k in range(count):
                if g is not self.groups or k + 2 < count:
                    low(g, k + 2)
                if self.add:
                    dve.wait_ge(self.product, g * RING + k + 1 + RING)
                    old = self.dst[:, bass.ds(g * RING + k, 1), :].rearrange("p o s -> p (o s)")
                    dve.tensor_tensor(old, old, self.ps[k][:], ALU.add).then_inc(self.taken, 1)
        self.loop(dve, body)

    def tensor(self, pe, x_ready=None):
        pe.sem_inc(self.product, RING)
        pe.sem_inc(self.taken, RING)

        def body(g, count):
            for k in range(count):
                pe.wait_ge(self.split, g * RING + k + 1 + RING)
                pe.wait_ge(self.taken, g * RING + k + 1)
                for kc in range(self.kc):
                    if x_ready is not None and k == 0:
                        pe.wait_ge(x_ready, kc + 1)
                    cols = slice(kc * P, (kc + 1) * P)
                    last = three_products(pe, self.ps[k][:], self.hi[:, k, cols], self.lo[:, k, cols],
                                          self.x_hi[:, kc, :], self.x_lo[:, kc, :], kc == 0, kc == self.kc - 1)
                last.then_inc(self.product, 1)
        self.loop(pe, body)


class PanelStream:

    def __init__(self, c, name, w, x_hi, x_lo, result, function):
        self.w, self.x_hi, self.x_lo, self.result, self.n = w, x_hi, x_lo, result, w.shape[0]
        self.function = function
        self.raw = c.sb(f"{name}_raw", [P, RING, PANEL])
        self.hi = c.sb(f"{name}_hi", [P, RING, PANEL], F32R)
        self.lo = c.sb(f"{name}_lo", [P, RING, PANEL], F32R)
        self.out = c.sb(f"{name}_out", [P, 2, SEQ])
        self.ps = [c.ps(f"{name}_ps{s}", [P, SEQ]) for s in range(2)]
        self.landed = [c.sem(f"{name}_landed{s}") for s in range(RING)]
        self.stored = [c.sem(f"{name}_stored{s}") for s in range(2)]
        self.high, self.split, self.product, self.active = (
            c.sem(f"{name}_{x}") for x in ("high", "split", "product", "active"))
        self.sems = [*self.landed, *self.stored, self.high, self.split, self.product, self.active]

    def sync(self, sp):
        for s in self.stored:
            sp.sem_inc(s, 16)

        def load(g, k):
            sp.wait_ge(self.split, g * RING + k + 1)
            sp.dma_start(self.raw[:, k, :], self.w[bass.ds(g * RING + k, 1)].rearrange("o p f -> p (o f)")
                         ).then_inc(self.landed[k], 16)

        def store(g, k):
            sp.wait_ge(self.active, g * RING + k + 1 + 2)
            sp.dma_start(self.result[bass.ds(g * RING + k, 1)].rearrange("o p f -> p (o f)"),
                         self.out[:, k % 2, :]).then_inc(self.stored[k % 2], 16)

        groups = self.n // RING
        for k in range(RING):
            load(0, k)
        with sp.Fori(0, groups - 1) as g:
            for k in range(RING):
                load(g + 1, k)
                store(g, k)
        for k in range(RING):
            store(groups - 1, k)
        for s in self.stored:
            sp.wait_ge(s, 16 + 16 * (self.n // 2))

    def start_high(self, act):
        act.sem_inc(self.active, 2)
        self.high_part(act, 0, 0)
        self.high_part(act, 0, 1)

    def start_low(self, eng):
        eng.sem_inc(self.split, RING)

    def start_tensor(self, pe):
        pe.sem_inc(self.product, RING)

    def high_part(self, act, g, k):
        s = k % RING
        act.wait_ge(self.landed[s], g * 16 + 16 * (k // RING + 1))
        act.wait_ge(self.product, g * RING + (k + 1))
        act.copy(self.hi[:, s, :], self.raw[:, s, :]).then_inc(self.high, 1)

    def scalar(self, act, g, k, ends):
        if not ends or g * RING + k + 2 < self.n:
            self.high_part(act, g, k + 2)
        s = k % 2
        act.wait_ge(self.product, g * RING + (k + 1 + RING))
        act.wait_ge(self.stored[s], g * (RING // 2 * 16) + 16 * (k // 2 + 1))
        act.activation(self.out[:, s, :], self.ps[s][:], self.function).then_inc(self.active, 1)

    def low(self, eng, g, k):
        s = k % RING
        eng.wait_ge(self.high, g * RING + (k + 1))
        eng.tensor_tensor(self.lo[:, s, :], self.raw[:, s, :], self.hi[:, s, :].bitcast(F32), ALU.subtract
                          ).then_inc(self.split, 1)

    def tensor(self, pe, g, k, part=slice(0, KC)):
        s = k % RING
        if part.start == 0:
            pe.wait_ge(self.split, g * RING + (k + 1 + RING))
            pe.wait_ge(self.active, g * RING + (k + 1))
        for kc in range(part.start, part.stop):
            cols = slice(kc * P, (kc + 1) * P)
            last = three_products(pe, self.ps[k % 2][:], self.hi[:, s, cols], self.lo[:, s, cols],
                                  self.x_hi[:, kc, :], self.x_lo[:, kc, :], kc == 0, kc == KC - 1)
        if part.stop == KC:
            last.then_inc(self.product, 1)


class Attention:

    def __init__(self, c, name, units, scale, ident, stream=None):
        self.units, self.scale, self.ident, self.stream = units, scale, ident, stream
        if stream is not None:
            self.every = len(units) // stream.n
            self.share = KC // self.every
        n = len(units)
        self.biased = c.sb(f"{name}_biased", [P, 2, SEQ])
        self.probs = c.sb(f"{name}_probs", [P, 2, SEQ])
        self.probsT = c.sb(f"{name}_probsT", [P, 2, SEQ])
        self.top = c.sb(f"{name}_top", [P, n])
        self.shift = c.sb(f"{name}_shift", [P, n])
        self.total = c.sb(f"{name}_total", [P, n])
        self.inverse = c.sb(f"{name}_inverse", [P, n])
        self.s_ps = [c.ps(f"{name}_s{i}", [P, SEQ]) for i in range(2)]
        self.t_ps = [c.ps(f"{name}_t{i}", [P, SEQ]) for i in range(2)]
        self.o_ps = [c.ps(f"{name}_o{i}", [P, SEQ]) for i in range(2)]
        (self.scored, self.maxed, self.shifted, self.exped, self.turned, self.copied, self.weighted,
         self.inverted, self.gated, self.stored) = self.sems = [
            c.sem(f"{name}_{x}") for x in ("scored", "maxed", "shifted", "exped", "turned", "copied",
                                           "weighted", "inverted", "gated", "stored")]
        self.gated_units = 0

    def vector(self, dve):
        n = len(self.units)
        for i in range(n + 3):
            if i < n:
                u, w = self.units[i], self.units[i]["width"]
                dve.wait_ge(self.scored, i + 1)
                if i >= 2:
                    dve.wait_ge(self.exped, i - 1)
                dve.tensor_tensor_reduce(out=self.biased[:, i % 2, :w], in0=self.s_ps[i % 2][:, :w], in1=u["bias"],
                                         scale=1.0, scalar=-3.0e38, op0=ALU.add, op1=ALU.max,
                                         accum_out=self.top[:, i:i + 1]).then_inc(self.maxed, 1)
                dve.wait_ge(self.maxed, i + 1)
                dve.tensor_scalar(self.shift[:, i:i + 1], self.top[:, i:i + 1], -self.scale, None, ALU.mult
                                  ).then_inc(self.shifted, 1)
            if i >= 3:
                j = i - 3
                dve.wait_ge(self.exped, j + 1)
                u, inverse = self.units[j], self.inverse[:, j:j + 1]
                dve.reciprocal(inverse, self.total[:, j:j + 1]).then_inc(self.inverted, 1)
                dve.wait_ge(self.inverted, j + 1)
                if u["gate"] is not None:
                    self.gated_units += 1
                    dve.tensor_tensor(inverse, inverse, u["gate"], ALU.mult).then_inc(self.gated, 1)
                    dve.wait_ge(self.gated, self.gated_units)
                dve.wait_ge(self.weighted, j + 1)
                result = self.o_ps[j % 2][:, :u["dv"]]
                if u["add"]:
                    dve.wait_ge(self.stored, j)
                    done = dve.scalar_tensor_tensor(u["out"], result, inverse, u["out"], ALU.mult, ALU.add)
                else:
                    done = dve.tensor_scalar(u["out"], result, inverse, None, ALU.mult)
                done.then_inc(self.stored, 1)

    def scalar(self, act):
        n = len(self.units)
        if self.stream is not None:
            self.stream.start_high(act)
        for i in range(n + 1):
            if self.stream is not None and i >= self.every and i % self.every == 0:
                self.stream.scalar(act, 0, i // self.every - 1, ends=True)
            if i < n:
                w = self.units[i]["width"]
                act.wait_ge(self.shifted, i + 1)
                if i >= 2:
                    act.wait_ge(self.turned, i - 1)
                act.activation(self.probs[:, i % 2, :w], self.biased[:, i % 2, :w], ACT.Exp, scale=self.scale,
                               bias=self.shift[:, i:i + 1], accum_out=self.total[:, i:i + 1]
                               ).then_inc(self.exped, 1)
            if i >= 1:
                j, w = i - 1, self.units[i - 1]["width"]
                act.wait_ge(self.turned, j + 1)
                if j >= 2:
                    act.wait_ge(self.weighted, j - 1)
                act.copy(self.probsT[:, j % 2, :w], self.t_ps[j % 2][:, :w]).then_inc(self.copied, 1)

    def tensor(self, pe):
        n = len(self.units)
        if self.stream is not None:
            self.stream.start_tensor(pe)
        for i in range(n + 2):
            if i < n:
                u = self.units[i]
                if i >= 2:
                    pe.wait_ge(self.maxed, i - 1)
                pe.matmul(self.s_ps[i % 2][:, :u["width"]], u["q"], u["k"], start=True, stop=True
                          ).then_inc(self.scored, 1)
            if 1 <= i <= n:
                j = i - 1
                pe.wait_ge(self.exped, j + 1)
                if j >= 2:
                    pe.wait_ge(self.copied, j - 1)
                for b in range(self.units[j]["width"] // P):
                    cols = slice(b * P, (b + 1) * P)
                    last = pe.transpose(self.t_ps[j % 2][:, cols], self.probs[:, j % 2, cols], self.ident[:])
                last.then_inc(self.turned, 1)
            if self.stream is not None and i < n:
                at = i % self.every * self.share
                self.stream.tensor(pe, 0, i // self.every, slice(at, at + self.share))
            if i >= 2:
                j = i - 2
                u = self.units[j]
                pe.wait_ge(self.copied, j + 1)
                if j >= 2:
                    pe.wait_ge(self.stored, j - 1)
                blocks = u["width"] // P
                for b in range(blocks):
                    last = pe.matmul(self.o_ps[j % 2][:, :u["dv"]], self.probsT[:, j % 2, b * P:(b + 1) * P],
                                     u["v"](b), start=b == 0, stop=b == blocks - 1)
                last.then_inc(self.weighted, 1)


def stream_low(stream):
    def program(pool):
        stream.start_low(pool)
        for k in range(stream.n):
            stream.low(pool, 0, k)
    return program


def norm_and_project(nc, name, hT, x_hi, x_lo, gain, w, dst, load_more=None):
    with ExitStack() as ctx:
        c = Chip(nc, ctx)
        proj = Projection(c, name, w, x_hi, x_lo, dst)
        norm = NormStage(c, name, hT, gain, c.ps(f"{name}_sum", [P, SEQ]), c.sb(f"{name}_sq", [P, 2, SEQ]),
                         c.sb(f"{name}_xn", [P, 2, SEQ]), c.sb(f"{name}_stat", [P, 2, SEQ]))
        with nc.Block() as block:
            @block.sync
            def _(sp):
                norm.sync(sp)
                proj.sync(sp)
                if load_more is not None:
                    load_more(sp)

            @block.gpsimd
            def _(pool):
                norm.gpsimd(pool)

            @block.scalar
            def _(act):
                norm.scalar_squares(act)

                def rest(act):
                    norm.scalar_root(act)
                    norm.scalar_high(act, x_hi)
                proj.scalar(act, rest)

            @block.vector
            def _(dve):
                def rest(dve):
                    norm.vector_inverse(dve)
                    norm.vector_split(dve, x_hi, x_lo)
                proj.vector(dve, norm.vector_add, rest)

            @block.tensor
            def _(pe):
                norm.tensor(pe)
                proj.tensor(pe, norm.x_split)
    clear_semaphores(nc, [*norm.sems, *proj.sems])


def project_onto(nc, name, x_hi, x_lo, w, hT):
    with ExitStack() as ctx:
        proj = Projection(Chip(nc, ctx), name, w, x_hi, x_lo, hT, add=True)
        with nc.Block() as block:
            block.sync(proj.sync)
            block.scalar(proj.scalar)
            block.vector(proj.vector)
            block.tensor(proj.tensor)
    clear_semaphores(nc, proj.sems)



A_GROUPS = 4
N_HEADS = 4
KV_LATENT = 256
IDX_HEADS = 4
IDX_DIM = 64
TILES = SEQ // P
TOPK = SEQ // 4
TAKEN = -3.4e38
FUTURE = -3.0e38
MASKED = -1e30

U0, V0, Q0, C0, QI0, KI0, WI0 = 0, 4, 8, 12, 14, 16, 17
N_PROJ1 = 18


def gate_and_prepare(nc, proj, kT, vv, wi, ident, ya_hi, ya_lo, d):
    with ExitStack() as ctx:
        c = Chip(nc, ctx)
        ones = c.sb("m1_ones", [P, P])
        wsT = c.sb("m1_wsT", [P, A_GROUPS, P])
        bs = c.sb("m1_bs", [1, A_GROUPS, P])
        vg = c.sb("m1_vg", [P, SEQ])
        vb = c.sb("m1_vb", [P, SEQ])
        gains = c.sb("m1_gains", [P, 4])
        wuk = c.sb("m1_wuk", [P, 2, P])
        wuv = c.sb("m1_wuv", [P, 2, P])
        rot = c.sb("m1_rot", [P, 2, P])
        inv = c.sb("m1_inv", [P, 2])
        posi = c.sb("m1_posi", [P, SEQ], I32)
        pos = c.sb("m1_pos", [P, SEQ])
        ang = c.sb("m1_ang", [P, SEQ])
        turns = c.sb("m1_turns", [P, SEQ])
        sin = [c.sb(f"m1_sin{i}", [P, SEQ]) for i in range(2)]
        cos = [c.sb(f"m1_cos{i}", [P, SEQ]) for i in range(2)]
        sq = c.sb("m1_sq", [P, 3 + N_HEADS, SEQ])
        ms = c.sb("m1_ms", [P, 2, SEQ])
        rstd = c.sb("m1_rstd", [P, SEQ])
        vn = c.sb("m1_vn", [P, TILES, SEQ])
        stats = c.sb("m1_stats", [P, TILES, 6])
        mv = c.sb("m1_mv", [P, TILES, 2])
        sd = c.sb("m1_sd", [P, TILES])
        turned = c.sb("m1_turned", [P, SEQ])
        banks = [c.ps(f"m1_bank{i}", [P, SEQ]) for i in range(8)]

        S = {x: c.sem(f"m1_{x}") for x in (
            "small", "positions", "const", "masked", "gelu", "vt", "ln_var", "ln_sd", "vnorm", "seq",
            "sq", "job", "took", "ms", "root", "half", "angle", "sines", "normed", "gated", "low")}
        small, job, took, seq = S["small"], S["job"], S["took"], S["seq"]
        SMALL = ["wsT", "bs", "vg", "vb", "gains", "wuk", "wuv", "rot"]
        R128, R64 = 0, 1
        JOBS = (["sum_c", "rot_qi0", "rot_qi1", "rot_ki"] + [f"sum_q{h}" for h in range(N_HEADS)]
                + ["k", "vv", "sum_k"] + [f"z{g}" for g in range(A_GROUPS)]
                + [f"rot_q{h}" for h in range(N_HEADS)] + ["rot_k", "wi"])
        NUM = {x: i for i, x in enumerate(JOBS)}
        SQS = ["c0", "c1"] + [f"q{h}" for h in range(N_HEADS)] + ["k"]
        QK = [f"q{h}" for h in range(N_HEADS)] + ["k"]

        def bank(x):
            return banks[4 + NUM[x] % 4]

        with nc.Block() as block:
            @block.sync
            def _(sp):
                sp.dma_start(posi[:], d["positions"].rearrange("a s -> (a s)").partition_broadcast(P)
                             ).then_inc(S["positions"], 16)
                sp.dma_start(inv[:], d["inv"]).then_inc(S["positions"], 16)
                sp.dma_start(rot[:], d["rot"]).then_inc(small, 16)
                sp.dma_start(gains[:], d["gains"]).then_inc(small, 16)
                sp.dma_start(wuk[:], d["wuk"]).then_inc(small, 16)
                sp.dma_start(wuv[:], d["wuv"]).then_inc(small, 16)
                sp.dma_start(wsT[:], d["wsT"]).then_inc(small, 16)
                sp.dma_start(bs[:], d["bs"]).then_inc(small, 16)
                sp.dma_start(vg[:], d["vg"].partition_broadcast(P)).then_inc(small, 16)
                sp.dma_start(vb[:], d["vb"].partition_broadcast(P)).then_inc(small, 16)

            @block.gpsimd
            def _(pool):
                pool.memset(ones[:], 1.0).then_inc(S["const"], 1)
                pool.memset(ident[:], 0.0).then_inc(S["const"], 1)
                pool.wait_ge(S["const"], 2)
                pool.affine_select(out=ident[:], in_=ident[:], compare_op=ALU.not_equal, fill=1.0, base=0,
                                   pattern=[[-1, P]], channel_multiplier=1).then_inc(S["const"], 1)
                pool.wait_ge(small, 16 * len(SMALL))
                pool.affine_select(out=wsT[:], in_=wsT[:], compare_op=ALU.is_ge, fill=0.0, base=0,
                                   pattern=[[0, A_GROUPS], [1, P]], channel_multiplier=-1
                                   ).then_inc(S["masked"], 1)
                for g in range(A_GROUPS):
                    pool.wait_ge(S["half"], g + 1)
                    pool.tensor_tensor(ya_lo[:, g, :], proj[:, U0 + g, :], ya_hi[:, g, :].bitcast(F32),
                                       ALU.subtract).then_inc(S["low"], 1)

            @block.scalar
            def _(act):
                for tiles in (slice(V0, V0 + 4), slice(U0, U0 + 4)):
                    act.activation(proj[:, tiles, :], proj[:, tiles, :], ACT.Gelu_apprx_tanh
                                   ).then_inc(S["gelu"], 1)
                    for i, x in enumerate(SQS[:-1]):
                        if tiles.start == V0:
                            src = proj[:, C0 + i, :] if i < 2 else proj[:, Q0 + i - 2, :]
                            act.activation(sq[:, i, :], src, ACT.Square).then_inc(S["sq"], 1)
                def root(n):
                    act.wait_ge(S["ms"], n + 1)
                    act.activation(ms[:, n % 2, :], ms[:, n % 2, :], ACT.Sqrt).then_inc(S["root"], 1)
                for kind in (R128, R64):
                    act.wait_ge(S["angle"], kind + 1)
                    act.activation(sin[kind][:], ang[:], ACT.Sin).then_inc(S["sines"], 1)
                    act.activation(cos[kind][:], ang[:], ACT.Sin, scale=0.5).then_inc(S["sines"], 1)
                act.wait_ge(S["ln_var"], 1)
                act.activation(sd[:], sd[:], ACT.Sqrt).then_inc(S["ln_sd"], 1)
                for n in range(1 + N_HEADS):
                    root(n)
                act.wait_ge(took, NUM["k"] + 1)
                act.activation(sq[:, 2 + N_HEADS, :], kT[:], ACT.Square).then_inc(S["sq"], 1)
                root(1 + N_HEADS)
                for g in range(A_GROUPS):
                    act.wait_ge(S["gated"], g + 1)
                    act.copy(ya_hi[:, g, :], proj[:, U0 + g, :]).then_inc(S["half"], 1)

            @block.vector
            def _(dve):
                done = [0]

                def then(instruction):
                    done[0] += 1
                    instruction.then_inc(seq, 1)
                    dve.wait_ge(seq, done[0])

                def take(x):
                    dve.wait_ge(job, NUM[x] + 1)

                TWO_PI_1, TWO_PI_2 = 6.28125, 1.9353071795e-3
                ROUND = 12582912.0
                dve.wait_ge(S["positions"], 32)
                then(dve.tensor_copy(pos[:], posi[:]))
                for kind in (R128, R64):
                    if kind:
                        dve.wait_ge(S["sines"], 2)
                    then(dve.tensor_scalar(ang[:], pos[:], inv[:, kind:kind + 1], None, ALU.mult))
                    then(dve.tensor_scalar(turns[:], ang[:], 1.0 / (2 * 3.141592653589793), ROUND, ALU.mult,
                                           ALU.add))
                    then(dve.tensor_scalar(turns[:], turns[:], -ROUND, None, ALU.add))
                    then(dve.scalar_tensor_tensor(ang[:], turns[:], -TWO_PI_1, ang[:], ALU.mult, ALU.add))
                    then(dve.scalar_tensor_tensor(ang[:], turns[:], -TWO_PI_2, ang[:], ALU.mult, ALU.add))
                    dve.tensor_scalar(ang[:], ang[:], 3.1415925, -3.1415925, ALU.min, ALU.max
                                      ).then_inc(S["angle"], 1)
                    if kind == R64:
                        break
                    for t in range(TILES):
                        dve.wait_ge(S["vt"], t + 1)
                        then(dve.bn_stats(stats[:, t, :], banks[t][:]))
                        then(dve.bn_aggr(mv[:, t, :], stats[:, t, :]))
                    dve.tensor_scalar(sd[:], mv[:, :, 1], EPS, None, ALU.add).then_inc(S["ln_var"], 1)

                def mean_square(x, features, n):
                    take(x)
                    dve.tensor_scalar(ms[:, n % 2, :], bank(x)[:], 1.0 / features, EPS, ALU.mult, ALU.add
                                      ).then_inc(S["ms"], 1)
                    dve.wait_ge(S["ms"], n + 1)
                    dve.sem_inc(took, 1)

                def reciprocal_root(n):
                    dve.wait_ge(S["root"], n + 1)
                    then(dve.reciprocal(rstd[:], ms[:, n % 2, :]))

                def rope(x, tile, kind):
                    take(x)
                    then(dve.tensor_tensor(tile, tile, cos[kind][:], ALU.mult))
                    dve.tensor_tensor(turned[:], bank(x)[:], sin[kind][:], ALU.mult).then_inc(took, 1)
                    dve.wait_ge(took, NUM[x] + 1)
                    then(dve.tensor_tensor(tile, tile, turned[:], ALU.add))

                dve.wait_ge(small, 16 * len(SMALL))
                mean_square("sum_c", KV_LATENT, 0)
                reciprocal_root(0)
                for k in range(2):
                    dve.scalar_tensor_tensor(proj[:, C0 + k, :], proj[:, C0 + k, :], gains[:, k:k + 1], rstd[:],
                                             ALU.mult, ALU.mult).then_inc(S["normed"] if k else seq, 1)
                    if not k:
                        done[0] += 1
                for kind in (R128, R64):
                    dve.wait_ge(S["sines"], 2 * kind + 2)
                    then(dve.tensor_tensor(cos[kind][:], cos[kind][:], cos[kind][:], ALU.mult))
                    then(dve.tensor_scalar(cos[kind][:], cos[kind][:], -2.0, 1.0, ALU.mult, ALU.add))
                rope("rot_qi0", proj[:, QI0, :], R64)
                rope("rot_qi1", proj[:, QI0 + 1, :], R64)
                rope("rot_ki", proj[:, KI0, :], R64)
                dve.wait_ge(S["ln_sd"], 1)
                then(dve.reciprocal(sd[:], sd[:]))
                for t in range(TILES):
                    then(dve.tensor_scalar(vn[:, t, :], banks[t][:], mv[:, t, 0:1], sd[:, t:t + 1], ALU.subtract,
                                           ALU.mult))
                    then(dve.tensor_tensor(vn[:, t, :], vn[:, t, :], vg[:], ALU.mult))
                    dve.tensor_tensor(vn[:, t, :], vn[:, t, :], vb[:], ALU.add).then_inc(S["vnorm"], 1)
                for h in range(N_HEADS):
                    mean_square(f"sum_q{h}", P, 1 + h)
                    reciprocal_root(1 + h)
                    dve.scalar_tensor_tensor(proj[:, Q0 + h, :], proj[:, Q0 + h, :], gains[:, 2:3], rstd[:],
                                             ALU.mult, ALU.mult).then_inc(S["normed"], 1)
                    dve.wait_ge(S["normed"], h + 2)
                take("k")
                dve.tensor_copy(kT[:], bank("k")[:]).then_inc(took, 1)
                take("vv")
                dve.tensor_copy(vv[:].rearrange("p t n -> p (t n)"), bank("vv")[:]).then_inc(took, 1)
                mean_square("sum_k", P, 1 + N_HEADS)
                reciprocal_root(1 + N_HEADS)
                dve.scalar_tensor_tensor(kT[:], kT[:], gains[:, 3:4], rstd[:], ALU.mult, ALU.mult
                                         ).then_inc(S["normed"], 1)
                dve.wait_ge(S["normed"], N_HEADS + 2)
                for g in range(A_GROUPS):
                    take(f"z{g}")
                    dve.tensor_tensor(proj[:, U0 + g, :], proj[:, U0 + g, :], bank(f"z{g}")[:], ALU.mult
                                      ).then_inc(S["gated"], 1)
                    dve.wait_ge(S["gated"], g + 1)
                    dve.sem_inc(took, 1)
                for i, x in enumerate(QK):
                    rope(f"rot_{x}", kT[:] if x == "k" else proj[:, Q0 + i, :], R128)
                take("wi")
                dve.tensor_scalar(wi[:], bank("wi")[:].rearrange("p (t n) -> p t n", t=TILES)[:, :, 0:IDX_HEADS],
                                  float(IDX_HEADS) ** -0.5, None, ALU.mult).then_inc(took, 1)

            @block.tensor
            def _(pe):
                def start(x):
                    if NUM[x] >= 4:
                        pe.wait_ge(took, NUM[x] - 3)

                def finish(instruction):
                    instruction.then_inc(job, 1)

                pe.wait_ge(S["const"], 3)
                pe.wait_ge(S["gelu"], 1)
                for t in range(TILES):
                    for f in range(4):
                        last = pe.transpose(banks[t][:, f * P:(f + 1) * P], proj[:, V0 + f, t * P:(t + 1) * P],
                                            ident[:])
                    last.then_inc(S["vt"], 1)
                pe.wait_ge(small, 16 * len(SMALL))
                start("sum_c")
                pe.wait_ge(S["sq"], 2)
                for k in range(2):
                    last = pe.matmul(bank("sum_c")[:], ones[:], sq[:, k, :], start=k == 0, stop=k == 1)
                finish(last)
                for x, tile in (("rot_qi0", QI0), ("rot_qi1", QI0 + 1), ("rot_ki", KI0)):
                    start(x)
                    finish(pe.matmul(bank(x)[:], rot[:, R64, :], proj[:, tile, :], start=True, stop=True))
                for h in range(N_HEADS):
                    x = f"sum_q{h}"
                    start(x)
                    pe.wait_ge(S["sq"], 3 + h)
                    finish(pe.matmul(bank(x)[:], ones[:], sq[:, 2 + h, :], start=True, stop=True))
                pe.wait_ge(S["normed"], 1)
                start("k")
                for k in range(2):
                    last = pe.matmul(bank("k")[:], wuk[:, k, :], proj[:, C0 + k, :], start=k == 0, stop=k == 1)
                finish(last)
                start("vv")
                for t in range(TILES):
                    for k in range(2):
                        last = pe.matmul(bank("vv")[:, t * P:(t + 1) * P], proj[:, C0 + k, t * P:(t + 1) * P],
                                         wuv[:, k, :], start=k == 0, stop=k == 1)
                finish(last)
                start("sum_k")
                pe.wait_ge(S["sq"], 3 + N_HEADS)
                finish(pe.matmul(bank("sum_k")[:], ones[:], sq[:, 2 + N_HEADS, :], start=True, stop=True))
                pe.wait_ge(S["masked"], 1)
                pe.wait_ge(S["vnorm"], TILES)
                for g in range(A_GROUPS):
                    start(f"z{g}")
                    for t in range(TILES):
                        out = bank(f"z{g}")[:, t * P:(t + 1) * P]
                        pe.matmul(out, vn[:, t, g * P:(g + 1) * P], wsT[:, g, :], start=True, stop=False)
                        last = pe.matmul(out, ones[0:1, :], bs[:, g, :], start=False, stop=True)
                    finish(last)
                pe.wait_ge(S["normed"], 1 + N_HEADS)
                for h in range(N_HEADS):
                    start(f"rot_q{h}")
                    finish(pe.matmul(bank(f"rot_q{h}")[:], rot[:, R128, :], proj[:, Q0 + h, :], start=True,
                                     stop=True))
                start("rot_k")
                pe.wait_ge(S["normed"], N_HEADS + 2)
                finish(pe.matmul(bank("rot_k")[:], rot[:, R128, :], kT[:], start=True, stop=True))
                start("wi")
                for t in range(TILES):
                    last = pe.transpose(bank("wi")[:, t * P:(t + 1) * P], proj[:, WI0, t * P:(t + 1) * P], ident[:])
                finish(last)
    clear_semaphores(nc, S.values())


def select_keys(nc, proj, wi, select, w_gates, x_hi, x_lo, gates):
    with ExitStack() as ctx:
        c = Chip(nc, ctx)
        relu = c.sb("sel_relu", [P, 4, SEQ])
        score = c.sb("sel_score", [P, TILES, SEQ])
        best = c.sb("sel_best", [P, 8])
        banks = [c.ps(f"sel_bank{i}", [P, SEQ]) for i in range(4)]
        S = {x: c.sem(f"sel_{x}") for x in ("logits", "relu", "added", "scored", "causal", "seq")}
        units = [(t, h) for t in range(1, TILES) for h in range(IDX_HEADS)]
        stream = PanelStream(c, "gs", w_gates, x_hi, x_lo, gates, ACT.Sigmoid)
        with nc.Block() as block:
            block.sync(stream.sync)

            @block.tensor
            def _(pe):
                stream.start_tensor(pe)
                for n, (t, h) in enumerate(units):
                    if n >= 4:
                        pe.wait_ge(S["relu"], n - 3)
                    half = slice(IDX_DIM * (h % 2), IDX_DIM * (h % 2 + 1))
                    pe.matmul(banks[n % 4][:, :(t + 1) * P], proj[half, QI0 + h // 2, t * P:(t + 1) * P],
                              proj[half, KI0, :(t + 1) * P], start=True, stop=True).then_inc(S["logits"], 1)
                for k in range(stream.n):
                    stream.tensor(pe, 0, k)

            @block.scalar
            def _(act):
                for n, (t, h) in enumerate(units):
                    act.wait_ge(S["logits"], n + 1)
                    if n >= 4:
                        act.wait_ge(S["added"], n - 3)
                    act.activation(relu[:, n % 4, :(t + 1) * P], banks[n % 4][:, :(t + 1) * P], ACT.Relu,
                                   scale=float(IDX_DIM) ** -0.5).then_inc(S["relu"], 1)
                    if n == 5:
                        stream.start_high(act)
                for k in range(stream.n):
                    stream.scalar(act, 0, k, ends=True)

            @block.gpsimd
            def _(pool):
                stream.start_low(pool)
                pool.memset(select[:, 0, :P], 0.0).then_inc(S["causal"], 1)
                pool.wait_ge(S["causal"], 1)
                pool.affine_select(out=select[:, 0, :P], in_=select[:, 0, :P], compare_op=ALU.is_ge, fill=MASKED,
                                   base=0, pattern=[[-1, P]], channel_multiplier=1).then_inc(S["causal"], 1)
                for t in range(1, TILES):
                    pool.wait_ge(S["added"], IDX_HEADS * t)
                    diagonal = score[:, t, t * P:(t + 1) * P]
                    pool.affine_select(out=diagonal, in_=diagonal, compare_op=ALU.is_ge, fill=FUTURE, base=0,
                                       pattern=[[-1, P]], channel_multiplier=1).then_inc(S["causal"], 1)
                for k in range(stream.n):
                    stream.low(pool, 0, k)

            @block.vector
            def _(dve):
                done = [0]

                def then(instruction):
                    done[0] += 1
                    instruction.then_inc(S["seq"], 1)
                    dve.wait_ge(S["seq"], done[0])

                for n, (t, h) in enumerate(units):
                    w = (t + 1) * P
                    dve.wait_ge(S["relu"], n + 1)
                    if h == 0:
                        dve.tensor_scalar(score[:, t, :w], relu[:, n % 4, :w], wi[:, t, h:h + 1], None, ALU.mult
                                          ).then_inc(S["added"], 1)
                    else:
                        dve.wait_ge(S["added"], n)
                        dve.scalar_tensor_tensor(score[:, t, :w], relu[:, n % 4, :w], wi[:, t, h:h + 1],
                                                 score[:, t, :w], ALU.mult, ALU.add).then_inc(S["added"], 1)
                for t in range(1, TILES):
                    w = (t + 1) * P
                    dve.wait_ge(S["causal"], 2 + t)
                    for _ in range(TOPK // 8):
                        then(dve.max(best[:], score[:, t, :w]))
                        then(dve.match_replace(score[:, t, :w], best[:], score[:, t, :w], TAKEN))
                    dve.tensor_scalar(select[:, t, :w], score[:, t, :w], (TAKEN + FUTURE) / 2, MASKED, ALU.is_gt,
                                      ALU.mult).then_inc(S["scored"], 1)
    clear_semaphores(nc, [*S.values(), *stream.sems])


def turn_to_features(nc, name, tok, n, hi, lo, ident):
    with ExitStack() as ctx:
        c = Chip(nc, ctx)
        banks = [c.ps(f"{name}_bank{i}", [P, SEQ]) for i in range(4)]
        turned, high, low = (c.sem(f"{name}_{x}") for x in ("turned", "high", "low"))
        with nc.Block() as block:
            @block.tensor
            def _(pe):
                for f in range(n):
                    if f >= 4:
                        pe.wait_ge(low, f - 3)
                    for t in range(TILES):
                        last = pe.transpose(banks[f % 4][:, t * P:(t + 1) * P], tok[:, t, f * P:(f + 1) * P],
                                            ident[:])
                    last.then_inc(turned, 1)

            @block.scalar
            def _(act):
                for f in range(n):
                    act.wait_ge(turned, f + 1)
                    act.copy(hi[:, f, :], banks[f % 4][:]).then_inc(high, 1)

            @block.vector
            def _(dve):
                for f in range(n):
                    dve.wait_ge(high, f + 1)
                    dve.tensor_tensor(lo[:, f, :], banks[f % 4][:], hi[:, f, :].bitcast(F32), ALU.subtract
                                      ).then_inc(low, 1)
    clear_semaphores(nc, [turned, high, low])


def attend_selected(nc, proj, kT, vv, select, ident, yb_hi, yb_lo):
    with ExitStack() as outer:
        yb = Chip(nc, outer).sb("yb", [P, TILES, N_HEADS * P])
        with ExitStack() as ctx:
            c = Chip(nc, ctx)

            def unit(t, h):
                w = (t + 1) * P
                return dict(q=proj[:, Q0 + h, t * P:(t + 1) * P], k=kT[:, :w], width=w, bias=select[:, t, :w],
                            v=lambda b: vv[:, b, :], dv=P, gate=None, add=False,
                            out=yb[:, t, h * P:(h + 1) * P])
            att = Attention(c, "att1", [unit(t, h) for t in range(TILES) for h in range(N_HEADS)],
                            float(P) ** -0.5, ident)
            with nc.Block() as block:
                block.scalar(att.scalar)
                block.vector(att.vector)
                block.tensor(att.tensor)
            clear_semaphores(nc, att.sems)
        turn_to_features(nc, "yb_turn", yb, N_HEADS, yb_hi, yb_lo, ident)


def merge_branches(nc, w, gates, ya_hi, ya_lo, yb_hi, yb_lo, m_hi, m_lo):
    with ExitStack() as ctx:
        c = Chip(nc, ctx)
        R = 3
        raw = c.sb("mg_raw", [P, R, PANEL])
        hi = c.sb("mg_hi", [P, R, PANEL], F32R)
        lo = c.sb("mg_lo", [P, R, PANEL], F32R)
        gate = c.sb("mg_gate", [P, R, 2, SEQ])
        m = c.sb("mg_m", [P, 2, SEQ])
        pa, pb = ([c.ps(f"mg_{x}{i}", [P, SEQ]) for i in range(2)] for x in ("pa", "pb"))
        landed = [c.sem(f"mg_landed{i}") for i in range(R)]
        gate_landed = [c.sem(f"mg_gate_landed{i}") for i in range(R)]
        S = {x: c.sem(f"mg_{x}") for x in ("high", "split", "product", "a", "b", "merged", "m_high", "m_split")}
        with nc.Block() as block:
            @block.sync
            def _(sp):
                for n in range(KC):
                    if n >= R:
                        sp.wait_ge(S["split"], n - R + 1)
                    sp.dma_start(raw[:, n % R, :], w[n]).then_inc(landed[n % R], 16)
                    if n >= R:
                        sp.wait_ge(S["merged"], n - R + 1)
                    sp.dma_start(gate[:, n % R], gates[2 * n:2 * n + 2].rearrange("n p s -> p n s")
                                 ).then_inc(gate_landed[n % R], 16)

            @block.scalar
            def _(act):
                def high(n):
                    act.wait_ge(landed[n % R], 16 * (n // R + 1))
                    if n >= R:
                        act.wait_ge(S["product"], n - R + 1)
                    act.copy(hi[:, n % R, :], raw[:, n % R, :]).then_inc(S["high"], 1)

                high(0)
                high(1)
                for n in range(KC):
                    if n + 2 < KC:
                        high(n + 2)
                    act.wait_ge(S["merged"], n + 1)
                    act.copy(m_hi[:, n, :], m[:, n % 2, :]).then_inc(S["m_high"], 1)

            @block.gpsimd
            def _(pool):
                for n in range(KC):
                    pool.wait_ge(S["high"], n + 1)
                    pool.tensor_tensor(lo[:, n % R, :], raw[:, n % R, :], hi[:, n % R, :].bitcast(F32),
                                       ALU.subtract).then_inc(S["split"], 1)

            @block.vector
            def _(dve):
                for n in range(KC):
                    now = gate[:, n % R]
                    dve.wait_ge(S["product"], n + 1)
                    dve.wait_ge(gate_landed[n % R], 16 * (n // R + 1))
                    dve.tensor_tensor(now[:, 0, :], now[:, 0, :], pa[n % 2][:], ALU.mult).then_inc(S["a"], 1)
                    dve.tensor_tensor(now[:, 1, :], now[:, 1, :], pb[n % 2][:], ALU.mult).then_inc(S["b"], 1)
                    dve.wait_ge(S["a"], n + 1)
                    dve.wait_ge(S["b"], n + 1)
                    if n >= 2:
                        dve.wait_ge(S["m_split"], n - 1)
                    dve.tensor_tensor(m[:, n % 2, :], now[:, 0, :], now[:, 1, :], ALU.add
                                      ).then_inc(S["merged"], 1)
                    dve.wait_ge(S["m_high"], n + 1)
                    dve.tensor_tensor(m_lo[:, n, :], m[:, n % 2, :], m_hi[:, n, :].bitcast(F32), ALU.subtract
                                      ).then_inc(S["m_split"], 1)

            @block.tensor
            def _(pe):
                for n in range(KC):
                    if n >= 2:
                        pe.wait_ge(S["merged"], n - 1)
                    pe.wait_ge(S["split"], n + 1)
                    for out, y_hi, y_lo, at in ((pa[n % 2], ya_hi, ya_lo, 0), (pb[n % 2], yb_hi, yb_lo, 4)):
                        for i in range(4):
                            cols = slice((at + i) * P, (at + i + 1) * P)
                            last = three_products(pe, out[:], hi[:, n % R, cols], lo[:, n % R, cols],
                                                  y_hi[:, i, :], y_lo[:, i, :], i == 0, i == 3)
                    last.then_inc(S["product"], 1)
    clear_semaphores(nc, [*landed, *gate_landed, *S.values()])


def first_mixer(nc, hT, x_hi, x_lo, d):
    with ExitStack() as ctx:
        c = Chip(nc, ctx)
        ya_hi, ya_lo, yb_hi, yb_lo = (c.sb(x, [P, 4, SEQ], F32R) for x in ("ya_hi", "ya_lo", "yb_hi", "yb_lo"))
        with ExitStack() as inner:
            c = Chip(nc, inner)
            proj = c.sb("m1_proj", [P, N_PROJ1, SEQ])
            norm_and_project(nc, "p1", hT, x_hi, x_lo, d["norm1_g"], d["w_in1"], proj)
            kT = c.sb("m1_kT", [P, SEQ])
            vv = c.sb("m1_vv", [P, TILES, P])
            wi = c.sb("m1_wi", [P, TILES, IDX_HEADS])
            ident = c.sb("m1_ident", [P, P])
            gate_and_prepare(nc, proj, kT, vv, wi, ident, ya_hi, ya_lo, d)
            select = c.sb("m1_select", [P, TILES, SEQ])
            select_keys(nc, proj, wi, select, d["w_gates"], x_hi, x_lo, d["gates"])
            attend_selected(nc, proj, kT, vv, select, ident, yb_hi, yb_lo)
        m_hi, m_lo = (Chip(nc, ctx).sb(x, [P, KC, SEQ], F32R) for x in ("m_hi", "m_lo"))
        merge_branches(nc, d["w_merge"], d["gates"], ya_hi, ya_lo, yb_hi, yb_lo, m_hi, m_lo)
        project_onto(nc, "wo", m_hi, m_lo, d["w_o"], hT)



PEER_HEADS = 8
N_KEYS = 128
PEER_TOPK = 16
HALVES = 2 * PEER_HEADS
SLOTS = PEER_HEADS * PEER_TOPK


EARLY_CHUNKS = (40, 40)


def route_tokens(nc, qT, subkeys, iota, rowT, colT, gateT, up_w, x_hi, x_lo, hidden):
    units = hidden.shape[0]
    with ExitStack() as ctx:
        c = Chip(nc, ctx)
        keys = c.sb("rt_keys", [P, HALVES, N_KEYS])
        ident = c.sb("rt_ident", [P, P])
        sub = c.sb("rt_sub", [P, 2, HALVES, N_KEYS])
        rest = c.sb("rt_rest", [P, HALVES, N_KEYS])
        top = c.sb("rt_top", [P, HALVES, PEER_TOPK])
        index = c.sb("rt_index", [P, HALVES, PEER_TOPK], U32)
        indexf = c.sb("rt_indexf", [P, HALVES, PEER_TOPK])
        cand = c.sb("rt_cand", [P, PEER_HEADS, PEER_TOPK, PEER_TOPK])
        cand_rest = c.sb("rt_cand_rest", [P, PEER_HEADS, PEER_TOPK * PEER_TOPK])
        best = c.sb("rt_best", [P, PEER_HEADS, PEER_TOPK])
        place = c.sb("rt_place", [P, PEER_HEADS, PEER_TOPK], U32)
        half = c.sb("rt_half", [P, 2, PEER_HEADS, PEER_TOPK], U32)
        halff = c.sb("rt_halff", [P, 2, PEER_HEADS, PEER_TOPK])
        found = c.sb("rt_found", [P, PEER_HEADS, PEER_TOPK, PEER_TOPK])
        result = c.sb("rt_result", [P, 3, PEER_HEADS, PEER_TOPK])
        total = c.sb("rt_total", [P, PEER_HEADS])
        banks = [c.ps(f"rt_bank{i}", [P, SEQ]) for i in range(4)]
        out_ps = c.ps("rt_out", [P, SEQ])
        stream = PanelStream(c, "rs", up_w, x_hi, x_lo, hidden, ACT.Gelu_apprx_tanh)
        share = units // TILES
        EXPS_AT, TURN_AT = share // 4, share * 2 // 3
        S = {x: c.sem(f"rt_{x}") for x in ("keys", "const", "scored", "copied", "searched", "seq", "shifted",
                                           "exped", "resulted", "turned", "stored")}
        with nc.Block() as block:
            @block.sync
            def _(sp):
                sp.dma_start(keys[:], subkeys).then_inc(S["keys"], 16)
                stream.sync(sp)

            @block.gpsimd
            def _(pool):
                stream.start_low(pool)
                pool.memset(ident[:], 0.0).then_inc(S["const"], 1)
                pool.wait_ge(S["const"], 1)
                pool.affine_select(out=ident[:], in_=ident[:], compare_op=ALU.not_equal, fill=1.0, base=0,
                                   pattern=[[-1, P]], channel_multiplier=1).then_inc(S["const"], 1)
                pool.iota(iota[:], pattern=[[1, N_KEYS]], base=0, channel_multiplier=0,
                          allow_small_or_imprecise_dtypes=True).then_inc(S["const"], 1)
                for n in range(units):
                    stream.low(pool, 0, n)

            @block.tensor
            def _(pe):
                pe.wait_ge(S["keys"], 16)
                pe.wait_ge(S["const"], 2)

                def turn(t):
                    pe.wait_ge(S["resulted"], t + 1)
                    if t >= 1:
                        pe.wait_ge(S["stored"], t)
                    for i in range(3):
                        last = pe.transpose(out_ps[:, i * P:(i + 1) * P],
                                            result[:, i].rearrange("p h k -> p (h k)"), ident[:])
                    last.then_inc(S["turned"], 1)

                def score(t):
                    for i in range(HALVES):
                        if i % 4 == 0 and t >= 1:
                            pe.wait_ge(S["copied"], 4 * (t - 1) + i // 4 + 1)
                        last = pe.matmul(banks[i // 4][:, (i % 4) * P:(i % 4 + 1) * P],
                                         qT[:, i, t * P:(t + 1) * P], keys[:, i, :], start=True, stop=True)
                        if i % 4 == 3:
                            last.then_inc(S["scored"], 1)

                stream.start_tensor(pe)
                score(0)
                for t in range(TILES):
                    if t + 1 < TILES:
                        score(t + 1)
                    for n in range(share):
                        if t >= 1 and n == TURN_AT:
                            turn(t - 1)
                        if t == TILES - 1 and n == share - 1:
                            turn(t)
                        stream.tensor(pe, 0, t * share + n)

            @block.scalar
            def _(act):
                def copy_scores(t):
                    for b in range(4):
                        act.wait_ge(S["scored"], 4 * t + b + 1)
                        if t >= 2:
                            act.wait_ge(S["searched"], t - 1)
                        act.copy(sub[:, t % 2, 4 * b:4 * b + 4, :].rearrange("p i n -> p (i n)"), banks[b][:]
                                 ).then_inc(S["copied"], 1)

                def exps(t):
                    act.wait_ge(S["shifted"], t + 1)
                    act.activation(result[:, 2], result[:, 2], ACT.Exp).then_inc(S["exped"], 1)

                copy_scores(0)
                stream.start_high(act)
                for t in range(TILES):
                    if t + 1 < TILES:
                        copy_scores(t + 1)
                    for n in range(share):
                        if t >= 1 and n == EXPS_AT:
                            exps(t - 1)
                        if t == TILES - 1 and n == share - 3:
                            exps(t)
                        stream.scalar(act, 0, t * share + n, ends=t == TILES - 1)

            @block.vector
            def _(dve):
                done = [0]

                def all_of(instructions):
                    for instruction in instructions:
                        done[0] += 1
                        instruction.then_inc(S["seq"], 1)
                    dve.wait_ge(S["seq"], done[0])

                def top16(n, scores, left, values, places):
                    all_of(dve.max(values(i)[:, 0:8], scores(i)) for i in range(n))
                    all_of(dve.match_replace(left(i), values(i)[:, 0:8], scores(i), TAKEN) for i in range(n))
                    all_of(dve.max(values(i)[:, 8:16], left(i)) for i in range(n))
                    all_of(dve.max_index(places(i)[:, 0:8], values(i)[:, 0:8], scores(i)) for i in range(n))
                    all_of(dve.max_index(places(i)[:, 8:16], values(i)[:, 8:16], left(i)) for i in range(n))

                def finish(t):
                    dve.wait_ge(S["exped"], t + 1)
                    all_of([dve.tensor_reduce(total[:], result[:, 2], AX.X, ALU.add)])
                    all_of([dve.reciprocal(total[:], total[:])])
                    dve.tensor_tensor(result[:, 2], result[:, 2], total[:].unsqueeze(2).broadcast_to(small),
                                      ALU.mult).then_inc(S["resulted"], 1)

                def keep(t):
                    dve.wait_ge(S["turned"], t + 1)
                    cols = slice(t * P, (t + 1) * P)
                    for i, to in enumerate((rowT, colT, gateT)):
                        last = dve.tensor_copy(to[:, cols], out_ps[:, i * P:(i + 1) * P])
                        if i < 2:
                            all_of([last])
                    last.then_inc(S["stored"], 1)

                small = [P, PEER_HEADS, PEER_TOPK]
                dve.wait_ge(S["const"], 3)
                for t in range(TILES):
                    dve.wait_ge(S["copied"], 4 * t + 4)
                    top16(HALVES, lambda i: sub[:, t % 2, i, :], lambda i: rest[:, i, :], lambda i: top[:, i, :],
                          lambda i: index[:, i, :])
                    all_of([dve.tensor_copy(indexf[:], index[:])])
                    by_half = top[:].rearrange("p (h two) k -> p h two k", two=2)
                    dve.sem_inc(S["searched"], 1)
                    if t >= 1:
                        finish(t - 1)
                    shape = [P, PEER_HEADS, PEER_TOPK, PEER_TOPK]
                    all_of([dve.tensor_tensor(cand[:], by_half[:, :, 0, :].unsqueeze(3).broadcast_to(shape),
                                              by_half[:, :, 1, :].unsqueeze(2).broadcast_to(shape), ALU.add)])
                    flat = cand[:].rearrange("p h a b -> p h (a b)")
                    top16(PEER_HEADS, lambda i: flat[:, i, :], lambda i: cand_rest[:, i, :],
                          lambda i: best[:, i, :], lambda i: place[:, i, :])
                    all_of([dve.tensor_scalar(half[:, 0], place[:], 4, None, ALU.logical_shift_right),
                            dve.tensor_scalar(half[:, 1], place[:], 15, None, ALU.bitwise_and)])
                    all_of([dve.tensor_copy(halff[:], half[:])])
                    ranks = iota[:, 0:PEER_TOPK].unsqueeze(1).unsqueeze(1).broadcast_to(shape)
                    keys_of = indexf[:].rearrange("p (h two) k -> p h two k", two=2)
                    if t >= 1:
                        keep(t - 1)
                    for side in range(2):
                        all_of([dve.tensor_tensor(found[:], halff[:, side].unsqueeze(3).broadcast_to(shape),
                                                  ranks, ALU.is_equal)])
                        all_of([dve.tensor_tensor(found[:], found[:],
                                                  keys_of[:, :, side, :].unsqueeze(2).broadcast_to(shape),
                                                  ALU.mult)])
                        all_of([dve.tensor_reduce(result[:, side], found[:], AX.X, ALU.add)])
                    dve.tensor_tensor(result[:, 2], best[:], best[:, :, 0:1].broadcast_to(small), ALU.subtract
                                      ).then_inc(S["shifted"], 1)
                finish(TILES - 1)
                keep(TILES - 1)
                dve.wait_ge(S["stored"], TILES)
    clear_semaphores(nc, [*S.values(), *stream.sems])


def build_routing(nc, iota, rowT, colT, gateT, routing, up_w, x_hi, x_lo, hidden):
    B = 8
    BLOCK = TOKENS
    TAIL = 2 * RING
    steps = BLOCK // B
    n_blocks = SEQ // BLOCK
    units = (hidden.shape[0] - TAIL) // n_blocks
    every = steps // units
    with ExitStack() as ctx:
        c = Chip(nc, ctx)
        hot = c.sb("br_hot", [P, 2, B, N_KEYS])
        row_hot = c.sb("br_row", [P, 2, B, N_KEYS])
        col_hot = c.sb("br_col", [P, 2, B, N_KEYS])
        block_out = c.sb("br_out", [P, 2, N_KEYS, BLOCK])
        banks = [c.ps(f"br_bank{i}", [P, 4, N_KEYS]) for i in range(4)]
        stream = PanelStream(c, "bs", up_w, x_hi, x_lo, hidden, ACT.Gelu_apprx_tanh)
        S = {x: c.sem(f"br_{x}") for x in ("hot", "rows", "cols", "product", "taken", "stored0", "stored1")}
        stored = [S["stored0"], S["stored1"]]
        shape = [P, B, N_KEYS]
        keys = iota[:].unsqueeze(1).broadcast_to(shape)
        with nc.Block() as block:
            def both(eng, body, unit=None):
                with eng.Fori(0, n_blocks // 2) as b2:
                    for o in range(2):
                        for step in range(steps):
                            if unit is not None and step % every == 0:
                                unit(b2 * (2 * units // RING), o * units + step // every, False)
                            body(b2, o, step, b2 * (2 * steps) + (o * steps + step), step % 2)
                if unit is not None:
                    for k in range(TAIL):
                        unit(n_blocks * units // RING, k, True)

            @block.vector
            def _(dve):
                def body(b2, o, step, n, k):
                    at = bass.ds(n * B, B)
                    dve.wait_ge(S["rows"], n + 1)
                    dve.tensor_tensor(hot[:, k], keys, rowT[:, at].unsqueeze(2).broadcast_to(shape),
                                      ALU.is_equal).then_inc(S["hot"], 1)
                    dve.wait_ge(S["product"], n + 1)
                    dve.tensor_tensor(col_hot[:, k], keys, colT[:, at].unsqueeze(2).broadcast_to(shape),
                                      ALU.is_equal).then_inc(S["cols"], 1)
                both(dve, body)

            @block.gpsimd
            def _(pool):
                pool.sem_inc(S["rows"], 2)
                stream.start_low(pool)

                def body(b2, o, step, n, k):
                    pool.wait_ge(S["hot"], n + 1)
                    pool.wait_ge(S["product"], n + 1)
                    pool.tensor_tensor(row_hot[:, k], hot[:, k],
                                       gateT[:, bass.ds(n * B, B)].unsqueeze(2).broadcast_to(shape), ALU.mult
                                       ).then_inc(S["rows"], 1)
                both(pool, body, lambda g, k, ends: stream.low(pool, g, k))

            @block.tensor
            def _(pe):
                pe.sem_inc(S["product"], 2)
                stream.start_tensor(pe)

                def body(b2, o, step, n, k):
                    pe.wait_ge(S["rows"], n + 1 + 2)
                    pe.wait_ge(S["cols"], n + 1)
                    pe.wait_ge(S["taken"], n + 1)
                    for b in range(B):
                        last = pe.matmul(banks[2 * k + b // 4][:, b % 4, :], row_hot[:, k, b, :],
                                         col_hot[:, k, b, :], start=True, stop=True)
                    last.then_inc(S["product"], 1)
                both(pe, body, lambda g, k, ends: stream.tensor(pe, g, k))

            @block.scalar
            def _(act):
                act.sem_inc(S["taken"], 2)
                for o in range(2):
                    act.sem_inc(stored[o], 16)
                stream.start_high(act)

                def body(b2, o, step, n, k):
                    act.wait_ge(S["product"], n + 1 + 2)
                    act.wait_ge(stored[o], b2 * 16 + 16)
                    for i in range(2):
                        at = step * B + 4 * i
                        last = act.copy(block_out[:, o, :, at:at + 4].rearrange("p n b -> p b n"),
                                        banks[2 * k + i][:])
                    last.then_inc(S["taken"], 1)
                    if step == steps - 1:
                        act.wait_ge(S["taken"], n + 1 + 2)
                        act.dma_start(routing[bass.ds(b2 * 2 + o, 1)].rearrange("o i j s -> i (o j s)"),
                                      block_out[:, o].rearrange("p j s -> p (j s)")).then_inc(stored[o], 16)
                both(act, body, lambda g, k, ends: stream.scalar(act, g, k, ends))
                for o in range(2):
                    act.wait_ge(stored[o], 16 + 16 * (n_blocks // 2))

            @block.sync
            def _(sp):
                stream.sync(sp)
    clear_semaphores(nc, [*S.values(), *stream.sems])


def add_chunks(nc, name, hT, hidden, routing, down_w):
    J = 4
    n_groups = hidden.shape[0] // J
    with ExitStack() as ctx:
        c = Chip(nc, ctx)
        b_raw = c.sb(f"{name}_b_raw", [P, J, D])
        b_hi = c.sb(f"{name}_b_hi", [P, 2 * J, D], F32R)
        b_lo = c.sb(f"{name}_b_lo", [P, 2 * J, D], F32R)
        g_hi = c.sb(f"{name}_g_hi", [P, 2 * J, SEQ], F32R)
        g_lo = c.sb(f"{name}_g_lo", [P, 2 * J, SEQ], F32R)
        unit = c.sb(f"{name}_unit", [P, J, SEQ])
        route = c.sb(f"{name}_route", [P, SEQ // TOKENS, J * TOKENS])
        prod = c.sb(f"{name}_prod", [P, 2, SEQ])
        y_ps = [c.ps(f"{name}_y{f}", [P, SEQ]) for f in range(KC)]
        b_landed = [c.sem(f"{name}_b_landed{s}") for s in range(J)]
        h_landed = [c.sem(f"{name}_h_landed{s}") for s in range(J)]
        r_landed = c.sem(f"{name}_r_landed")
        b_high, b_split, prod_done, hid_high, hid_split, y_done, y_added = named = [
            c.sem(f"{name}_{x}") for x in ("b_high", "b_split", "prod_done", "hid_high", "hid_split", "y_done",
                                           "y_added")]

        def pairs(eng, body):
            with eng.Fori(0, n_groups // 2 - 1) as p:
                for half in range(2):
                    body(p, half, False)
            for half in range(2):
                body(n_groups // 2 - 1, half, half == 1)

        with nc.Block() as block:
            @block.sync
            def _(sp):
                def body(p, half, ends):
                    for j in range(J):
                        n = p * (2 * J) + (half * J + j)
                        sp.wait_ge(prod_done, n + 1)
                        sp.dma_start(unit[:, j, :], hidden[bass.ds(n, 1)].rearrange("o p f -> p (o f)")
                                     ).then_inc(h_landed[j], 16)
                    first = p * (2 * J) + half * J
                    sp.wait_ge(prod_done, first + J)
                    sp.dma_start(route[:], routing_of(routing, first, J)).then_inc(r_landed, 16)
                    for j in range(J):
                        n = p * (2 * J) + (half * J + j)
                        sp.wait_ge(b_split, n + 1)
                        sp.dma_start(b_raw[:, j, :], down_w(n)).then_inc(b_landed[j], 16)
                pairs(sp, body)

            @block.scalar
            def _(act):
                def body(p, half, ends):
                    for j in range(J):
                        i = half * J + j
                        act.wait_ge(y_done, p * (2 * KC) + (half + 1) * KC)
                        act.wait_ge(prod_done, p * (2 * J) + (i + 1 + J))
                        act.copy(g_hi[:, i, :], prod[:, j % 2, :]).then_inc(hid_high, 1)
                        act.wait_ge(b_landed[j], p * 32 + (16 * half + 16))
                        act.copy(b_hi[:, i, :], b_raw[:, j, :]).then_inc(b_high, 1)
                pairs(act, body)

            @block.gpsimd
            def _(pool):
                pool.sem_inc(b_split, J)

                def body(p, half, ends):
                    for j in range(J):
                        i = half * J + j
                        pool.wait_ge(b_high, p * (2 * J) + (i + 1))
                        pool.tensor_tensor(b_lo[:, i, :], b_raw[:, j, :], b_hi[:, i, :].bitcast(F32),
                                           ALU.subtract).then_inc(b_split, 1)
                pairs(pool, body)

            @block.vector
            def _(dve):
                dve.sem_inc(prod_done, J)
                dve.sem_inc(hid_split, 2)
                dve.sem_inc(y_added, KC)

                def one_unit(p, i):
                    n, s, j = p * (2 * J) + i, i % (2 * J), i % J
                    dve.wait_ge(h_landed[j], p * 32 + 16 * (i // J + 1))
                    dve.wait_ge(r_landed, p * 32 + 16 * (i // J + 1))
                    dve.wait_ge(hid_split, n + 1)
                    dve.tensor_tensor(in_blocks(prod[:, j % 2, :]), in_blocks(unit[:, j, :]),
                                      route[:, :, j * TOKENS:(j + 1) * TOKENS], ALU.mult).then_inc(prod_done, 1)
                    dve.wait_ge(hid_high, n + 1)
                    dve.tensor_tensor(g_lo[:, s, :], prod[:, j % 2, :], g_hi[:, s, :].bitcast(F32),
                                      ALU.subtract).then_inc(hid_split, 1)

                for j in range(J):
                    one_unit(0, j)

                def body(p, half, ends):
                    for f in range(KC):
                        dve.wait_ge(y_done, p * (2 * KC) + (half * KC + f + 1 + 2 * KC))
                        dve.tensor_tensor(hT[:, f, :], hT[:, f, :], y_ps[f][:], ALU.add).then_inc(y_added, 1)
                        if f < J and not ends:
                            one_unit(p, (half + 1) * J + f)
                pairs(dve, body)

            @block.tensor
            def _(pe):
                pe.sem_inc(y_done, 2 * KC)

                def body(p, half, ends):
                    for f in range(KC):
                        pe.wait_ge(y_added, p * (2 * KC) + (half * KC + f + 1))
                        for j in range(J):
                            i = half * J + j
                            if f == 0:
                                pe.wait_ge(b_split, p * (2 * J) + (i + 1 + J))
                                pe.wait_ge(hid_split, p * (2 * J) + (i + 1 + 2))
                            cols = slice(f * P, (f + 1) * P)
                            last = three_products(pe, y_ps[f][:], b_hi[:, i, cols], b_lo[:, i, cols],
                                                  g_hi[:, i, :], g_lo[:, i, :], j == 0, j == J - 1)
                        last.then_inc(y_done, 1)
                pairs(pe, body)
    clear_semaphores(nc, [*b_landed, *h_landed, r_landed, *named])


def experts(nc, hT, x_hi, x_lo, d, routing, hidden):
    searching, building = EARLY_CHUNKS
    early = searching + building
    up_w = d["peer_u"]
    with ExitStack() as ctx:
        c = Chip(nc, ctx)
        iota = c.sb("ex_iota", [P, N_KEYS])
        rowT, colT, gateT = (c.sb(f"ex_{x}", [P, SEQ]) for x in ("rowT", "colT", "gateT"))
        with ExitStack() as inner:
            qT = Chip(nc, inner).sb("ex_qT", [P, HALVES, SEQ])
            norm_and_project(nc, "pq", hT, x_hi, x_lo, d["norm2_g"], d["peer_wq"], qT)
            route_tokens(nc, qT, d["subkeys"], iota, rowT, colT, gateT, up_w[0:searching], x_hi, x_lo,
                         hidden[0:searching])
        build_routing(nc, iota, rowT, colT, gateT, routing, up_w[searching:early], x_hi, x_lo,
                      hidden[searching:early])
    rows = d["peer_v"].rearrange("(i j) f -> i j f", j=N_KEYS)

    def down(start):
        return lambda n: rows[:, bass.ds(start + n, 1), :].rearrange("i o f -> i (o f)")
    add_chunks(nc, "early", hT, hidden, routing, down(0))
    hidden_stage(nc, "peer", hT, x_hi, x_lo, up_w[early:], down(early), routing=routing, column=early)



NSA_HEADS = 8
NSA_GROUPS = 2
NSA_HD = 64
CMP_LEN = 32
CMP_STRIDE = 16
CMP_HID = 256
CMP_BLOCKS = (SEQ - CMP_LEN) // CMP_STRIDE + 1
HG_HEADS = 4
CHUNK = 16
N_CHUNKS = SEQ // CHUNK
F_FLOOR = 1e-30
PITCH = P + CHUNK

NQ0, KCMP, VCMP, KSEL, VSEL, KWIN, VWIN, GL = 0, 4, 5, 6, 7, 8, 9, 10
N_PROJ2 = 11


def compress_and_attend(nc, proj, ident, w1k, w1_landed, vsel, vwin, gates, bias, o_tok, d):
    scale = float(NSA_HD) ** -0.5
    slopes = [2.0 ** (-8.0 * (h + 1) / NSA_HEADS) / scale for h in range(NSA_HEADS)]
    NB = CMP_BLOCKS
    BOTH = NSA_GROUPS * NB
    with ExitStack() as ctx:
        c = Chip(nc, ctx)
        w1v = c.sb("cp_w1v", [P, CMP_LEN, CMP_HID])
        w2k = c.sb("cp_w2k", [P, 2, 3 * NSA_HD])
        w2v = c.sb("cp_w2v", [P, 2, NSA_HD])
        pos = c.sb("cp_pos", [P, 2, CMP_LEN])
        blocks = c.sb("cp_blocks", [P, 2, CMP_LEN, NSA_GROUPS, NB])
        hidden_rows = c.sb("cp_hidden_rows", [BOTH, 2 * CMP_HID])
        hidden = c.sb("cp_hidden", [P, 2, 2, NSA_GROUPS, NB])
        kcT = c.sb("cp_kcT", [P, NB])
        vc = c.sb("cp_vc", [NB, NSA_GROUPS * NSA_HD])
        cbias = c.sb("cp_cbias", [P, NSA_HEADS, TILES, NB])
        away = c.sb("cp_away", [P, TILES, NB])
        far = bias[:, NSA_HEADS - 1]
        s = c.sb("cp_s", [P, 2, NSA_HEADS, NB])
        top = c.sb("cp_top", [P, NSA_HEADS])
        total = c.sb("cp_total", [P, NSA_HEADS])
        pT = c.sb("cp_pT", [NB, NSA_HEADS, P])
        small_ps = c.ps("cp_small", [P, SEQ])
        turn_ps = [c.ps(f"cp_turn{i}", [P, SEQ]) for i in range(2)]
        o_ps = c.ps("cp_ops", [P, SEQ])
        pT_ps = [c.ps(f"cp_pTps{i}", [P, SEQ]) for i in range(2)]
        s_ps = [turn_ps, [c.ps(f"cp_s{i}", [P, SEQ]) for i in range(2)]]
        S = {x: c.sem(f"cp_{x}") for x in (
            "w", "w1v", "hturned", "hidden", "cleared", "const", "biases", "turned", "copied", "gates", "gated", "blocks", "hid", "gelu", "kc", "kcopied",
            "scored", "seq", "shifted", "exped", "weights", "pturned", "pcopied", "out", "stored")}
        n_small = 3
        with nc.Block() as block:
            @block.sync
            def _(sp):
                sp.dma_start(pos[:], d["cmp_pos"]).then_inc(S["w"], 16)
                sp.dma_start(w2k[:, :, NSA_HD:2 * NSA_HD], d["cmp_w2"][:, 0]).then_inc(S["w"], 16)
                sp.dma_start(w2v[:], d["cmp_w2"][:, 1]).then_inc(S["w"], 16)
                sp.dma_start(w1v[:], d["cmp_w1"][1]).then_inc(S["w1v"], 16)
                sp.wait_ge(S["w1v"], 16)

            @block.gpsimd
            def _(pool):
                pool.memset(blocks[:], 0.0).then_inc(S["cleared"], 1)
                pool.memset(ident[:], 0.0).then_inc(S["const"], 1)
                pool.memset(w2k[:, :, 0:NSA_HD], 0.0).then_inc(S["const"], 1)
                pool.memset(w2k[:, :, 2 * NSA_HD:], 0.0).then_inc(S["const"], 1)
                pool.wait_ge(S["const"], 3)
                pool.affine_select(out=ident[:], in_=ident[:], compare_op=ALU.not_equal, fill=1.0, base=0,
                                   pattern=[[-1, P]], channel_multiplier=1).then_inc(S["const"], 1)
                pool.iota(away[:], pattern=[[-P, TILES], [CMP_STRIDE, NB]], base=CMP_LEN - 1,
                          channel_multiplier=-1, allow_small_or_imprecise_dtypes=True).then_inc(S["const"], 1)
                pool.iota(far, pattern=[[1, 7 * P]], base=-3 * P, channel_multiplier=-1,
                          allow_small_or_imprecise_dtypes=True).then_inc(S["const"], 1)
                pool.wait_ge(S["const"], 6)
                for h in range(NSA_HEADS):
                    pool.tensor_scalar(cbias[:, h], away[:], slopes[h], None, ALU.mult).then_inc(S["const"], 1)
                pool.wait_ge(S["const"], 6 + NSA_HEADS)
                pool.affine_select(out=cbias[:], in_=cbias[:], compare_op=ALU.is_ge, fill=MASKED,
                                   base=1 - CMP_LEN, pattern=[[0, NSA_HEADS], [P, TILES], [-CMP_STRIDE, NB]],
                                   channel_multiplier=1).then_inc(S["biases"], 1)
                pool.wait_ge(S["gates"], TILES)
                first = gates[:, 0, 0:3 * NSA_HEADS:3]
                pool.affine_select(out=first, in_=first, compare_op=ALU.is_ge, fill=0.0, base=1 - CMP_LEN,
                                   pattern=[[0, NSA_HEADS]], channel_multiplier=1).then_inc(S["gated"], 1)
                for h in range(NSA_HEADS):
                    if h == NSA_HEADS - 1:
                        pool.wait_ge(S["const"], 6 + 2 * NSA_HEADS - 1)
                    pool.tensor_scalar(bias[:, h], far, slopes[h], None, ALU.mult).then_inc(S["const"], 1)
                pool.wait_ge(S["const"], 6 + 2 * NSA_HEADS)
                pool.affine_select(out=bias[:], in_=bias[:], compare_op=ALU.is_ge, fill=MASKED, base=3 * P,
                                   pattern=[[0, NSA_HEADS], [-1, 7 * P]], channel_multiplier=1
                                   ).then_inc(S["biases"], 1)

            @block.tensor
            def _(pe):
                pe.wait_ge(S["const"], 4)
                n = 0
                for t in range(TILES):
                    if n >= 2:
                        pe.wait_ge(S["copied"], n - 1)
                    for i, tile in enumerate((VSEL, VWIN, GL)):
                        last = pe.transpose(turn_ps[n % 2][:, i * P:(i + 1) * P], proj[:, tile, t * P:(t + 1) * P],
                                            ident[:])
                    last.then_inc(S["turned"], 1)
                    n += 1
                pe.wait_ge(S["w"], 16 * n_small)
                pe.wait_ge(w1_landed, 16)
                pe.wait_ge(S["blocks"], 8)
                for kv, w1 in enumerate((w1k, w1v)):
                    if kv:
                        pe.wait_ge(S["w1v"], 16)
                    for l in range(CMP_LEN):
                        last = pe.matmul(pT_ps[0][:BOTH, kv * CMP_HID:(kv + 1) * CMP_HID],
                                         blocks[:, kv, l].rearrange("p g n -> p (g n)"), w1[:, l, :], start=l == 0,
                                         stop=l == CMP_LEN - 1)
                last.then_inc(S["hid"], 1)
                pe.wait_ge(S["gelu"], 1)
                for i in range(4):
                    last = pe.transpose(pT_ps[1][:, i * BOTH:(i + 1) * BOTH], hidden_rows[:, i * P:(i + 1) * P],
                                        ident[:BOTH, :BOTH])
                last.then_inc(S["hturned"], 1)
                pe.wait_ge(S["hidden"], 1)
                for g in range(NSA_GROUPS):
                    for i in range(2):
                        at = NSA_HD * (1 - g)
                        last = pe.matmul(small_ps[:, 0:NB], w2k[:, i, at:at + P], hidden[:, 0, i, g, :],
                                         start=g == 0 and i == 0, stop=g == 1 and i == 1)
                for g in range(NSA_GROUPS):
                    for i in range(2):
                        last = pe.matmul(small_ps[0:NB, P + g * NSA_HD:P + (g + 1) * NSA_HD], hidden[:, 1, i, g, :],
                                         w2v[:, i, :], start=i == 0, stop=i == 1)
                last.then_inc(S["kc"], 1)
                pe.wait_ge(S["kcopied"], 2)
                pe.wait_ge(S["copied"], TILES)

                def score(t):
                    if t >= 2:
                        pe.wait_ge(S["shifted"], t - 1)
                    for h in range(NSA_HEADS):
                        part = slice(h // 4 * NSA_HD, (h // 4 + 1) * NSA_HD)
                        last = pe.matmul(s_ps[t % 2][h // 4][:, h % 4 * NB:(h % 4 + 1) * NB],
                                         proj[part, NQ0 + h % 4, t * P:(t + 1) * P], kcT[part, :], start=True,
                                         stop=True)
                    last.then_inc(S["scored"], 1)

                score(0)
                for t in range(TILES):
                    if t + 1 < TILES:
                        score(t + 1)
                    pe.wait_ge(S["weights"], t + 1)
                    if t >= 1:
                        pe.wait_ge(S["pcopied"], 2 * t)
                    for h in range(NSA_HEADS):
                        last = pe.transpose(pT_ps[h // 4][0:NB, (h % 4) * P:(h % 4 + 1) * P], s[:, t % 2, h, :],
                                            ident[:])
                    last.then_inc(S["pturned"], 1)
                    pe.wait_ge(S["pcopied"], 2 * t + 2)
                    if t >= 1:
                        pe.wait_ge(S["stored"], t)
                    for h in range(NSA_HEADS):
                        g = h // 4
                        last = pe.matmul(o_ps[:, h * NSA_HD:(h + 1) * NSA_HD], pT[:, h, :],
                                         vc[:, g * NSA_HD:(g + 1) * NSA_HD], start=True, stop=True)
                    last.then_inc(S["out"], 1)

            @block.scalar
            def _(act):
                for t in range(TILES):
                    act.wait_ge(S["turned"], t + 1)
                    act.activation(gates[:, t, :], turn_ps[t % 2][:, 2 * P:2 * P + 3 * NSA_HEADS], ACT.Sigmoid
                                   ).then_inc(S["gates"], 1)
                act.wait_ge(S["hid"], 1)
                act.activation(hidden_rows[:], pT_ps[0][:BOTH, :], ACT.Gelu_apprx_tanh).then_inc(S["gelu"], 1)

                def exps(t):
                    act.wait_ge(S["shifted"], t + 1)
                    act.activation(s[:, t % 2], s[:, t % 2], ACT.Exp, scale=scale).then_inc(S["exped"], 1)

                exps(0)
                for t in range(TILES):
                    if t + 1 < TILES:
                        exps(t + 1)
                    act.wait_ge(S["pturned"], t + 1)
                    for i in range(2):
                        act.copy(pT[:, 4 * i:4 * i + 4, :].rearrange("p h q -> p (h q)"), pT_ps[i][0:NB, :]
                                 ).then_inc(S["pcopied"], 1)

            @block.vector
            def _(dve):
                done = [0]

                def then(instruction):
                    done[0] += 1
                    instruction.then_inc(S["seq"], 1)
                    dve.wait_ge(S["seq"], done[0])

                dve.wait_ge(S["w"], 16 * n_small)
                dve.wait_ge(S["cleared"], 1)
                for kv, tile in enumerate((KCMP, VCMP)):
                    for a in range(2):
                        tokens = proj[:, tile, CMP_STRIDE * a:CMP_STRIDE * (a + NB)]
                        place = pos[:, kv, CMP_STRIDE * a:CMP_STRIDE * (a + 1)]
                        for g in range(NSA_GROUPS):
                            part = slice(g * NSA_HD, (g + 1) * NSA_HD)
                            dve.tensor_tensor(blocks[part, kv, CMP_STRIDE * a:CMP_STRIDE * (a + 1), g, :],
                                              tokens[part].rearrange("p (c r) -> p r c", r=CMP_STRIDE),
                                              place[part].unsqueeze(2).broadcast_to([NSA_HD, CMP_STRIDE, NB]),
                                              ALU.add).then_inc(S["blocks"], 1)
                for t in range(TILES):
                    dve.wait_ge(S["gates"], t + 1)
                    then(dve.tensor_copy(vsel[:, t, :], turn_ps[t % 2][:, 0:P]))
                    dve.tensor_copy(vwin[:, t, :], turn_ps[t % 2][:, P:2 * P]).then_inc(S["copied"], 1)
                dve.wait_ge(S["hturned"], 1)
                dve.tensor_copy(hidden[:].rearrange("p a b g n -> p (a b g n)"), pT_ps[1][:, :4 * BOTH]
                                ).then_inc(S["hidden"], 1)
                dve.wait_ge(S["kc"], 1)
                dve.tensor_copy(kcT[:], small_ps[:, 0:NB]).then_inc(S["kcopied"], 1)
                dve.tensor_copy(vc[:], small_ps[0:NB, P:2 * P]).then_inc(S["kcopied"], 1)
                dve.wait_ge(S["biases"], 1)
                dve.wait_ge(S["gated"], 1)
                wide = [P, NSA_HEADS, NB]

                def shift(t):
                    now = s[:, t % 2]
                    dve.wait_ge(S["scored"], t + 1)
                    if t >= 2:
                        dve.wait_ge(S["pturned"], t - 1)
                    for g in range(NSA_GROUPS):
                        heads = slice(4 * g, 4 * g + 4)
                        scores = s_ps[t % 2][g][:, :4 * NB].rearrange("p (h n) -> p h n", n=NB)
                        then(dve.tensor_tensor(now[:, heads], scores, cbias[:, heads, t, :], ALU.add))
                    then(dve.tensor_reduce(top[:], now, AX.X, ALU.max))
                    dve.tensor_tensor(now, now, top[:].unsqueeze(2).broadcast_to(wide), ALU.subtract
                                      ).then_inc(S["shifted"], 1)

                shift(0)
                for t in range(TILES):
                    now = s[:, t % 2]
                    if t + 1 < TILES:
                        shift(t + 1)
                    dve.wait_ge(S["exped"], t + 1)
                    then(dve.tensor_reduce(total[:], now, AX.X, ALU.add))
                    then(dve.reciprocal(total[:], total[:]))
                    then(dve.tensor_tensor(total[:], gates[:, t, 0:3 * NSA_HEADS:3], total[:], ALU.mult))
                    dve.tensor_tensor(now, now, total[:].unsqueeze(2).broadcast_to(wide), ALU.mult
                                      ).then_inc(S["weights"], 1)
                    dve.wait_ge(S["out"], t + 1)
                    dve.tensor_copy(o_tok[:, t, :], o_ps[:]).then_inc(S["stored"], 1)
    clear_semaphores(nc, S.values())


def second_mixer(nc, hT, x_hi, x_lo, d):
    with ExitStack() as ctx:
        c = Chip(nc, ctx)
        o_tok = c.sb("n_otok", [P, TILES, NSA_HEADS * NSA_HD])
        ident = c.sb("n_ident", [P, P])
        with ExitStack() as inner:
            c = Chip(nc, inner)
            proj = c.sb("n_proj", [P, N_PROJ2, SEQ])
            vsel, vwin = (c.sb(x, [P, TILES, P]) for x in ("n_vsel", "n_vwin"))
            gates = c.sb("n_gates", [P, TILES, 3 * NSA_HEADS])
            bias = c.sb("n_bias", [P, NSA_HEADS, 7 * P])
            w1_landed = c.sem("n_w1_landed")
            with ExitStack() as compressing:
                w1k = Chip(nc, compressing).sb("n_w1k", [P, CMP_LEN, CMP_HID])

                def load_w1k(sp):
                    sp.dma_start(w1k[:], d["cmp_w1"][0]).then_inc(w1_landed, 16)
                norm_and_project(nc, "p2", hT, x_hi, x_lo, d["mix_norm"], d["w_nsa"], proj, load_w1k)
                compress_and_attend(nc, proj, ident, w1k, w1_landed, vsel, vwin, gates, bias, o_tok, d)

            def unit(t, h, branch):
                part = slice(h // 4 * NSA_HD, (h // 4 + 1) * NSA_HD)
                w, at = (t + 1) * P, (TILES - 1 - t) * P
                keys, values = ((KSEL, vsel), (KWIN, vwin))[branch - 1]
                return dict(q=proj[part, NQ0 + h % 4, t * P:(t + 1) * P], k=proj[part, keys, :w], width=w,
                            bias=bias[:, h, at:at + w], v=lambda b: values[:, b, part], dv=NSA_HD, add=True,
                            gate=gates[:, t, 3 * h + branch:3 * h + branch + 1],
                            out=o_tok[:, t, h * NSA_HD:(h + 1) * NSA_HD])
            with ExitStack() as attending:
                c = Chip(nc, attending)
                stream = PanelStream(c, "p3", d["w_hg"], x_hi, x_lo, d["hg_proj"], ACT.Copy)
                att = Attention(c, "att2", [unit(t, h, branch) for t in range(TILES) for branch in (1, 2)
                                            for h in range(NSA_HEADS)], float(NSA_HD) ** -0.5, ident, stream)
                with nc.Block() as block:
                    block.sync(stream.sync)
                    block.gpsimd(stream_low(stream))
                    block.scalar(att.scalar)
                    block.vector(att.vector)
                    block.tensor(att.tensor)
                clear_semaphores(nc, [*att.sems, *stream.sems, w1_landed])
        hgrn(nc, hT, x_hi, x_lo, o_tok, ident, d)
    project_onto(nc, "wo2", x_hi[:, 4:8, :], x_lo[:, 4:8, :], d["w_out"][:, :, 4 * P:], hT)


HQ, HF, HI, HG = 0, 4, 8, 12
N_PROJ3 = 16


def hgrn_operands(nc, projections, proj, ident, write, fold, ends, v_tok, w_tok, lower_bound):
    with ExitStack() as ctx:
        c = Chip(nc, ctx)
        lb = c.sb("hf_lb", [P, HG_HEADS])
        lb_e = c.sb("hf_lbe", [P, HG_HEADS])
        free = c.sb("hf_free", [P, HG_HEADS])
        sig = c.sb("hf_sig", [P, HG_HEADS, SEQ])
        tiny = c.sb("hf_tiny", [P, HG_HEADS, SEQ])
        inside = c.sb("hf_inside", [P, HG_HEADS * SEQ])
        part = c.sb("hf_part", [P, 1], I32)
        odd = c.sb("hf_odd", [P, 1], I32)
        parity = c.sb("hf_parity", [P, 2])
        banks = [c.ps(f"hf_bank{i}", [P, SEQ]) for i in range(4)]
        S = {x: c.sem(f"hf_{x}") for x in ("lb", "lb_shift", "lb_exp", "const", "sigmoids", "f", "seq", "logs",
                                           "b", "eb", "rest", "erest", "w", "turned", "taken")}
        landed = {x: c.sem(f"hf_landed{x}") for x in (HQ, HF, HI, HG)}
        q, z, inp, gate = (proj[:, x:x + 4, :] for x in (HQ, HF, HI, HG))

        def flat(x):
            return x.rearrange("p h s -> p (h s)")

        def chunked(x):
            return flat(x).rearrange("p (c i) -> p c i", i=CHUNK)
        HALF = [slice(0, 2), slice(2, 4)]
        PART = 2.0 ** -50
        with nc.Block() as block:
            @block.sync
            def _(sp):
                sp.dma_start(lb[:], lower_bound).then_inc(S["lb"], 16)
                for x in (HF, HI, HQ, HG):
                    sp.dma_start(proj[:, x:x + 4, :], projections[x:x + 4].rearrange("n p s -> p n s")
                                 ).then_inc(landed[x], 16)

            @block.gpsimd
            def _(pool):
                pool.memset(inside[:], 1.0).then_inc(S["const"], 1)
                pool.iota(part[:], pattern=[[0, 1]], base=0, channel_multiplier=1).then_inc(S["const"], 1)
                pool.wait_ge(S["const"], 2)
                pool.memset(inside[:].rearrange("p (c i) -> p c i", i=CHUNK)[:, :, 0:1], 0.0
                            ).then_inc(S["const"], 1)

            @block.scalar
            def _(act):
                act.wait_ge(S["lb_shift"], 1)
                act.activation(lb_e[:], lb_e[:], ACT.Exp).then_inc(S["lb_exp"], 1)
                act.wait_ge(landed[HF], 16)
                for e in HALF:
                    act.activation(flat(sig[:, e]), flat(z[:, e]), ACT.Sigmoid).then_inc(S["sigmoids"], 1)
                for e in HALF:
                    act.activation(flat(write[:, e]), flat(z[:, e]), ACT.Sigmoid, scale=-1.0
                                   ).then_inc(S["sigmoids"], 1)
                act.wait_ge(landed[HQ], 16)
                act.activation(flat(q), flat(q), ACT.Silu).then_inc(S["sigmoids"], 1)
                act.wait_ge(landed[HG], 16)
                act.activation(flat(gate), flat(gate), ACT.Silu).then_inc(S["sigmoids"], 1)
                for n, e in enumerate(HALF):
                    act.wait_ge(S["f"], 2 * n + 2)
                    act.activation(flat(z[:, e]), flat(z[:, e]), ACT.Ln).then_inc(S["logs"], 1)
                    act.activation(flat(tiny[:, e]), flat(tiny[:, e]), ACT.Ln, scale=1.0 / PART
                                   ).then_inc(S["logs"], 1)
                for n, e in enumerate(HALF):
                    act.wait_ge(S["b"], n + 1)
                    act.activation(flat(tiny[:, e]), flat(z[:, e]), ACT.Exp).then_inc(S["eb"], 1)
                    act.wait_ge(S["rest"], n + 1)
                    act.activation(flat(sig[:, e]), flat(sig[:, e]), ACT.Exp).then_inc(S["erest"], 1)

            @block.vector
            def _(dve):
                done = [0]

                def then(instruction):
                    done[0] += 1
                    instruction.then_inc(S["seq"], 1)
                    dve.wait_ge(S["seq"], done[0])

                dve.wait_ge(S["const"], 3)
                then(dve.tensor_scalar(odd[:], part[:], CHUNK.bit_length() - 1, 1, ALU.logical_shift_right,
                                       ALU.bitwise_and))
                then(dve.tensor_copy(parity[:, 1:2], odd[:]))
                then(dve.tensor_scalar(parity[:, 0:1], parity[:, 1:2], -1.0, 1.0, ALU.mult, ALU.add))
                dve.wait_ge(S["lb"], 16)
                dve.tensor_tensor(lb_e[:], lb[:], lb[:], ALU.subtract).then_inc(S["lb_shift"], 1)
                dve.wait_ge(S["lb_exp"], 1)
                then(dve.reciprocal(lb[:], lb_e[:]))
                then(dve.tensor_tensor(lb_e[:], lb_e[:], lb[:], ALU.mult))
                then(dve.tensor_tensor(lb[:], lb_e[:], lb_e[:], ALU.subtract))
                then(dve.tensor_scalar(free[:], lb[:], -1.0, 1.0, ALU.mult, ALU.add))
                for n, e in enumerate(HALF):
                    dve.wait_ge(S["sigmoids"], n + 1)
                    for h in range(e.start, e.stop):
                        then(dve.tensor_scalar(sig[:, h, :], sig[:, h, :], free[:, h:h + 1], lb[:, h:h + 1], ALU.mult,
                                               ALU.add))
                    dve.tensor_scalar(flat(tiny[:, e]), flat(sig[:, e]), F_FLOOR, PART, ALU.max, ALU.min
                                      ).then_inc(S["f"], 1)
                    dve.wait_ge(S["sigmoids"], 2 + n + 1)
                    dve.tensor_scalar(flat(z[:, e]), flat(sig[:, e]), PART, None, ALU.max).then_inc(S["f"], 1)
                for h in range(HG_HEADS):
                    then(dve.tensor_scalar(write[:, h, :], write[:, h, :], free[:, h:h + 1], None, ALU.mult))
                for t in range(TILES):
                    dve.wait_ge(S["turned"], t + 1)
                    dve.tensor_copy(v_tok[:, t, :], banks[t][:]).then_inc(S["taken"], 1)
                for n, e in enumerate(HALF):
                    dve.wait_ge(S["logs"], 2 * n + 2)
                    then(dve.tensor_tensor(flat(sig[:, e]), flat(z[:, e]), flat(tiny[:, e]), ALU.add))
                    dve.tensor_tensor_scan(flat(z[:, e]), inside[:, :2 * SEQ], flat(sig[:, e]), 0.0, ALU.mult,
                                           ALU.add).then_inc(S["b"], 1)
                    dve.wait_ge(S["b"], n + 1)
                    half = chunked(z[:, e])
                    dve.tensor_tensor(chunked(sig[:, e]), half[:, :, CHUNK - 1:CHUNK].broadcast_to(half.shape), half,
                                      ALU.subtract).then_inc(S["rest"], 1)
                dve.wait_ge(S["sigmoids"], 6)
                for n, e in enumerate(HALF):
                    dve.wait_ge(S["eb"], n + 1)
                    then(dve.tensor_tensor(flat(fold[:, e]), flat(q[:, e]), flat(tiny[:, e]), ALU.mult))
                    then(dve.tensor_copy(ends[:, e.start * N_CHUNKS:e.stop * N_CHUNKS],
                                         chunked(tiny[:, e])[:, :, CHUNK - 1]))
                    dve.wait_ge(S["erest"], n + 1)
                    dve.tensor_tensor(flat(sig[:, e]), flat(sig[:, e]), flat(write[:, e]), ALU.mult
                                      ).then_inc(S["w"], 1)
                for t in range(TILES):
                    dve.wait_ge(S["turned"], TILES + t + 1)
                    for i in range(2):
                        last = dve.tensor_scalar(w_tok[:, i, t, :], banks[t][:], parity[:, i:i + 1], None, ALU.mult)
                        last.then_inc(S["taken"], 1)

            @block.tensor
            def _(pe):
                def turn(x):
                    for t in range(TILES):
                        for h in range(HG_HEADS):
                            last = pe.transpose(banks[t][:, h * P:(h + 1) * P], x[:, h, t * P:(t + 1) * P],
                                                ident[:])
                        last.then_inc(S["turned"], 1)
                pe.wait_ge(landed[HI], 16)
                turn(inp)
                pe.wait_ge(S["w"], 2)
                pe.wait_ge(S["taken"], TILES)
                turn(sig)
    clear_semaphores(nc, [*S.values(), *landed.values()])


def hgrn_outputs(nc, proj, write, fold, ends, v_tok, w_tok, ident, out_norm, scratch, y_hi, y_lo, w_out, o_hi,
                 o_lo, hT):
    with ExitStack() as ctx:
        c = Chip(nc, ctx)
        bc, qc, kc = (c.sb(f"ho_{x}", [P, CHUNK, P]) for x in ("b", "q", "k"))
        pair = c.sb("ho_pair", [P, 3, CHUNK, P])
        weights = c.sb("ho_weights", [P, CHUNK * CHUNK])
        zeros = c.sb("ho_zeros", [P, scratch.shape[0] * scratch.shape[1] // P])
        inner = c.sb("ho_inner", [P, HG_HEADS * TILES, P])
        state = c.sb("ho_state", [P, 2, HG_HEADS, P])
        ones = c.sb("ho_ones", [P, P])
        gain = c.sb("ho_gain", [P, 1])
        OUT_KC = w_out.shape[2] // P
        n_out = w_out.shape[0]
        OUT_FIRST = n_out // 2
        out_raw = c.sb("ho_out_raw", [P, 2, OUT_KC * P])
        out_hi = c.sb("ho_out_hi", [P, 2, OUT_KC * P], F32R)
        out_lo = c.sb("ho_out_lo", [P, 2, OUT_KC * P], F32R)
        out_landed = [c.sem(f"ho_out_landed{i}") for i in range(2)]
        sq, ms = (x[:].rearrange("p i d -> p (i d)").rearrange("p (h s) -> p h s", h=HG_HEADS) for x in (bc, qc))
        o_ps = [c.ps(f"ho_o{h}", [P, SEQ]) for h in range(HG_HEADS)]
        kv_ps = [c.ps(f"ho_kv{i}", [P, HG_HEADS, P]) for i in range(2)]
        banks = [c.ps(f"ho_bank{i}", [P, SEQ]) for i in range(2)]
        S = {x: c.sem(f"ho_{x}") for x in (
            "gain", "const", "turned", "chunked", "zeros", "cleared", "diff", "exp", "keyed", "product", "summed",
            "placed", "loaded", "written", "state", "read", "whole", "out_high", "out_split", "out_product", "out_added", "sq", "sum", "mean", "root", "rstd", "normed",
            "out", "high", "low")}
        sources = [proj[:, HF:HF + 4, :], write[:], proj[:, HQ:HQ + 4, :]]
        n_banks = CHUNK * P // SEQ
        BESIDE = 27

        def steps_by(j):
            return BESIDE * sum(CHUNK - i for i in range(j + 1)) // sum(range(CHUNK + 1))

        with nc.Block() as block:
            @block.sync
            def _(sp):
                sp.dma_start(gain[:], out_norm).then_inc(S["gain"], 16)
                sp.wait_ge(S["zeros"], 2)
                sp.dma_start(scratch.rearrange("a x -> (a x)").rearrange("(p x) -> p x", p=P), zeros[:]
                             ).then_inc(S["cleared"], 16)
                def load_out(k):
                    if k >= 2:
                        sp.wait_ge(S["out_split"], k - 1)
                    sp.dma_start(out_raw[:, k % 2, :], w_out[k]).then_inc(out_landed[k % 2], 16)

                for k in range(4):
                    load_out(k)
                sp.wait_ge(S["cleared"], 16)
                sp.wait_ge(S["summed"], CHUNK)
                for a in range(HG_HEADS * TILES):
                    to = scratch[a].rearrange("(c x) -> c x", c=P // CHUNK)[:, :CHUNK * PITCH]
                    sp.dma_start(to.rearrange("c (s y) -> c s y", y=PITCH)[:, :, :CHUNK],
                                 weights[a * (P // CHUNK):(a + 1) * (P // CHUNK), :].rearrange(
                                     "c (s t) -> c s t", t=CHUNK)).then_inc(S["placed"], 16)
                sp.wait_ge(S["placed"], 16 * HG_HEADS * TILES)
                sp.dma_start(inner[:], scratch[:, :P * PITCH].rearrange("a (s y) -> s a y", y=PITCH)[:, :, :P]
                             ).then_inc(S["loaded"], 16)
                for k in range(4, n_out):
                    load_out(k)

            @block.tensor
            def _(pe):
                for n in range(3 * n_banks):
                    x = sources[n // n_banks].rearrange("p h s -> p (h s)").rearrange("p (c i) -> p c i", i=CHUNK)
                    if n >= 2:
                        pe.wait_ge(S["chunked"], n - 1)
                    for k in range(SEQ // P):
                        last = pe.transpose(banks[n % 2][:, k * P:(k + 1) * P], x[:, :, n % n_banks * 4 + k],
                                            ident[:])
                    last.then_inc(S["turned"], 1)
                for n in range(N_CHUNKS):
                    if n < N_CHUNKS - 1:
                        tile, rows = n * CHUNK // P, slice(n // 2 % 4 * 32, n // 2 % 4 * 32 + 32)
                        if n >= 2:
                            pe.wait_ge(S["state"], n - 1)
                        for h in range(HG_HEADS):
                            cols = slice(h * P, (h + 1) * P)
                            last = pe.matmul(kv_ps[n % 2][:, h, :], w_tok[rows, n % 2, tile, cols],
                                             v_tok[rows, tile, cols], start=True, stop=True)
                        last.then_inc(S["written"], 1)
                    if n >= 1:
                        pe.wait_ge(S["state"], n)
                        at = slice(n * CHUNK, (n + 1) * CHUNK)
                        for h in range(HG_HEADS):
                            last = pe.matmul(o_ps[h][:, at], state[:, n % 2, h, :], fold[:, h, at], start=n == 1,
                                             stop=False, skip_group_check=True)
                        last.then_inc(S["read"], 1)

                def out_panel(k):
                    pe.wait_ge(S["out_split"], k + 1)
                    if k >= 2:
                        pe.wait_ge(S["out_added"], k - 1)
                    for kc in range(OUT_KC):
                        cols = slice(kc * P, (kc + 1) * P)
                        last = three_products(pe, banks[k % 2][:], out_hi[:, k % 2, cols], out_lo[:, k % 2, cols],
                                              o_hi[:, kc, :], o_lo[:, kc, :], kc == 0, kc == OUT_KC - 1)
                    last.then_inc(S["out_product"], 1)

                pe.wait_ge(S["chunked"], 3 * n_banks)
                for k in range(OUT_FIRST):
                    out_panel(k)
                pe.wait_ge(S["loaded"], 16)
                for h in range(HG_HEADS):
                    for t in range(TILES):
                        last = pe.matmul(o_ps[h][:, t * P:(t + 1) * P], v_tok[:, t, h * P:(h + 1) * P],
                                         inner[:, h * TILES + t, :], start=False, stop=t == TILES - 1,
                                         skip_group_check=True)
                    last.then_inc(S["whole"], 1)
                pe.wait_ge(S["const"], 1)
                pe.wait_ge(S["out_added"], OUT_FIRST)
                for h in range(HG_HEADS):
                    pe.wait_ge(S["sq"], h + 1)
                    if h >= 2:
                        pe.wait_ge(S["mean"], h - 1)
                    pe.matmul(banks[h % 2][:], ones[:], sq[:, h, :], start=True, stop=True).then_inc(S["sum"], 1)
                pe.wait_ge(S["mean"], HG_HEADS)
                for k in range(OUT_FIRST, n_out):
                    out_panel(k)

            @block.scalar
            def _(act):
                for n in range(3 * n_banks):
                    act.wait_ge(S["turned"], n + 1)
                    to = (bc, kc, qc)[n // n_banks][:, n % n_banks * 4:n % n_banks * 4 + 4, :]
                    act.copy(to.rearrange("p i d -> p (i d)"), banks[n % 2][:]).then_inc(S["chunked"], 1)

                def out_high(k):
                    act.wait_ge(out_landed[k % 2], 16 * (k // 2 + 1))
                    if k >= 2:
                        act.wait_ge(S["out_product"], k - 1)
                    act.copy(out_hi[:, k % 2, :], out_raw[:, k % 2, :]).then_inc(S["out_high"], 1)

                out_high(0)
                out_high(1)
                for j in range(CHUNK):
                    act.wait_ge(S["diff"], j + 1)
                    x = pair[:, j % 3, :CHUNK - j, :]
                    act.activation(x, x, ACT.Exp).then_inc(S["exp"], 1)
                for k in range(2, OUT_FIRST + 2):
                    out_high(k)
                for h in range(HG_HEADS):
                    act.wait_ge(S["whole"], h + 1)
                    act.activation(sq[:, h, :], o_ps[h][:], ACT.Square).then_inc(S["sq"], 1)
                for h in range(HG_HEADS):
                    act.wait_ge(S["mean"], h + 1)
                    act.activation(ms[:, h, :], ms[:, h, :], ACT.Sqrt).then_inc(S["root"], 1)
                for k in range(OUT_FIRST + 2, n_out):
                    out_high(k)
                for h in range(HG_HEADS):
                    act.wait_ge(S["out"], h + 1)
                    act.copy(y_hi[:, h, :], ms[:, h, :]).then_inc(S["high"], 1)

            @block.gpsimd
            def _(pool):
                pool.memset(zeros[:], 0.0).then_inc(S["zeros"], 1)
                pool.memset(weights[:], 0.0).then_inc(S["zeros"], 1)
                pool.memset(ones[:], 1.0).then_inc(S["const"], 1)

                def out_low(k):
                    pool.wait_ge(S["out_high"], k + 1)
                    pool.tensor_tensor(out_lo[:, k % 2, :], out_raw[:, k % 2, :], out_hi[:, k % 2, :].bitcast(F32),
                                       ALU.subtract).then_inc(S["out_split"], 1)

                out_low(0)
                out_low(1)
                pool.wait_ge(S["chunked"], 2 * n_banks)
                for j in range(CHUNK):
                    pool.wait_ge(S["exp"], j + 1)
                    x = pair[:, j % 3, :CHUNK - j, :]
                    pool.tensor_tensor(x, x, kc[:, :CHUNK - j, :], ALU.mult).then_inc(S["keyed"], 1)
                for k in range(2, n_out):
                    out_low(k)

            @block.vector
            def _(dve):
                dve.wait_ge(S["chunked"], n_banks)

                def diff(j):
                    if j >= 3:
                        dve.wait_ge(S["summed"], j - 2)
                    dve.tensor_tensor(pair[:, j % 3, :CHUNK - j, :], bc[:, j:, :], bc[:, :CHUNK - j, :],
                                      ALU.subtract).then_inc(S["diff"], 1)

                def add_out(k):
                    dve.wait_ge(S["out_product"], k + 1)
                    dve.tensor_tensor(hT[:, k, :], hT[:, k, :], banks[k % 2][:], ALU.add
                                      ).then_inc(S["out_added"], 1)

                def step(n):
                    dve.wait_ge(S["written"], n + 1)
                    if n == 0:
                        dve.tensor_copy(state[:, 1], kv_ps[0][:]).then_inc(S["state"], 1)
                        return
                    dve.wait_ge(S["state"], n)
                    if n >= 2:
                        dve.wait_ge(S["read"], n - 1)
                    for h in range(HG_HEADS):
                        end = ends[:, h * N_CHUNKS + n:h * N_CHUNKS + n + 1]
                        last = dve.scalar_tensor_tensor(state[:, (n + 1) % 2, h, :], state[:, n % 2, h, :], end,
                                                        kv_ps[n % 2][:, h, :], ALU.mult, ALU.add)
                    last.then_inc(S["state"], 1)

                diff(0)
                diff(1)
                dve.wait_ge(S["chunked"], 3 * n_banks)
                dve.wait_ge(S["zeros"], 2)
                n = 0
                for j in range(CHUNK):
                    x = pair[:, j % 3, :CHUNK - j, :]
                    if j + 2 < CHUNK:
                        diff(j + 2)
                    while n < steps_by(j):
                        step(n)
                        n += 1
                    dve.wait_ge(S["keyed"], j + 1)
                    dve.tensor_tensor(x, x, qc[:, j:, :], ALU.mult).then_inc(S["product"], 1)
                    dve.wait_ge(S["product"], j + 1)
                    dve.tensor_reduce(weights[:, j:j + (CHUNK + 1) * (CHUNK - j - 1) + 1:CHUNK + 1], x, AX.X,
                                      ALU.add).then_inc(S["summed"], 1)
                for n in range(BESIDE, N_CHUNKS - 1):
                    step(n)
                for k in range(OUT_FIRST):
                    add_out(k)
                for h in range(HG_HEADS):
                    dve.wait_ge(S["sum"], h + 1)
                    dve.tensor_scalar(ms[:, h, :], banks[h % 2][:], 1.0 / P, EPS, ALU.mult, ALU.add
                                      ).then_inc(S["mean"], 1)
                dve.wait_ge(S["gain"], 16)
                for h in range(HG_HEADS):
                    dve.wait_ge(S["root"], h + 1)
                    dve.reciprocal(sq[:, h, :], ms[:, h, :]).then_inc(S["rstd"], 1)
                    dve.wait_ge(S["rstd"], h + 1)
                    dve.scalar_tensor_tensor(sq[:, h, :], o_ps[h][:], gain[:, 0:1], sq[:, h, :], ALU.mult,
                                             ALU.mult).then_inc(S["normed"], 1)
                    dve.wait_ge(S["normed"], h + 1)
                    dve.tensor_tensor(ms[:, h, :], sq[:, h, :], proj[:, HG + h, :], ALU.mult
                                      ).then_inc(S["out"], 1)
                    add_out(OUT_FIRST + h)
                for h in range(HG_HEADS):
                    dve.wait_ge(S["high"], h + 1)
                    dve.tensor_tensor(y_lo[:, h, :], ms[:, h, :], y_hi[:, h, :].bitcast(F32), ALU.subtract
                                      ).then_inc(S["low"], 1)
    clear_semaphores(nc, [*S.values(), *out_landed])


def hgrn(nc, hT, x_hi, x_lo, o_tok, ident, d):
    with ExitStack() as ctx:
        c = Chip(nc, ctx)
        proj = c.sb("h_proj", [P, N_PROJ3, SEQ])
        turn_to_features(nc, "on_turn", o_tok, 4, x_hi, x_lo, ident)
        fold = c.sb("h_fold", [P, HG_HEADS, SEQ])
        ends = c.sb("h_ends", [P, HG_HEADS * N_CHUNKS])
        v_tok = c.sb("h_vtok", [P, TILES, HG_HEADS * P])
        w_tok = c.sb("h_wtok", [P, 2, TILES, HG_HEADS * P])
        write = o_tok
        hgrn_operands(nc, d["hg_proj"], proj, ident, write, fold, ends, v_tok, w_tok, d["lower_bound"])
        hgrn_outputs(nc, proj, write, fold, ends, v_tok, w_tok, ident, d["out_norm"], d["hg_scratch"],
                     x_hi[:, 4:8, :], x_lo[:, 4:8, :], d["w_out"][:, :, :4 * P], x_hi[:, :4, :], x_lo[:, :4, :], hT)


def final_norm(nc, hT, gain, out):
    with ExitStack() as ctx:
        c = Chip(nc, ctx)
        result = c.sb("fn_result", [P, KC, SEQ])
        norm = NormStage(c, "fn", hT, gain, c.ps("fn_sum", [P, SEQ]), c.sb("fn_sq", [P, 2, SEQ]), None,
                         c.sb("fn_stat", [P, 2, SEQ]))
        scaled, stored = c.sem("fn_scaled"), c.sem("fn_stored")
        with nc.Block() as block:
            @block.sync
            def _(sp):
                norm.sync(sp)
                for k in range(KC):
                    sp.wait_ge(scaled, k + 1)
                    sp.dma_start(out[:, k, :], result[:, k, :]).then_inc(stored, 16)
                sp.wait_ge(stored, 16 * KC)

            @block.gpsimd
            def _(pool):
                norm.gpsimd(pool)

            @block.scalar
            def _(act):
                norm.scalar_squares(act)
                norm.scalar_root(act)

            @block.vector
            def _(dve):
                norm.vector_add(dve)
                norm.vector_inverse(dve)
                for k in range(KC):
                    dve.scalar_tensor_tensor(result[:, k, :], hT[:, k, :], norm.gain[:, k:k + 1],
                                             norm.stat[:, 0, :], ALU.mult, ALU.mult).then_inc(scaled, 1)

            @block.tensor
            def _(pe):
                norm.tensor(pe)
    clear_semaphores(nc, [*norm.sems, scaled, stored])


def build_program(nc, a, out):
    with ExitStack() as ctx:
        c = Chip(nc, ctx)
        hT = c.sb("hT", [P, KC, SEQ])
        x_hi, x_lo = (c.sb(x, [P, KC, SEQ], F32R) for x in ("x_hi", "x_lo"))
        routing = nc.dram_tensor("routing", [SEQ // TOKENS, N_KEYS, N_KEYS, TOKENS], F32).ap()
        a["hg_scratch"] = nc.dram_tensor("hg_scratch", [HG_HEADS * TILES, P // CHUNK * (CHUNK * PITCH + CHUNK)],
                                         F32).ap()
        hidden = nc.dram_tensor("hidden", [sum(EARLY_CHUNKS), P, SEQ], F32).ap()
        a["hg_proj"] = nc.dram_tensor("hg_proj", [N_PROJ3, P, SEQ], F32).ap()
        a["gates"] = nc.dram_tensor("gates", [2 * KC, P, SEQ], F32).ap()
        loaded = c.sem("h_loaded")
        with nc.Block() as block:
            @block.sync
            def _(sp):
                sp.dma_start(hT[:], a["x"]).then_inc(loaded, 16)
                sp.wait_ge(loaded, 16)
        first_mixer(nc, hT, x_hi, x_lo, a)
        experts(nc, hT, x_hi, x_lo, a, routing, hidden)

        def down(w):
            return lambda n: w[bass.ds(n, 1)].rearrange("o p f -> p (o f)")
        hidden_stage(nc, "ffn1", hT, x_hi, x_lo, a["gu1"], down(a["down1"]), norm_g=a["ffn1_norm"])
        second_mixer(nc, hT, x_hi, x_lo, a)
        hidden_stage(nc, "ffn2", hT, x_hi, x_lo, a["gu2"], down(a["down2"]), norm_g=a["ffn2_norm"])
        final_norm(nc, hT, a["final_norm"], out)



def panels(w):
    import numpy as np
    k, n = w.shape
    return np.ascontiguousarray(w.reshape(k // P, P, n // P, P).transpose(2, 1, 0, 3)).reshape(n // P, P, k)


def columns(g):
    import numpy as np
    return np.ascontiguousarray(g.reshape(-1, P).T)


def rotary_constants():
    import numpy as np
    inv, rot = np.zeros((P, 2), np.float32), np.zeros((P, 2, P), np.float32)
    for kind, half, heads in ((0, 16, (0,)), (1, 8, (0, 64))):
        freq = np.power(np.float32(500000.0), -np.arange(half, dtype=np.float32) * np.float32(2.0 / (2 * half)))
        for at in heads:
            for i in range(half):
                inv[at + i, kind] = inv[at + half + i, kind] = freq[i]
                rot[at + half + i, kind, at + i] = -1.0
                rot[at + i, kind, at + half + i] = 1.0
    return inv, rot


def laid_out(inputs):
    import numpy as np
    I = {k: np.asarray(v) for k, v in inputs.items()}
    cat, stack, whole = np.concatenate, np.stack, np.ascontiguousarray
    w_in = I["w_in"][0]
    at = [512, 1024, 1536, 1792, 2048, 2112, 2116]
    k_idx = w_in[:, at[4]:at[5]]
    w_in1 = cat([w_in[:, :at[4]], k_idx, k_idx, w_in[:, at[5]:at[5] + P]], 1)
    gates = w_in[:, at[6]:]
    w_gates = stack([panels(gates[:, :D]), panels(gates[:, D:])], 1).reshape(2 * KC, P, PANEL)
    w_merge = cat([panels(I["w_a_out"][0]), panels(I["w_b_out"][0])], 2)
    inv, rot = rotary_constants()
    w2 = I["w_in_2"][0]
    q_end, gl = NSA_HEADS * NSA_HD, NSA_HEADS * NSA_HD + 6 * P
    q2 = w2[:, :q_end].reshape(D, 2, 4, NSA_HD).transpose(0, 2, 1, 3).reshape(D, q_end)
    w_nsa = cat([q2, w2[:, q_end:gl], w2[:, gl:gl + P]], 1)

    def twice(x):
        return cat([x, x], 0)

    def gate_up(w):
        w = np.pad(w.reshape(KC, P, 2, -1), ((0, 0), (0, 0), (0, 0), (0, -w.shape[1] // 2 % P)))
        w = w.reshape(KC, P, 2, -1, P)
        return whole(w.transpose(3, 2, 1, 0, 4)).reshape(-1, P, PANEL)

    def down(w):
        return np.pad(w, ((0, -w.shape[0] % P), (0, 0))).reshape(-1, P, D)

    return dict(
        x=whole(I["x"][0].reshape(SEQ, KC, P).transpose(2, 1, 0)), positions=I["positions"],
        norm1_g=columns(I["norm1_g"][0]), w_in1=panels(w_in1), w_gates=w_gates, w_merge=w_merge, w_o=panels(I["w_o"][0]),
        inv=inv, rot=rot,
        gains=columns(cat([I["kv_norm_g"][0], I["q_norm_g"][0], I["k_norm_g"][0]])),
        wuk=whole(I["w_uk"][0].reshape(2, P, P).transpose(1, 0, 2)),
        wuv=whole(I["w_uv"][0].reshape(2, P, P).transpose(1, 0, 2)),
        wsT=whole(I["spatial_w"][0].transpose(2, 0, 1)), bs=I["spatial_b"].reshape(1, A_GROUPS, P),
        vg=I["v_norm_g"][0], vb=I["v_norm_b"][0],
        norm2_g=columns(I["norm2_g"][0]), peer_wq=panels(I["peer_wq"][0]),
        subkeys=whole(I["peer_subkeys"][0].reshape(HALVES, N_KEYS, P).transpose(2, 0, 1)),
        peer_u=whole(I["peer_u"][0].reshape(N_KEYS, N_KEYS, KC, P).transpose(1, 3, 2, 0)).reshape(N_KEYS, P, PANEL),
        peer_v=I["peer_v"][0],
        ffn1_norm=columns(I["ffn1_norm_2"][0]), gu1=gate_up(I["ffn1_w_gu_2"][0]), down1=down(I["ffn1_w_down_2"][0]),
        mix_norm=columns(I["mix_norm_2"][0]), w_nsa=panels(w_nsa), w_hg=panels(w2[:, gl + 3 * NSA_HEADS:]),
        w_out=panels(I["w_out_2"][0]),
        cmp_pos=stack([twice(I["cmp_pos_k_2"][0].T), twice(I["cmp_pos_v_2"][0].T)], 1),
        cmp_w1=stack([twice(I[x][0].reshape(CMP_LEN, NSA_HD, CMP_HID).transpose(1, 0, 2))
                      for x in ("cmp_k_w1_2", "cmp_v_w1_2")]),
        cmp_w2=stack([I[x][0].reshape(2, P, NSA_HD).transpose(1, 0, 2) for x in ("cmp_k_w2_2", "cmp_v_w2_2")], 1),
        lower_bound=columns(I["hgrn_lower_bound_2"][0]), out_norm=columns(I["hgrn_out_norm_2"][0]),
        ffn2_norm=columns(I["ffn2_norm_2"][0]), gu2=gate_up(I["ffn2_w_gu_2"][0]), down2=down(I["ffn2_w_down_2"][0]),
        final_norm=columns(I["final_norm_2"]))


def kernel(**inputs):
    import numpy as np
    import concourse.bacc as bacc
    from concourse.bass_utils import run_bass_kernel_spmd

    nc = bacc.Bacc("TRN2", target_bir_lowering=False, num_devices=1)
    arrays, args = {}, {}
    for name, value in laid_out(inputs).items():
        value = np.ascontiguousarray(value)
        arrays[f"in_{name}"] = value
        args[name] = nc.dram_tensor(f"in_{name}", value.shape, mybir.dt.from_np(value.dtype),
                                    kind="ExternalInput").ap()
    out = nc.dram_tensor("out", (P, KC, SEQ), F32, kind="ExternalOutput").ap()
    build_program(nc, args, out)
    result = run_bass_kernel_spmd(nc, [arrays], core_ids=[0]).results[0]["out"]
    return np.ascontiguousarray(result.transpose(2, 1, 0)).reshape(1, SEQ, D)
```
